# Optimizing a Trainium2 kernel written in Bass

```python
import jax, jax.numpy as jnp
from jax import lax
import numpy as np

D_MODEL = 1024
BATCH = 1
SEQ = 128
DEPTH = 2
DEC_BATCH = 1
DEC_SEQ = 256
PAST_LEN = 128

GRID_W = 64
BRANCH_W = 256
HEAD_DIM = 64
N_BRANCH = 4
CONV_K = 31
FNET_GROUPS = 4
FNET_GDIM = BRANCH_W // FNET_GROUPS
WIN_Q_HEADS = 4
WIN_KV_HEADS = 2
WINDOW = 128
WIN_BLOCK = 128
NA_HEADS = 4
NA_ROWS = 8
NA_COLS = 16
ROPE_THETA = 10000.0
ATTN_SCALE = HEAD_DIM ** -0.5
N_EXPERTS = 16
EXPERT_FF = 1024
EC_CAPACITY = 2
EPS = 1e-6
NEG = -1e30

COLS_A = 2 * BRANCH_W
COLS_B = BRANCH_W
COLS_CQ = WIN_Q_HEADS * HEAD_DIM
COLS_CKV = WIN_KV_HEADS * HEAD_DIM
COLS_D = NA_HEADS * HEAD_DIM
COLS_GATE = N_BRANCH * D_MODEL
IN_COLS = COLS_A + COLS_B + COLS_CQ + 2 * COLS_CKV + 3 * COLS_D + COLS_GATE
SPLITS = (COLS_A,
          COLS_A + COLS_B,
          COLS_A + COLS_B + COLS_CQ,
          COLS_A + COLS_B + COLS_CQ + COLS_CKV,
          COLS_A + COLS_B + COLS_CQ + 2 * COLS_CKV,
          COLS_A + COLS_B + COLS_CQ + 2 * COLS_CKV + COLS_D,
          COLS_A + COLS_B + COLS_CQ + 2 * COLS_CKV + 2 * COLS_D,
          COLS_A + COLS_B + COLS_CQ + 2 * COLS_CKV + 3 * COLS_D)

kernel_name = 'hybrid_diffusion_parallel_mixers_ec_moe_step'

def rms_norm(x, g):
    xf = x.astype(jnp.float32)
    y = xf * lax.rsqrt(jnp.mean(xf * xf, axis=-1, keepdims=True) + EPS)
    return (y * g.astype(jnp.float32)).astype(x.dtype)

def layer_norm(x, g, b):
    xf = x.astype(jnp.float32)
    mu = jnp.mean(xf, axis=-1, keepdims=True)
    var = jnp.mean(jnp.square(xf - mu), axis=-1, keepdims=True)
    y = (xf - mu) * lax.rsqrt(var + EPS) * g.astype(jnp.float32) + b.astype(jnp.float32)
    return y.astype(x.dtype)

def ada_modulation(cond, w_ada, b_ada):
    m = jax.nn.silu(cond) @ w_ada + b_ada
    return jnp.split(m[..., None, :], 6, axis=-1)

def axial_rope(x):
    L = x.shape[1]
    t = jnp.arange(L)
    row, col = t // GRID_W, t % GRID_W

    def rot(xh, pos):
        half = xh.shape[-1] // 2
        freqs = 1.0 / (ROPE_THETA ** (jnp.arange(half, dtype=jnp.float32) / half))
        ang = pos.astype(jnp.float32)[:, None] * freqs[None, :]
        cos = jnp.cos(ang)[:, None, :].astype(xh.dtype)
        sin = jnp.sin(ang)[:, None, :].astype(xh.dtype)
        x1, x2 = xh[..., :half], xh[..., half:]
        return jnp.concatenate([x1 * cos - x2 * sin, x1 * sin + x2 * cos], axis=-1)

    r = HEAD_DIM // 2
    return jnp.concatenate([rot(x[..., :r], row), rot(x[..., r:], col)], axis=-1)

def depthwise_conv(u, w, b):
    ch = u.shape[-1]
    y = lax.conv_general_dilated(u, w[:, None, :], window_strides=(1,),
                                 padding=((CONV_K // 2, CONV_K // 2),),
                                 dimension_numbers=('NWC', 'WIO', 'NWC'),
                                 feature_group_count=ch)
    return y + b

def fourier_mix(f):
    B, L, _ = f.shape
    fg = f.reshape(B, L, FNET_GROUPS, FNET_GDIM).astype(jnp.float32)
    out = jnp.fft.fft2(fg, axes=(1, 3), norm='ortho').real
    return out.reshape(B, L, BRANCH_W).astype(f.dtype)

def ctx_attention(q, k, v, sink):
    B, L, hq, d = q.shape
    hkv = k.shape[1]
    g = hq // hkv
    qh = q.reshape(B, L, hkv, g, d).transpose(0, 2, 3, 1, 4)
    s = jnp.einsum('bkgqd,bkcd->bkgqc', qh, k).astype(jnp.float32) * ATTN_SCALE
    if sink is not None:
        sk = jnp.broadcast_to(sink.astype(jnp.float32).reshape(1, hkv, g, 1, 1), s.shape[:-1] + (1,))
        p = jax.nn.softmax(jnp.concatenate([s, sk], axis=-1), axis=-1)[..., :-1]
    else:
        p = jax.nn.softmax(s, axis=-1)
    o = jnp.einsum('bkgqc,bkcd->bkgqd', p.astype(v.dtype), v)
    return o.transpose(0, 3, 1, 2, 4).reshape(B, L, hq * d)

def window_attention(q, k, v, ctx_k, ctx_v, sink):
    B, L, hq, d = q.shape
    hkv = k.shape[2]
    g = hq // hkv
    nb = L // WIN_BLOCK
    qb = q.reshape(B, nb, WIN_BLOCK, hkv, g, d).transpose(0, 3, 4, 1, 2, 5)

    def band(t):
        tp = jnp.pad(t, ((0, 0), (WIN_BLOCK, WIN_BLOCK), (0, 0), (0, 0)))
        tp = tp.reshape(B, nb + 2, WIN_BLOCK, hkv, d).transpose(0, 3, 1, 2, 4)
        return jnp.concatenate([tp[:, :, 0:nb], tp[:, :, 1:nb + 1], tp[:, :, 2:nb + 2]], axis=3)

    kb, vb = band(k), band(v)
    n = jnp.arange(nb)[:, None, None]
    a = jnp.arange(WIN_BLOCK)[None, :, None]
    j = jnp.arange(3 * WIN_BLOCK)[None, None, :]
    kpos = (n - 1) * WIN_BLOCK + j
    valid = (jnp.abs(j - WIN_BLOCK - a) <= WINDOW) & (kpos >= 0) & (kpos < L)
    s_loc = jnp.einsum('bkgnqd,bknjd->bkgnqj', qb, kb).astype(jnp.float32) * ATTN_SCALE
    s_loc = jnp.where(valid, s_loc, NEG)
    s_ctx = jnp.einsum('bkgnqd,bkcd->bkgnqc', qb, ctx_k).astype(jnp.float32) * ATTN_SCALE
    s_sink = jnp.broadcast_to(sink.astype(jnp.float32).reshape(1, hkv, g, 1, 1, 1), s_ctx.shape[:-1] + (1,))
    p = jax.nn.softmax(jnp.concatenate([s_loc, s_ctx, s_sink], axis=-1), axis=-1).astype(v.dtype)
    nloc = 3 * WIN_BLOCK
    lc = ctx_k.shape[2]
    o = (jnp.einsum('bkgnqj,bknjd->bkgnqd', p[..., :nloc], vb)
         + jnp.einsum('bkgnqc,bkcd->bkgnqd', p[..., nloc:nloc + lc], ctx_v))
    return o.transpose(0, 3, 4, 1, 2, 5).reshape(B, L, hq * d)

def neighborhood_attention(q, k, v, ctx_k, ctx_v, rel_bias):
    B, L, H, d = q.shape
    rows = L // GRID_W
    kr = min(NA_ROWS, rows)

    def grid(t):
        return t.reshape(B, rows, GRID_W, H, d).transpose(0, 3, 1, 2, 4)

    qg, kg, vg = grid(q), grid(k), grid(v)
    r = jnp.arange(rows)
    row_idx = jnp.clip(r - kr // 2, 0, rows - kr)[:, None] + jnp.arange(kr)[None, :]
    k_rows = kg[:, :, row_idx]
    v_rows = vg[:, :, row_idx]
    cq = jnp.arange(GRID_W)
    col_start = jnp.clip(cq - NA_COLS // 2, 0, GRID_W - NA_COLS)[:, None]
    col_ok = (cq[None, :] >= col_start) & (cq[None, :] < col_start + NA_COLS)
    row_off = row_idx - r[:, None] + (NA_ROWS - 1)
    col_off = jnp.clip(cq[None, :] - cq[:, None] + (NA_COLS - 1), 0, 2 * NA_COLS - 2)
    bias = rel_bias.astype(jnp.float32)[:, row_off[:, None, :, None], col_off[None, :, None, :]]
    s = jnp.einsum('bhrqd,bhrkwd->bhrqkw', qg, k_rows).astype(jnp.float32) * ATTN_SCALE + bias
    s = jnp.where(col_ok[:, None, :], s, NEG).reshape(B, H, rows, GRID_W, kr * GRID_W)
    s_ctx = jnp.einsum('bhrqd,bhcd->bhrqc', qg, ctx_k).astype(jnp.float32) * ATTN_SCALE
    p = jax.nn.softmax(jnp.concatenate([s, s_ctx], axis=-1), axis=-1).astype(v.dtype)
    nloc = kr * GRID_W
    p_loc = p[..., :nloc].reshape(B, H, rows, GRID_W, kr, GRID_W)
    o = (jnp.einsum('bhrqkw,bhrkwd->bhrqd', p_loc, v_rows)
         + jnp.einsum('bhrqc,bhcd->bhrqd', p[..., nloc:], ctx_v))
    return o.transpose(0, 2, 3, 1, 4).reshape(B, L, H * d)

def token_mixers(h, w_in, conv_w, conv_b, conv_ln_g, conv_ln_b, win_sink, na_bias, w_branch, w_out, ctx):
    B, L, _ = h.shape
    z = h @ w_in
    a_in, f_in, cq, ck, cv, dq, dk, dv, gate_logits = jnp.split(z, SPLITS, axis=-1)
    ga, gb = jnp.split(a_in, 2, axis=-1)
    br_a = jax.nn.silu(layer_norm(depthwise_conv(ga * jax.nn.sigmoid(gb), conv_w, conv_b), conv_ln_g, conv_ln_b))
    br_b = fourier_mix(f_in)
    cq = cq.reshape(B, L, WIN_Q_HEADS, HEAD_DIM)
    ck = ck.reshape(B, L, WIN_KV_HEADS, HEAD_DIM)
    cv = cv.reshape(B, L, WIN_KV_HEADS, HEAD_DIM)
    dq = dq.reshape(B, L, NA_HEADS, HEAD_DIM)
    dk = dk.reshape(B, L, NA_HEADS, HEAD_DIM)
    dv = dv.reshape(B, L, NA_HEADS, HEAD_DIM)
    if ctx is None:
        win_k, win_v = ck.transpose(0, 2, 1, 3), cv.transpose(0, 2, 1, 3)
        nat_k, nat_v = dk.transpose(0, 2, 1, 3), dv.transpose(0, 2, 1, 3)
        br_c = ctx_attention(cq, win_k, win_v, win_sink)
        br_d = ctx_attention(dq, nat_k, nat_v, None)
        ctx_out = (win_k, win_v, nat_k, nat_v)
    else:
        win_k, win_v, nat_k, nat_v = ctx
        br_c = window_attention(axial_rope(cq), axial_rope(ck), cv, win_k, win_v, win_sink)
        br_d = neighborhood_attention(dq, dk, dv, nat_k, nat_v, na_bias)
        ctx_out = ()
    branches = jnp.stack([br_a, br_b, br_c, br_d], axis=2)
    proj = jnp.einsum('blnc,ncd->blnd', branches, w_branch)
    gates = jax.nn.sigmoid(gate_logits.reshape(B, L, N_BRANCH, D_MODEL).astype(jnp.float32)).astype(h.dtype)
    merged = jnp.einsum('blnd,blnd->bld', gates, proj)
    return merged @ w_out, ctx_out

def expert_choice_ffn(h, w_router, w_gate, w_up, w_down):
    B, L, D = h.shape
    cap = EC_CAPACITY * L // N_EXPERTS
    aff = jax.nn.softmax((h @ w_router).astype(jnp.float32), axis=-1)
    g, idx = lax.top_k(jnp.swapaxes(aff, 1, 2), cap)
    xs = jax.vmap(lambda hb, ib: hb[ib])(h, idx)
    a = jnp.einsum('becd,edf->becf', xs, w_gate)
    u = jnp.einsum('becd,edf->becf', xs, w_up)
    y = jnp.einsum('becf,efd->becd', jax.nn.silu(a) * u, w_down) * g[..., None].astype(h.dtype)
    return jax.vmap(lambda ib, yb: jnp.zeros((L, D), yb.dtype).at[ib.reshape(-1)].add(yb.reshape(-1, D)))(idx, y)

def setup_inputs(seed: int = 0) -> dict:
    key = jax.random.key(seed)
    ks = jax.random.split(key, 32)

    def nrm(k, shape, s):
        return jax.random.normal(k, shape, jnp.float32) * s

    return {
        'x_prompt': nrm(ks[0], (BATCH, SEQ, D_MODEL), 1.0),
        'x_sample': nrm(ks[1], (DEC_BATCH, DEC_SEQ, D_MODEL), 1.0),
        'cache_win_k': nrm(ks[2], (DEC_BATCH, DEPTH, WIN_KV_HEADS, PAST_LEN, HEAD_DIM), 1.0),
        'cache_win_v': nrm(ks[3], (DEC_BATCH, DEPTH, WIN_KV_HEADS, PAST_LEN, HEAD_DIM), 1.0),
        'cache_nat_k': nrm(ks[4], (DEC_BATCH, DEPTH, NA_HEADS, PAST_LEN, HEAD_DIM), 1.0),
        'cache_nat_v': nrm(ks[5], (DEC_BATCH, DEPTH, NA_HEADS, PAST_LEN, HEAD_DIM), 1.0),
        'c': nrm(ks[6], (DEC_BATCH, D_MODEL), 1.0),
        'c_ctx': nrm(ks[7], (D_MODEL,), 1.0),
        'norm1_g': 1.0 + nrm(ks[8], (DEPTH, D_MODEL), 0.02),
        'norm2_g': 1.0 + nrm(ks[9], (DEPTH, D_MODEL), 0.02),
        'w_ada': nrm(ks[10], (DEPTH, D_MODEL, 6 * D_MODEL), 0.5 * D_MODEL ** -0.5),
        'b_ada': nrm(ks[11], (DEPTH, 6 * D_MODEL), 0.02),
        'w_in': nrm(ks[12], (DEPTH, D_MODEL, IN_COLS), D_MODEL ** -0.5),
        'conv_w': nrm(ks[13], (DEPTH, CONV_K, BRANCH_W), CONV_K ** -0.5),
        'conv_b': nrm(ks[14], (DEPTH, BRANCH_W), 0.02),
        'conv_ln_g': 1.0 + nrm(ks[15], (DEPTH, BRANCH_W), 0.02),
        'conv_ln_b': nrm(ks[16], (DEPTH, BRANCH_W), 0.02),
        'win_sink': nrm(ks[17], (DEPTH, WIN_Q_HEADS), 0.5),
        'na_bias': nrm(ks[18], (DEPTH, NA_HEADS, 2 * NA_ROWS - 1, 2 * NA_COLS - 1), 0.2),
        'w_branch': nrm(ks[19], (DEPTH, N_BRANCH, BRANCH_W, D_MODEL), BRANCH_W ** -0.5),
        'w_out': nrm(ks[20], (DEPTH, D_MODEL, D_MODEL), D_MODEL ** -0.5),
        'w_router': nrm(ks[21], (DEPTH, D_MODEL, N_EXPERTS), D_MODEL ** -0.5),
        'w_e_gate': nrm(ks[22], (DEPTH, N_EXPERTS, D_MODEL, EXPERT_FF), D_MODEL ** -0.5),
        'w_e_up': nrm(ks[23], (DEPTH, N_EXPERTS, D_MODEL, EXPERT_FF), D_MODEL ** -0.5),
        'w_e_down': nrm(ks[24], (DEPTH, N_EXPERTS, EXPERT_FF, D_MODEL), EXPERT_FF ** -0.5),
        'final_norm_g': 1.0 + nrm(ks[25], (D_MODEL,), 0.02),
    }

def reference(x_prompt, x_sample, cache_win_k, cache_win_v, cache_nat_k, cache_nat_v, c, c_ctx,
              norm1_g, norm2_g, w_ada, b_ada, w_in, conv_w, conv_b, conv_ln_g, conv_ln_b,
              win_sink, na_bias, w_branch, w_out, w_router, w_e_gate, w_e_up, w_e_down, final_norm_g):
    xp, xs = x_prompt, x_sample
    wk_list, wv_list, nk_list, nv_list = [], [], [], []
    for l in range(DEPTH):
        mix_w = (w_in[l], conv_w[l], conv_b[l], conv_ln_g[l], conv_ln_b[l], win_sink[l], na_bias[l], w_branch[l], w_out[l])
        ffn_w = (w_router[l], w_e_gate[l], w_e_up[l], w_e_down[l])
        sh1, sc1, g1, sh2, sc2, g2 = ada_modulation(c_ctx, w_ada[l], b_ada[l])
        mix, (wk, wv, nk, nv) = token_mixers(rms_norm(xp, norm1_g[l]) * (1 + sc1) + sh1, *mix_w, None)
        xp = xp + g1 * mix
        xp = xp + g2 * expert_choice_ffn(rms_norm(xp, norm2_g[l]) * (1 + sc2) + sh2, *ffn_w)
        wk_list.append(wk)
        wv_list.append(wv)
        nk_list.append(nk)
        nv_list.append(nv)
        ctx = (cache_win_k[:, l], cache_win_v[:, l], cache_nat_k[:, l], cache_nat_v[:, l])
        sh1, sc1, g1, sh2, sc2, g2 = ada_modulation(c, w_ada[l], b_ada[l])
        mix, _ = token_mixers(rms_norm(xs, norm1_g[l]) * (1 + sc1) + sh1, *mix_w, ctx)
        xs = xs + g1 * mix
        xs = xs + g2 * expert_choice_ffn(rms_norm(xs, norm2_g[l]) * (1 + sc2) + sh2, *ffn_w)
    y_prompt = rms_norm(xp, final_norm_g)
    y_sample = rms_norm(xs, final_norm_g)
    new_win_k = jnp.stack(wk_list, axis=1)
    new_win_v = jnp.stack(wv_list, axis=1)
    new_nat_k = jnp.stack(nk_list, axis=1)
    new_nat_v = jnp.stack(nv_list, axis=1)
    return (y_prompt, y_sample, new_win_k, new_win_v, new_nat_k, new_nat_v)


_drawn_inputs = setup_inputs


def setup_inputs(seed=0):
    import zlib

    import numpy as np

    out = dict(_drawn_inputs(seed))
    spreads = {}
    factors = {'cache_win_k': 4.584,
     'cache_win_v': 3.955,
     'cache_nat_k': 2.87,
     'norm1_g': 2.912,
     'norm2_g': 6.754,
     'conv_b': 8.0,
     'conv_ln_g': 8.0,
     'conv_ln_b': 8.0,
     'win_sink': 64.0,
     'na_bias': 8.0,
     'final_norm_g': 7.781}
    for name, (base, spread) in spreads.items():
        noise = np.random.default_rng([zlib.crc32(name.encode()), seed]).standard_normal(out[name].shape)
        drawn = base * np.exp(spread * noise) if base else spread * noise
        out[name] = __import__('jax').numpy.asarray(drawn.astype(out[name].dtype))
    for name, factor in factors.items():
        out[name] = (out[name] * factor).astype(out[name].dtype)
    return out
```

```python
from contextlib import ExitStack

import numpy as np

import concourse.bass as bass
from concourse import mybir

F32 = mybir.dt.float32
ALU = mybir.AluOpType
ACT = mybir.ActivationFunctionType
AX_X = mybir.AxisListType.X

P = 128
D = 1024
KT = D // P
SEQ, DEC = 128, 256
TOK = SEQ + DEC
TT = TOK // P
DEPTH = 2
BW = 256
HD = 64
CONV_K = 31
NE, FF = 16, 1024
CAP_P, CAP_S = 2 * SEQ // NE, 2 * DEC // NE
SLOTS = 32
GRP = 4
EPS = 1e-6
NEG = -1e30
SCALE = HD ** -0.5
CH = 512
NADA = 6 * D // CH
PADC = CONV_K // 2
UW = PADC + SEQ + 2 * PADC + DEC + PADC
AW = UW - CONV_K + 1
USAMP = PADC + SEQ + 2 * PADC
NSLOT = 6

CONST_COLS = dict(ident=128, dft_s=1024, dft_p=256, dftc=256, cos=256, sin=256, rot=128,
                  winmask=512, namask=512, iota=32, esum=256)


def const_at(name):
    at = 0
    for n, w in CONST_COLS.items():
        if n == name:
            return at, at + w
        at += w


def constants():
    c = np.zeros((P, sum(CONST_COLS.values())), np.float32)

    def put(name, a):
        lo, hi = const_at(name)
        c[:, lo:hi] = np.asarray(a, np.float64).reshape(P, hi - lo)

    put("ident", np.eye(P))

    def dft(n):
        k = np.outer(np.arange(n), np.arange(n)) % n
        return np.cos(2 * np.pi * k / n), np.sin(2 * np.pi * k / n)

    cs, ss = dft(DEC)
    both = np.concatenate([cs, ss], 1) / np.sqrt(DEC)
    put("dft_s", both.reshape(2, P, 2 * DEC).transpose(1, 0, 2))
    cp, sp = dft(SEQ)
    put("dft_p", np.concatenate([cp, sp], 1) / np.sqrt(SEQ))
    cc, sc = dft(HD)
    eye2 = np.eye(2)
    put("dftc", np.concatenate([np.kron(eye2, cc), -np.kron(eye2, sc)], 1) / np.sqrt(HD))
    t = np.arange(DEC)
    row, col = t // 64, t % 64
    d = np.arange(P) % HD
    freqs = (1.0 / (np.float32(10000.0) ** (np.arange(16, dtype=np.float32) / np.float32(16)))).astype(np.float32)
    pos = np.where((d // 32 == 0)[:, None], row[None], col[None]).astype(np.float32)
    ang = pos * freqs[d % 16][:, None]
    put("cos", np.cos(ang))
    put("sin", np.sin(ang))
    r = np.zeros((P, P))
    for m in range(P):
        if m % 32 < 16:
            r[m + 16, m] = -1.0
        else:
            r[m - 16, m] = 1.0
    put("rot", r)
    q, k = np.arange(DEC)[:, None], np.arange(DEC)[None]
    win = np.where(np.abs(k - q) <= 128, 0.0, NEG)
    put("winmask", win.reshape(2, P, DEC).transpose(1, 0, 2))
    start = np.clip(q % 64 - 8, 0, 48)
    na = np.where((k % 64 >= start) & (k % 64 < start + 16), 0.0, NEG)
    put("namask", na.reshape(2, P, DEC).transpose(1, 0, 2))
    put("iota", np.tile(np.arange(SLOTS), (P, 1)))
    e = np.zeros((P, 2, P))
    for i in range(2):
        e[i::32, i, :] = 1.0
    put("esum", e)
    return c


class BankTurns:

    def __init__(self):
        self.at, self.turns, self.copies = {}, [0] * 8, [0] * 8

    def add(self, name, bank, copies=1):
        self.at[name] = (bank, self.turns[bank], self.copies[bank], copies)
        self.turns[bank] += 1
        self.copies[bank] += copies


def build(nc, A):
    ctx = ExitStack()
    with ctx:
        def sb(name, shape):
            return ctx.enter_context(nc.sbuf_tensor(name, shape, F32))

        sems = []

        def sem(name):
            s = ctx.enter_context(nc.semaphore(name))
            sems.append(s)
            return s

        once = {n: ctx.enter_context(nc.semaphore(n)) for n in
                ("x_in", "cond_in", "cond_t", "cond_zero", "cond_ready",
                 "fin_g_in", "fin_sq", "fin_ms", "fin_sd", "fin_rs", "fin_n", "fin_y", "fin_out")}

        ring = sb("ring", [P, NSLOT, KT // 2 * D])
        X = sb("X", [P, TT, D])
        XN = sb("XN", [P, TT, D])
        C = sb("C", [P, sum(CONST_COLS.values())])
        GROW = sb("GROW", [P, 2, 2, D])
        condT = sb("condT", [P, KT, 32])
        MOD = sb("MOD", [P, 48, 2])
        SC = sb("SC", [P, 2, KT, 2])
        PRM = sb("PRM", [P, 132])
        SS = sb("SS", [P, 4])
        MS = sb("MS", [P, 4])
        SD = sb("SD", [P, 4])
        RS = sb("RS", [P, 4])
        WR = sb("WR", [P, KT, NE])
        arena = sb("arena", [P, 13900])
        psum = ctx.enter_context(nc.psum_tensor("psum", [P, 8, 512], F32))

        def cst(name, **kw):
            lo, hi = const_at(name)
            return C[:, lo:hi]

        ident = cst("ident")
        dft_s = cst("dft_s").rearrange("p (k n) -> p k n", k=2)
        dft_p = cst("dft_p")
        dftc = cst("dftc").rearrange("p (k n) -> p k n", k=2)
        cosT, sinT, rot = cst("cos"), cst("sin"), cst("rot")
        winmask = cst("winmask").rearrange("p (q n) -> p q n", q=2)
        namask = cst("namask").rearrange("p (q n) -> p q n", q=2)
        iota = cst("iota")
        esum = cst("esum").rearrange("p (i n) -> p i n", i=2)

        cursor = [0]

        def part(n, base=None):
            lo = cursor[0] if base is None else base
            if base is None:
                cursor[0] += n
            return arena[:, lo:lo + n]

        HT = part(KT * TOK).rearrange("p (k t) -> p k t", k=KT)
        mrg_at = cursor[0]
        MRG = part(KT * TOK).rearrange("p (k t) -> p k t", k=KT)
        LNX = part(TT * BW, mrg_at).rearrange("p (t c) -> p t c", t=TT)
        ADAS = part(2 * CH, mrg_at + 768).rearrange("p (b n) -> p b n", b=2)
        ZF = part(TT * BW, mrg_at + 1792).rearrange("p (t c) -> p t c", t=TT)
        U = part(2 * UW).rearrange("p (c n) -> p c n", c=2)
        ACC = part(2 * AW).rearrange("p (c n) -> p c n", c=2)
        LATE = part(2 * CH, cursor[0] - 2 * AW - 2 * UW).rearrange("p (b n) -> p b n", b=2)

        def adas(c):
            return (ADAS if c < 4 else LATE)[:, c % 2, :]

        CT = part(3 * P).rearrange("p (c n) -> p c n", c=3)
        KC = part(6 * HD).rearrange("p (h d) -> p h d", h=6)
        VC = part(6 * HD).rearrange("p (h d) -> p h d", h=6)
        ZV = part(TT * 384).rearrange("p (t c) -> p t c", t=TT)
        KO = part(384)
        SIG = part(2 * TOK).rearrange("p (b n) -> p b n", b=2)
        GP = part(2 * TOK).rearrange("p (b n) -> p b n", b=2)
        WOT = part(2 * CH, cursor[0] - 4 * TOK).rearrange("p (b n) -> p b n", b=2)
        PTB = part(2 * 384).rearrange("p (b n) -> p b n", b=2)
        PR = part(2 * P).rearrange("p (b n) -> p b n", b=2)
        BN = part(TT * 6).rearrange("p (t n) -> p t n", t=TT)
        MV = part(TT * 2).rearrange("p (t n) -> p t n", t=TT)
        LSD = part(TT)
        LRS = part(TT)
        SINK = part(4)
        MX = part(4)
        NM = part(4)
        DS = part(4)
        ES = part(4)
        SM = part(4)
        RI = part(4)
        assert cursor[0] <= 13900, cursor[0]
        tmp = ring[:, 4:6, :].rearrange("p s n -> p (s n)")
        QC = tmp[:, 0:768].rearrange("p (a t) -> p a t", a=2)
        KTC = tmp[:, 768:1152]
        DQ = tmp[:, 1152:1920].rearrange("p (a t) -> p a t", a=2)
        DK = tmp[:, 1920:2688].rearrange("p (a t) -> p a t", a=2)
        NAB = tmp[:, 2688:4736].rearrange("p (q h n) -> p q h n", q=2, h=4)
        SCB = tmp[:, 4736:6272].rearrange("p (h n) -> p h n", h=4)
        FG = tmp[:, 6272:7808].rearrange("p (c n) -> p c n", c=2)
        ROTT = tmp[:, 7808:8064]
        BRT = XN[:, :, :].rearrange("p t n -> p (t n)").rearrange("p (b c t) -> p b c t", b=4, c=2)
        cursor[0] = KT * TOK
        XE = part(KT * GRP * 64).rearrange("p (k e s) -> p k e s", k=KT, e=GRP)
        SEL = part(TT * P).rearrange("p (t e s) -> p t e s", t=TT, e=GRP)
        SELG = part(TT * P).rearrange("p (t e s) -> p t e s", t=TT, e=GRP)
        PG = part(TT * P).rearrange("p (t n) -> p t n", t=TT)
        TMP = part(FF)
        AA = part(FF)
        AT = part(KT * 64).rearrange("p (k s) -> p k s", k=KT)
        YS = part(D)
        YP = part(D)
        CMB = part(2 * CH).rearrange("p (b n) -> p b n", b=2)
        AFF = part(TT * NE).rearrange("p (t e) -> p t e", t=TT)
        POSG = part(TT * NE).rearrange("p (g n) -> p g n", g=NE // GRP)
        AFFG = part(TT * NE).rearrange("p (g n) -> p g n", g=NE // GRP)
        WK = part(TOK)
        MSK = part(TOK)
        ONE = part(TOK)
        CUM = part(TOK)
        M8 = part(8)
        RMX = part(4)
        RSM = part(4)
        RRI = part(4)
        assert cursor[0] <= 13900, cursor[0]

        with nc.Block() as block:
            @block.sync
            def _(sp):
                sp.dma_start(C[:, :], A["const"]).then_inc(once["x_in"], 16)
                sp.dma_start(X[:, 0, :], A["x_prompt"].rearrange("b s d -> (b s) d")).then_inc(once["x_in"], 16)
                sp.dma_start(X[:, 1:3, :], A["x_sample"].rearrange("b (t p) d -> p (b t) d", p=P)).then_inc(once["x_in"], 16)
                sp.dma_start(XN[0:8, 0, 0:P], A["c_ctx"].rearrange("(k p) -> k p", p=P)).then_inc(once["cond_in"], 16)
                sp.dma_start(XN[8:16, 0, 0:P], A["c"].rearrange("b (k p) -> (b k) p", p=P)).then_inc(once["cond_in"], 16)
                sp.wait_ge(once["x_in"], 48)

            @block.vector
            def _(dve):
                nc.vector.memset(condT[:, :, :], 0.0).then_inc(once["cond_zero"], 1)

            @block.tensor
            def _(pe):
                pe.wait_ge(once["cond_in"], 32)
                pe.wait_ge(once["x_in"], 48)
                nc.tensor.transpose(psum[:, 0, 0:16], XN[0:16, 0, 0:P], ident[0:16, 0:16]).then_inc(once["cond_t"], 1)

            @block.scalar
            def _(act):
                act.wait_ge(once["cond_zero"], 1)
                act.wait_ge(once["cond_t"], 1)
                nc.scalar.activation(condT[:, :, 0:2], psum[:, 0, 0:16].rearrange("p (i k) -> p k i", i=2),
                                     ACT.Silu).then_inc(once["cond_ready"], 1)
                act.wait_ge(once["cond_ready"], 1)

        land = [sem(f"land{s}") for s in range(NSLOT)]
        e_land = [sem(f"e_land{s}") for s in range(NSLOT)]
        full = [sem(f"full{b}") for b in range(8)]
        free = [sem(f"free{b}") for b in range(8)]
        e_full = [sem(f"e_full{b}") for b in range(8)]
        e_free = [sem(f"e_free{b}") for b in range(8)]
        names = ("prm_in grow_in sink_in cache_in nab_in nab_ready u_zero sq_done ms_ready sd_ready rs_ready xn_ready "
                 "sc_ready dve_step route_step conv_step rope_ready scores_done scores_read nmax_ready exps_done p_ready "
                 "pv0 pv1 gate_add out_kv n2_sq n2_ms n2_sd n2_rs n2_xn wr_in router_max router_exp aff_ready affg_ready "
                 "cum_ready sel_ready selg_ready e_half e_down_half silu_done x_done").split()
        S = {n: sem(n) for n in names}

        order = ["ada0", "ada1", "ada2", "ada3", "w0", "w1", "w2", "w3", "wb01", "w6", "ada4", "w7", "ada5", "w4", "ada6",
                 "w5", "ada7", "wb23", "w8", "ada8", "w9", "ada9", "w10", "ada10", "w11", "ada11", "wo0", "wo1"]
        done_at = {n: i - 8 for i, n in enumerate(order[:8])}
        done_at.update(wb01=15, wb23=31, w6=3, w7=7, w4=11, w5=15, w8=19, w9=23, w10=27, w11=31, wo0=32, wo1=32)
        done_at.update({f"ada{4 + m}": 4 * m + 3.5 for m in range(8)})
        unit_at, used, before, latest, units = {}, [0] * NSLOT, {}, {}, []
        for name in order:
            s = min(range(4), key=lambda x: done_at[latest[x]] if x in latest else x - 100)
            units.append((name, s))
            unit_at[name] = (s, used[s])
            before[name] = latest.get(s)
            latest[s] = name
            used[s] += 1

        def slot(name, cols):
            return ring[:, unit_at[name][0], :].rearrange("p (k n) -> p k n", n=cols)

        ln_var_step = [2 + 3 + 3 + 3 + 1]

        T = BankTurns()
        seq = {"a": 0, "b": 0}

        def tile_a(name):
            T.add(name, seq["a"] % 4)
            seq["a"] += 1

        def tile_b(name):
            T.add(name, 4 + seq["b"] % 4)
            seq["b"] += 1

        tile_b("prm")
        for c in range(4):
            tile_a(f"ada{c}")
            tile_b(f"md{c}")
        for k in range(KT):
            tile_a(f"xt{k}")
        for n in ("gb0", "ga0", "gb1", "ga1", "zf0", "zf1", "zf2", "cq0", "cq1"):
            tile_a(n)
        for n in ("ctxT", "fgs0", "fgp0", "fgs1", "fgp1"):
            tile_b(n)
        tile_a("ck")
        tile_b("fo0")
        tile_b("fo1")
        for n in ("zcv", "dq0", "dq1", "dk0", "dk1", "zdv0", "zdv1", "zdv2"):
            tile_a(n)
        for n in ("ko", "rot0", "rot1", "rotk"):
            tile_b(n)
        for n in ("lt0", "lt1", "lt2", "lb0", "lb1"):
            tile_b(n)
        while seq["b"] % 4:
            seq["b"] += 1
        GATE_CHUNKS = (4, 5, 10, 11)

        def ada_small_tiles(c):
            for n in ([f"gr{c}_0", f"gr{c}_1"] if c in GATE_CHUNKS else [f"md{c}"]):
                tile_a(n)

        GATE_ORDER = [1, 0, 2, 3]
        ATT = [("c", 0), ("c", 1), ("d", 0), ("d", 1), ("c", None), ("d", None)]
        for n in GATE_ORDER:
            for k in range(KT):
                idx = GATE_ORDER.index(n) * KT + k
                g = idx // 2 - 1
                if idx % 2 == 0 and 0 <= g < len(ATT):
                    for h in range(4):
                        tile_b(f"pt{g}_{h}")
                    tile_a(f"o{g}")
                tile_a(f"g{n}_{k}")
                tile_a(f"p{n}_{k}")
                if idx % 4 == 3:
                    tile_a(f"ada{4 + idx // 4}")
                if idx % 4 == 0 and idx:
                    ada_small_tiles(3 + idx // 4)
        ada_small_tiles(NADA - 1)
        for t in range(TT):
            for half in range(2):
                tile_a(f"wo{t}_{half}")

        for k in range(KT):
            tile_a(f"yt{k}")
        for n in ("rt", "aft", "post"):
            tile_b(n)

        def open_tile(pe, name):
            b, _, copies_before, _ = T.at[name]
            if copies_before:
                pe.wait_ge(free[b], copies_before)
            return psum[:, b, :]

        def close_tile(ins, name):
            ins.then_inc(full[T.at[name][0]], 1)

        def take(eng, name):
            b, n, _, _ = T.at[name]
            eng.wait_ge(full[b], n + 1)
            return psum[:, b, :]

        def release(ins, name):
            ins.then_inc(free[T.at[name][0]], 1)

        def copied(eng, name):
            b, _, copies_before, copies = T.at[name]
            eng.wait_ge(free[b], copies_before + copies)

        last_tile = {f"ada{c}": f"ada{c}" for c in range(NADA)}
        last_tile.update(w0="ga1", w1="cq1", w2="dq1", w3="zdv2", wb01="p0_7", wb23="p3_7", wo0="wo2_1", wo1="wo2_1")
        last_tile.update({f"w{4 + 2 * n + h}": f"g{n}_{4 * h + 3}" for n in range(4) for h in range(2)})

        def w_unit(l, name):
            kind = name[:3]
            if kind == "ada":
                c = int(name[3:])
                return A["w_ada"][bass.ds(l, 1), :, c * CH:(c + 1) * CH].rearrange("o (k p) n -> p (o k) n", p=P)
            if name[:2] == "wb":
                b = int(name[2])
                return A["w_branch"][bass.ds(l, 1), b:b + 2].rearrange("o b (c p) n -> p (o b c) n", p=P)
            if name[:2] == "wo":
                h = int(name[2])
                return A["w_out"][bass.ds(l, 1), h * 512:(h + 1) * 512, :].rearrange("o (k p) n -> p (o k) n", p=P)
            c = int(name[1:])
            return A["w_in"][bass.ds(l, 1), :, c * CH:(c + 1) * CH].rearrange("o (k p) n -> p (o k) n", p=P)

        E_SRC = (("w_e_gate", 0, 0), ("w_e_up", 0, 2), ("w_e_gate", 1, 1), ("w_e_up", 1, 3), ("w_e_down", 0, 4), ("w_e_down", 1, 5))

        def e_unit(l, e, name, half):
            return A[name][bass.ds(l, 1), bass.ds(e, 1), half * 512:(half + 1) * 512, :].rearrange(
                "o e (k p) n -> p (o e k) n", p=P)

        def e_dst(s):
            return ring[:, s, :].rearrange("p (k n) -> p k n", n=D)

        E = BankTurns()
        for k in range(KT):
            E.add(f"xe{k}", 6 + k % 2)
        E.add("pg", 7)
        for j in range(GRP):
            for half in range(2):
                E.add(f"gu{j}_{half}", 2 * (j % 2) + half)
            E.add(f"at{j}", 6)
            E.add(f"y{j}", 4 + j % 2, 2)
        for i in range(6):
            E.add(f"cm{i}", (7, 0, 1, 2, 3, 6)[i])

        def e_open(pe, g, name):
            b, _, copies_before, _ = E.at[name]
            pe.wait_ge(e_free[b], g * E.copies[b] + copies_before + 1)
            return psum[:, b, :]

        def e_close(ins, name):
            ins.then_inc(e_full[E.at[name][0]], 1)

        def e_take(eng, g, name):
            b, n, _, _ = E.at[name]
            eng.wait_ge(e_full[b], g * E.turns[b] + n + 1)
            return psum[:, b, :]

        def e_release(ins, name):
            ins.then_inc(e_free[E.at[name][0]], 1)

        def e_copied(eng, g, name):
            b, _, copies_before, copies = E.at[name]
            eng.wait_ge(e_free[b], g * E.copies[b] + copies_before + copies + 1)

        def modulate_act(dst, src, which, sec, k, i):
            return nc.scalar.activation(dst, src, ACT.Identity, scale=SC[:, which, k, i:i + 1], bias=MOD[:, sec * KT + k, i:i + 1])

        def modulate_dve(dst, src, which, sec, k, i):
            return nc.vector.tensor_scalar(dst, src, SC[:, which, k, i:i + 1], MOD[:, sec * KT + k, i:i + 1], ALU.mult, ALU.add)

        def rms_part_act(act, sq_sem, ms_sem, sd_sem):
            for t in range(TT):
                nc.scalar.activation(XN[:, t, :], X[:, t, :], ACT.Square, accum_out=SS[:, t:t + 1]).then_inc(sq_sem, 1)
            act.wait_ge(ms_sem, 1)
            nc.scalar.activation(SD[:, 0:TT], MS[:, 0:TT], ACT.Sqrt).then_inc(sd_sem, 1)

        def rms_part_dve(dve, sq_sem, ms_sem, sd_sem, rs_sem, xn_sem):
            dve.wait_ge(sq_sem, TT)
            nc.vector.tensor_scalar(MS[:, 0:TT], SS[:, 0:TT], 1.0 / D, EPS, ALU.mult, ALU.add).then_inc(ms_sem, 1)
            dve.wait_ge(sd_sem, 1)
            nc.vector.reciprocal(RS[:, 0:TT], SD[:, 0:TT]).then_inc(rs_sem, 1)
            dve.wait_ge(rs_sem, 1)
            for t in range(TT):
                nc.vector.tensor_scalar(XN[:, t, :], X[:, t, :], RS[:, t:t + 1], None, ALU.mult).then_inc(xn_sem, 1)

        with nc.Fori(0, DEPTH) as l:
            with nc.Block() as block:
                @block.sync
                def _(sp):
                    def parameters():
                        for dst, src in (
                            (PR[0:48, 0, :], A["b_ada"][bass.ds(l, 1)].rearrange("o (r p) -> (o r) p", p=P)),
                            (PR[48:56, 0, :], A["norm1_g"][bass.ds(l, 1)].rearrange("o (r p) -> (o r) p", p=P)),
                            (PR[56:64, 0, :], A["norm2_g"][bass.ds(l, 1)].rearrange("o (r p) -> (o r) p", p=P)),
                            (PR[0:62, 1, :], A["conv_w"][bass.ds(l, 1)].rearrange("o k (c p) -> (o k c) p", p=P)),
                            (PR[62:64, 1, :], A["conv_b"][bass.ds(l, 1)].rearrange("o (r p) -> (o r) p", p=P)),
                            (PR[64:66, 1, :], A["conv_ln_g"][bass.ds(l, 1)].rearrange("o (r p) -> (o r) p", p=P)),
                            (PR[66:68, 1, :], A["conv_ln_b"][bass.ds(l, 1)].rearrange("o (r p) -> (o r) p", p=P)),
                        ):
                            sp.dma_start(dst, src).then_inc(S["prm_in"], 16)
                        sp.dma_start(NAB[:, :, :, :].rearrange("p q h n -> p q (h n)"),
                                     A["na_grid"][bass.ds(l, 1)].rearrange("o q p n -> p (o q) n")).then_inc(S["nab_in"], 16)
                        sp.dma_start(SINK, A["win_sink"][bass.ds(l, 1)].broadcast_to((P, 4))).then_inc(S["sink_in"], 16)
                        for name, h0, nh in (("cache_win", 0, 2), ("cache_nat", 2, 4)):
                            for kv, dst in (("k", KC), ("v", VC)):
                                sp.dma_start(dst[:, h0:h0 + nh, :], A[f"{name}_{kv}"][:, bass.ds(l, 1)].rearrange(
                                    "b o h t d -> t (b o h) d")).then_inc(S["cache_in"], 16)

                    def gate_biases():
                        sp.dma_start(WR[:, :, :], A["w_router"][bass.ds(l, 1)].rearrange("o (k p) e -> p (o k) e", p=P)).then_inc(
                            S["wr_in"], 16)
                        for gate, sec in ((0, 2), (1, 5)):
                            for i in range(2):
                                sp.dma_start(GROW[:, gate, i, :], A["b_ada"][bass.ds(l, 1), sec * D:(sec + 1) * D].broadcast_to(
                                    (P, D))).then_inc(S["grow_in"], 16)

                    def prompt_kv():
                        copied(sp, "ko")
                        for n in ("zcv", "zdv0"):
                            copied(sp, n)
                        for name, src, h0, nh in (("new_win_k", KO, 0, 2), ("new_nat_k", KO, 2, 4),
                                                  ("new_win_v", ZV[:, 0, :], 0, 2), ("new_nat_v", ZV[:, 0, :], 2, 4)):
                            sp.dma_start(A[name][:, bass.ds(l, 1)].rearrange("b o h t d -> t (b o h) d"),
                                         src[:, h0 * HD:(h0 + nh) * HD].rearrange("p (h d) -> p h d", d=HD)).then_inc(S["out_kv"], 16)

                    for name, s in units:
                        cols = D if name[:2] in ("wb", "wo") else CH
                        if before[name]:
                            take(sp, last_tile[before[name]])
                        sp.dma_start(slot(name, cols), w_unit(l, name)).then_inc(land[s], 16)
                        if name == "ada3":
                            parameters()
                        elif name == "w3":
                            gate_biases()
                        elif name == "w7":
                            prompt_kv()
                    sp.wait_ge(S["out_kv"], 64)
                    for name, half, s in E_SRC:
                        if s in latest:
                            take(sp, last_tile[latest[s]])
                        elif s == NSLOT - 2:
                            copied(sp, f"o{len(ATT) - 1}")
                        sp.dma_start(e_dst(s), e_unit(l, 0, name, half)).then_inc(e_land[s], 16)

                @block.gpsimd
                def _(pool):
                    nc.gpsimd.memset(U[:, :, :], 0.0).then_inc(S["u_zero"], 1)
                    pool.wait_ge(S["nab_in"], 16)
                    nc.gpsimd.tensor_tensor(NAB, NAB, namask.unsqueeze(2).broadcast_to((P, 2, 4, DEC)),
                                            ALU.add).then_inc(S["nab_ready"], 1)

                @block.tensor
                def _(pe):
                    def landed(name):
                        s, n = unit_at[name]
                        pe.wait_ge(land[s], 16 * (n + 1))

                    ps = open_tile(pe, "prm")
                    pe.wait_ge(S["prm_in"], 7 * 16)
                    nc.tensor.transpose(ps[:, 0:64], PR[0:64, 0, :], ident[0:64, 0:64])
                    close_tile(nc.tensor.transpose(ps[:, 64:132], PR[0:68, 1, :], ident[0:68, 0:68]), "prm")

                    def ada_main(c):
                        name = f"ada{c}"
                        ps = open_tile(pe, name)
                        landed(name)
                        w = slot(name, CH)
                        for k2 in range(2):
                            for j in range(4):
                                ins = nc.tensor.matmul(ps[32 * j:32 * j + 32, :], condT[:, 4 * k2 + j, :], w[:, 4 * k2 + j, :],
                                                       start=(k2 == 0), stop=(k2 == 1))
                        close_tile(ins, name)

                    def ada_mod(c):
                        ps = open_tile(pe, f"md{c}")
                        copied(pe, f"ada{c}")
                        for s in range(4):
                            ins = nc.tensor.matmul(ps[:, 2 * s:2 * s + 2], adas(c)[:, s * P:(s + 1) * P], esum[:, :, 0],
                                                   start=True, stop=True)
                        close_tile(ins, f"md{c}")

                    def ada_gate(c):
                        for i in range(2):
                            ps = open_tile(pe, f"gr{c}_{i}")
                            copied(pe, f"ada{c}")
                            ins = nc.tensor.matmul(ps[:, :], esum[:, i, :], adas(c), start=True, stop=True)
                            close_tile(ins, f"gr{c}_{i}")

                    def ada_small(c):
                        (ada_gate if c in GATE_CHUNKS else ada_mod)(c)

                    for c in range(4):
                        ada_main(c)
                        if c:
                            ada_mod(c - 1)
                    ada_mod(3)

                    pe.wait_ge(S["xn_ready"], TT)
                    for k in range(KT):
                        ps = open_tile(pe, f"xt{k}")
                        for t in range(TT):
                            ins = nc.tensor.transpose(ps[:, t * P:(t + 1) * P], XN[:, t, k * P:(k + 1) * P], ident)
                        close_tile(ins, f"xt{k}")

                    first_ht = [True]

                    def zt(tile, unit, lhs):
                        ps = open_tile(pe, tile)
                        for k in range(KT):
                            if first_ht[0]:
                                copied(pe, f"xt{k}")
                            ins = nc.tensor.matmul(ps[:, 0:TOK], lhs(k), HT[:, k, :], start=(k == 0), stop=(k == KT - 1))
                        first_ht[0] = False
                        close_tile(ins, tile)
                        return ins

                    def zrow(tile, t, rhs, n, at=0, last=True):
                        if at == 0:
                            open_tile(pe, tile)
                        ps = psum[:, T.at[tile][0], :]
                        for k in range(KT):
                            ins = nc.tensor.matmul(ps[:, at:at + n], HT[:, k, t * P:(t + 1) * P], rhs(k),
                                                   start=(k == 0), stop=(k == KT - 1))
                        if last:
                            close_tile(ins, tile)
                        return ins

                    landed("w0")
                    w = slot("w0", CH)
                    for n, c0 in (("gb0", 256), ("ga0", 0), ("gb1", 384), ("ga1", 128)):
                        zt(n, "w0", lambda k: w[:, k, c0:c0 + P])
                    landed("w1")
                    w = slot("w1", CH)
                    for t in range(TT):
                        zrow(f"zf{t}", t, lambda k: w[:, k, 0:256], 256)
                    for a in range(2):
                        zt(f"cq{a}", "w1", lambda k: w[:, k, 256 + a * P:384 + a * P])
                    ps = open_tile(pe, "ctxT")
                    pe.wait_ge(S["cache_in"], 64)
                    for c in range(3):
                        ins = nc.tensor.transpose(ps[:, c * P:(c + 1) * P],
                                                  KC[:, 2 * c:2 * c + 2, :].rearrange("p h d -> p (h d)"), ident)
                    close_tile(ins, "ctxT")
                    for t in range(TT):
                        copied(pe, f"zf{t}")
                    for c in range(2):
                        ps = open_tile(pe, f"fgs{c}")
                        for t in range(2):
                            ins = nc.tensor.matmul(ps[:, :], ZF[:, 1 + t, c * P:(c + 1) * P], dft_s[:, t, :],
                                                   start=(t == 0), stop=(t == 1))
                        close_tile(ins, f"fgs{c}")
                        ps = open_tile(pe, f"fgp{c}")
                        close_tile(nc.tensor.matmul(ps[:, 0:256], ZF[:, 0, c * P:(c + 1) * P], dft_p, start=True, stop=True),
                                   f"fgp{c}")
                    landed("w2")
                    w2 = slot("w2", CH)
                    zt("ck", "w2", lambda k: w2[:, k, 0:128])
                    for c in range(2):
                        ps = open_tile(pe, f"fo{c}")
                        copied(pe, f"fgs{c}")
                        copied(pe, f"fgp{c}")
                        for x in range(2):
                            ins = nc.tensor.matmul(ps[:, 0:TOK], dftc[:, x, :], FG[:, c, x * TOK:(x + 1) * TOK],
                                                   start=(x == 0), stop=(x == 1))
                        close_tile(ins, f"fo{c}")
                    for t in range(TT):
                        zrow("zcv", t, lambda k: w2[:, k, 128:256], P, t * P, t == TT - 1)
                    for a in range(2):
                        zt(f"dq{a}", "w2", lambda k: w2[:, k, 256 + a * P:384 + a * P])
                    landed("w3")
                    w3 = slot("w3", CH)
                    for a in range(2):
                        zt(f"dk{a}", "w3", lambda k: w3[:, k, a * P:(a + 1) * P])
                    for t in range(TT):
                        zrow(f"zdv{t}", t, lambda k: w3[:, k, 256:512], 256)
                    ps = open_tile(pe, "ko")
                    for n in ("cq0", "cq1", "ck", "dk0", "dk1"):
                        copied(pe, n)
                    for c, src in enumerate((KTC[:, 0:P], DK[:, 0, 0:P], DK[:, 1, 0:P])):
                        ins = nc.tensor.transpose(ps[:, c * P:(c + 1) * P], src, ident)
                    close_tile(ins, "ko")
                    for n, src in (("rot0", QC[:, 0, P:TOK]), ("rot1", QC[:, 1, P:TOK]), ("rotk", KTC[:, P:TOK])):
                        ps = open_tile(pe, n)
                        close_tile(nc.tensor.matmul(ps[:, 0:DEC], rot, src, start=True, stop=True), n)
                    pe.wait_ge(S["conv_step"], 2 * CONV_K)
                    for t in range(TT):
                        ps = open_tile(pe, f"lt{t}")
                        a0 = 0 if t == 0 else USAMP - PADC + (t - 1) * P
                        for c in range(2):
                            ins = nc.tensor.transpose(ps[:, c * P:(c + 1) * P], ACC[:, c, a0:a0 + P], ident)
                        close_tile(ins, f"lt{t}")
                    for t in range(TT):
                        copied(pe, f"lt{t}")
                    for c in range(2):
                        ps = open_tile(pe, f"lb{c}")
                        for t in range(TT):
                            ins = nc.tensor.transpose(ps[:, t * P:(t + 1) * P], LNX[:, t, c * P:(c + 1) * P], ident)
                        close_tile(ins, f"lb{c}")

                    def att_scores(g):
                        br, qt = ATT[g]
                        if g == 0:
                            pe.wait_ge(S["rope_ready"], 3)
                            for n in ("ctxT", "dq0", "dq1", "zcv", "zdv0", "zdv1", "zdv2"):
                                copied(pe, n)
                        q0 = 0 if qt is None else P + qt * P
                        for h in range(4):
                            b = 4 + h
                            pe.wait_ge(free[b], T.at[f"pt{g}_{h}"][2])
                            if br == "c":
                                r = slice(64 * (h // 2), 64 * (h // 2) + 64)
                                q, kk, ct = QC[r, h % 2, q0:q0 + P], KTC[r, :], CT[r, 0, :]
                            else:
                                r = slice(64 * (h % 2), 64 * (h % 2) + 64)
                                q, kk, ct = DQ[r, h // 2, q0:q0 + P], DK[r, h // 2, :], CT[r, 1 + h // 2, :]
                            if qt is None:
                                ins = nc.tensor.matmul(psum[:, b, 0:P], q, kk[:, 0:P], start=True, stop=True)
                            else:
                                nc.tensor.matmul(psum[:, b, 0:DEC], q, kk[:, P:TOK], start=True, stop=True)
                                ins = nc.tensor.matmul(psum[:, b, DEC:DEC + P], q, ct, start=True, stop=True)
                        ins.then_inc(S["scores_done"], 1)

                    def att_out(g):
                        br, qt = ATT[g]
                        nk = 1 if qt is None else 3
                        pe.wait_ge(S["scores_read"], g + 1)
                        pe.wait_ge(S["p_ready"], g + 1)

                        def probs_t(h):
                            name = f"pt{g}_{h}"
                            b = T.at[name][0]
                            for j in range(nk):
                                ins = nc.tensor.transpose(psum[:, b, j * P:(j + 1) * P], SCB[:, h, j * P:(j + 1) * P], ident)
                            close_tile(ins, name)

                        def pv(h):
                            copied(pe, f"pt{g}_{h}")
                            if br == "c":
                                kv = h // 2
                                vl, vc = slice(kv * HD, (kv + 1) * HD), kv
                            else:
                                vl, vc = slice(P + h * HD, P + (h + 1) * HD), 2 + h
                            vs = [ZV[:, 0, vl]] if qt is None else [ZV[:, 1, vl], ZV[:, 2, vl], VC[:, vc, :]]
                            for j in range(nk):
                                ins = nc.tensor.matmul(po[64 * (h % 2):64 * (h % 2) + 64, (h // 2) * P:(h // 2 + 1) * P],
                                                       vs[j], PTB[:, h % 2, j * P:(j + 1) * P],
                                                       start=(j == 0), stop=(j == nk - 1))
                            if h < 2:
                                ins.then_inc(S[f"pv{h}"], 1)
                            elif h == 3:
                                close_tile(ins, f"o{g}")

                        po = None
                        probs_t(0)
                        probs_t(1)
                        po = open_tile(pe, f"o{g}")
                        pv(0)
                        probs_t(2)
                        pv(1)
                        probs_t(3)
                        pv(2)
                        pv(3)

                    for n in GATE_ORDER:
                        wb = slot("wb01" if n < 2 else "wb23", D)
                        landed("wb01" if n < 2 else "wb23")
                        for k in range(KT):
                            idx = GATE_ORDER.index(n) * KT + k
                            if idx % 2 == 0:
                                g = idx // 2
                                if 1 <= g <= len(ATT):
                                    att_out(g - 1)
                                if g < len(ATT):
                                    att_scores(g)
                            unit = f"w{4 + 2 * n + k // 4}"
                            if k % 4 == 0:
                                landed(unit)
                            wg = slot(unit, CH)
                            zt(f"g{n}_{k}", unit, lambda kk: wg[:, kk, (k % 4) * P:(k % 4 + 1) * P])
                            ps = open_tile(pe, f"p{n}_{k}")
                            if k == 0:
                                for x in {1: ("fo0", "fo1"), 0: ("lb0", "lb1"), 2: ("o4", "o1"), 3: ("o5", "o3")}[n]:
                                    copied(pe, x)
                            for c in range(2):
                                ins = nc.tensor.matmul(ps[:, 0:TOK], wb[:, 2 * (n % 2) + c, k * P:(k + 1) * P], BRT[:, n, c, :],
                                                       start=(c == 0), stop=(c == 1))
                            close_tile(ins, f"p{n}_{k}")
                            if idx % 4 == 3:
                                ada_main(4 + idx // 4)
                            if idx % 4 == 0 and idx:
                                ada_small(3 + idx // 4)
                    ada_small(NADA - 1)

                    landed("wo0")
                    landed("wo1")
                    pe.wait_ge(S["gate_add"], 3 * KT)
                    for t in range(TT):
                        for half in range(2):
                            ps = open_tile(pe, f"wo{t}_{half}")
                            for k in range(KT):
                                wo = slot(f"wo{k // 4}", D)
                                ins = nc.tensor.matmul(ps[:, :], MRG[:, k, t * P:(t + 1) * P],
                                                       wo[:, k % 4, half * CH:(half + 1) * CH], start=(k == 0), stop=(k == KT - 1))
                            close_tile(ins, f"wo{t}_{half}")

                @block.scalar
                def _(act):
                    rms_part_act(act, S["sq_done"], S["ms_ready"], S["sd_ready"])

                    def copy_out(name, dst, src):
                        ps = take(act, name)
                        release(nc.scalar.activation(dst, src(ps), ACT.Copy), name)

                    for c in range(4):
                        copy_out(f"ada{c}", adas(c), lambda ps: ps)
                    act.wait_ge(S["sc_ready"], 1)
                    for k in range(0, KT, 2):
                        ps = take(act, f"xt{k}")
                        modulate_act(HT[:, k, 0:P], ps[:, 0:P], 0, 0, k, 0)
                        release(modulate_act(HT[:, k, P:TOK], ps[:, P:TOK], 0, 0, k, 1), f"xt{k}")
                    for c in range(2):
                        ps = take(act, f"gb{c}")
                        release(nc.scalar.activation(SIG[:, c, :], ps[:, 0:TOK], ACT.Sigmoid), f"gb{c}")
                    for t in range(TT):
                        copy_out(f"zf{t}", ZF[:, t, :], lambda ps: ps[:, 0:BW])
                    for a in range(2):
                        nc.scalar.activation(QC[64 * a:64 * a + 64, 0, :], take(act, f"cq{a}")[0:64, 0:TOK], ACT.Copy)
                        copy_out(f"cq{a}", QC[64 * a:64 * a + 64, 1, :], lambda ps: ps[64:128, 0:TOK])
                    copy_out("ctxT", CT, lambda ps: ps[:, 0:384].rearrange("p (c n) -> p c n", c=3))
                    for c in range(2):
                        fg = FG[:, c, :].rearrange("p (x n) -> p x n", x=2)
                        copy_out(f"fgs{c}", fg[:, :, P:TOK], lambda ps: ps.rearrange("p (x n) -> p x n", x=2))
                        copy_out(f"fgp{c}", fg[:, :, 0:P], lambda ps: ps[:, 0:256].rearrange("p (x n) -> p x n", x=2))
                    copy_out("ck", KTC, lambda ps: ps[:, 0:TOK])
                    for c in range(2):
                        copy_out(f"fo{c}", BRT[:, 1, c, :], lambda ps: ps[:, 0:TOK])
                    copy_out("zcv", ZV[:, :, 0:P], lambda ps: ps[:, 0:384].rearrange("p (t n) -> p t n", t=TT))
                    for n, dst in (("dq0", DQ[:, 0, :]), ("dq1", DQ[:, 1, :]), ("dk0", DK[:, 0, :]), ("dk1", DK[:, 1, :])):
                        copy_out(n, dst, lambda ps: ps[:, 0:TOK])
                    for t in range(TT):
                        copy_out(f"zdv{t}", ZV[:, t, P:384], lambda ps: ps[:, 0:256])
                    copy_out("ko", KO, lambda ps: ps[:, 0:384])
                    act.wait_ge(S["dve_step"], ln_var_step[0])
                    nc.scalar.activation(LSD, MV[:, :, 1], ACT.Sqrt).then_inc(S["exps_done"], 1)
                    for c in range(2):
                        ps = take(act, f"lb{c}")
                        release(nc.scalar.activation(BRT[:, 0, c, :], ps[:, 0:TOK], ACT.Silu, scale=PRM[:, 128 + c:129 + c],
                                                     bias=PRM[:, 130 + c:131 + c]), f"lb{c}")
                    for idx in range(4 * KT):
                        n, k = GATE_ORDER[idx // KT], idx % KT
                        g = idx // 2 if idx % 2 == 0 else None
                        if g is not None and 1 <= g <= len(ATT):
                            nk = 1 if ATT[g - 1][1] is None else 3
                            for h in (0, 2):
                                if h == 2:
                                    act.wait_ge(S["pv0"], g)
                                copy_out(f"pt{g-1}_{h}", PTB[:, 0, 0:nk * P], lambda ps: ps[:, 0:nk * P])
                        if idx == 0:
                            copied(act, "ga0")
                            copied(act, "ga1")
                        if idx >= 2:
                            m, kk = GATE_ORDER[(idx - 2) // KT], (idx - 2) % KT
                            copied(act, f"p{m}_{kk}")
                        ps = take(act, f"g{n}_{k}")
                        release(nc.scalar.activation(SIG[:, idx % 2, :], ps[:, 0:TOK], ACT.Sigmoid), f"g{n}_{k}")
                        if g is not None and g < len(ATT):
                            w = P if ATT[g][1] is None else TOK
                            act.wait_ge(S["nmax_ready"], g + 1)
                            if ATT[g][0] == "c":
                                nc.scalar.activation(ES, DS, ACT.Exp)
                            for h in range(4):
                                ins = nc.scalar.activation(SCB[:, h, 0:w], SCB[:, h, 0:w], ACT.Exp, bias=NM[:, h:h + 1],
                                                           accum_out=SM[:, h:h + 1])
                            ins.then_inc(S["exps_done"], 1)
                        if idx % 4 == 3:
                            copy_out(f"ada{4 + idx // 4}", adas(4 + idx // 4), lambda ps: ps)

                @block.vector
                def _(dve):
                    steps = [0]

                    def step(ins):
                        steps[0] += 1
                        ins.then_inc(S["dve_step"], 1)

                    def settle():
                        dve.wait_ge(S["dve_step"], steps[0])

                    rms_part_dve(dve, S["sq_done"], S["ms_ready"], S["sd_ready"], S["rs_ready"], S["xn_ready"])
                    ps = take(dve, "prm")
                    release(nc.vector.tensor_copy(PRM[:, :], ps[:, 0:132]), "prm")

                    def shift_scale(c):
                        ps = take(dve, f"md{c}")
                        release(nc.vector.tensor_tensor(MOD[:, 4 * c:4 * c + 4, :], ps[:, 0:8].rearrange("p (n i) -> p n i", i=2),
                                                        PRM[:, 4 * c:4 * c + 4].unsqueeze(2).broadcast_to((P, 4, 2)), ALU.add), f"md{c}")

                    def gain(which, scale_sec, col):
                        nc.vector.scalar_tensor_tensor(
                            SC[:, which, :, :], MOD[:, scale_sec * KT:(scale_sec + 1) * KT, :], 1.0,
                            PRM[:, col:col + KT].unsqueeze(2).broadcast_to((P, KT, 2)), ALU.add, ALU.mult).then_inc(S["sc_ready"], 1)

                    copied(dve, "prm")
                    for c in range(4):
                        shift_scale(c)
                    for c in (2, 3):
                        copied(dve, f"md{c}")
                    gain(0, 1, 48)
                    dve.wait_ge(S["sc_ready"], 1)
                    for k in range(1, KT, 2):
                        ps = take(dve, f"xt{k}")
                        modulate_dve(HT[:, k, 0:P], ps[:, 0:P], 0, 0, k, 0)
                        release(modulate_dve(HT[:, k, P:TOK], ps[:, P:TOK], 0, 0, k, 1), f"xt{k}")
                    dve.wait_ge(S["u_zero"], 1)
                    for c in range(2):
                        ps = take(dve, f"ga{c}")
                        copied(dve, f"gb{c}")
                        step(nc.vector.tensor_tensor(U[:, c, PADC:PADC + SEQ], ps[:, 0:P], SIG[:, c, 0:P], ALU.mult))
                        release(nc.vector.tensor_tensor(U[:, c, USAMP:USAMP + DEC], ps[:, P:TOK], SIG[:, c, P:TOK], ALU.mult),
                                f"ga{c}")
                    settle()
                    copied(dve, "ga0")
                    copied(dve, "ga1")
                    for k in range(CONV_K):
                        for c in range(2):
                            w = PRM[:, 64 + 2 * k + c:65 + 2 * k + c]
                            if k == 0:
                                ins = nc.vector.tensor_scalar(ACC[:, c, :], U[:, c, 0:AW], w, PRM[:, 126 + c:127 + c],
                                                              ALU.mult, ALU.add)
                            else:
                                dve.wait_ge(S["conv_step"], 2 * (k - 1) + c + 1)
                                ins = nc.vector.scalar_tensor_tensor(ACC[:, c, :], U[:, c, k:k + AW], w, ACC[:, c, :],
                                                                     ALU.mult, ALU.add)
                            ins.then_inc(S["conv_step"], 1)
                    for i, (n, x) in enumerate((("rot0", QC[:, 0, P:TOK]), ("rot1", QC[:, 1, P:TOK]), ("rotk", KTC[:, P:TOK]))):
                        ps = take(dve, n)
                        step(nc.vector.tensor_tensor(x, x, cosT, ALU.mult))
                        release(nc.vector.tensor_tensor(ROTT, ps[:, 0:DEC], sinT, ALU.mult), n)
                        settle()
                        copied(dve, n)
                        nc.vector.tensor_tensor(x, x, ROTT, ALU.add).then_inc(S["rope_ready"], 1)
                        dve.wait_ge(S["rope_ready"], i + 1)
                    dve.wait_ge(S["grow_in"], 64)

                    def gate_rows(c):
                        gate, half = (0, c - 4) if c < 6 else (1, c - 10)
                        for i in range(2):
                            ps = take(dve, f"gr{c}_{i}")
                            dst = GROW[:, gate, i, half * CH:(half + 1) * CH]
                            release(nc.vector.tensor_tensor(dst, dst, ps, ALU.add), f"gr{c}_{i}")

                    def ada_end(c):
                        if c in GATE_CHUNKS:
                            gate_rows(c)
                        else:
                            shift_scale(c)
                        if c == 9:
                            copied(dve, "md8")
                            copied(dve, "md9")
                            gain(1, 4, 56)

                    for t in range(TT):
                        ps = take(dve, f"lt{t}")
                        step(nc.vector.bn_stats(BN[:, t, :], ps[:, 0:BW]))
                    settle()
                    for t in range(TT):
                        step(nc.vector.bn_aggr(MV[:, t, :], BN[:, t, :]))
                    settle()
                    step(nc.vector.tensor_scalar(MV[:, :, 1], MV[:, :, 1], EPS, None, ALU.add))
                    assert steps[0] == ln_var_step[0], steps[0]
                    dve.wait_ge(S["exps_done"], 1)
                    step(nc.vector.reciprocal(LRS, LSD))
                    settle()
                    for t in range(TT):
                        release(nc.vector.tensor_scalar(LNX[:, t, :], psum[:, T.at[f"lt{t}"][0], 0:BW], MV[:, t, 0:1],
                                                        LRS[:, t:t + 1], ALU.subtract, ALU.mult), f"lt{t}")
                    dve.wait_ge(S["sink_in"], 16)
                    dve.wait_ge(S["nab_ready"], 1)
                    adds = [0]

                    def gate_mul(idx):
                        n, k = GATE_ORDER[idx // KT], idx % KT
                        copied(dve, f"g{n}_{k}")
                        ps = take(dve, f"p{n}_{k}")
                        if idx < KT:
                            release(nc.vector.tensor_tensor(MRG[:, k, :], SIG[:, idx % 2, :], ps[:, 0:TOK], ALU.mult), f"p{n}_{k}")
                        else:
                            if adds[0]:
                                dve.wait_ge(S["gate_add"], adds[0])
                            release(nc.vector.tensor_tensor(GP[:, idx % 2, :], SIG[:, idx % 2, :], ps[:, 0:TOK], ALU.mult),
                                    f"p{n}_{k}")
                            copied(dve, f"p{n}_{k}")
                            nc.vector.tensor_tensor(MRG[:, k, :], MRG[:, k, :], GP[:, idx % 2, :], ALU.add).then_inc(S["gate_add"], 1)
                            adds[0] += 1

                    for idx in range(4 * KT):
                        g = idx // 2 if idx % 2 == 0 else None
                        if g is not None and 1 <= g <= len(ATT):
                            br, qt = ATT[g - 1]
                            nk = 1 if qt is None else 3
                            for h in (1, 3):
                                ps = take(dve, f"pt{g-1}_{h}")
                                if h == 3:
                                    dve.wait_ge(S["pv1"], g)
                                release(nc.vector.tensor_copy(PTB[:, 1, 0:nk * P], ps[:, 0:nk * P]), f"pt{g-1}_{h}")
                            ps = take(dve, f"o{g-1}")
                            t0 = 0 if qt is None else P + qt * P
                            release(nc.vector.tensor_copy(BRT[:, 2 if br == "c" else 3, :, t0:t0 + P],
                                                          ps[:, 0:2 * P].rearrange("p (c n) -> p c n", c=2)), f"o{g-1}")
                        if g is not None and g < len(ATT):
                            br, qt = ATT[g]
                            w = P if qt is None else TOK
                            dve.wait_ge(S["scores_done"], g + 1)
                            if qt is None:
                                nc.vector.tensor_scalar(SCB[:, :, 0:P], psum[:, 4:8, 0:P], SCALE, None, ALU.mult).then_inc(
                                    S["scores_read"], 1)
                            else:
                                bias = NAB[:, qt, :, :] if br == "d" else winmask[:, qt, :].unsqueeze(1).broadcast_to((P, 4, DEC))
                                step(nc.vector.scalar_tensor_tensor(SCB[:, :, 0:DEC], psum[:, 4:8, 0:DEC], SCALE, bias, ALU.mult,
                                                                    ALU.add))
                                nc.vector.tensor_scalar(SCB[:, :, DEC:TOK], psum[:, 4:8, DEC:TOK], SCALE, None, ALU.mult).then_inc(
                                    S["scores_read"], 1)
                                settle()
                            dve.wait_ge(S["scores_read"], g + 1)
                            step(nc.vector.tensor_reduce(MX, SCB[:, :, 0:w], AX_X, ALU.max))
                            settle()
                            if br == "c":
                                step(nc.vector.tensor_tensor(MX, MX, SINK, ALU.max))
                                settle()
                                step(nc.vector.tensor_tensor(DS, SINK, MX, ALU.subtract))
                            nc.vector.tensor_scalar(NM, MX, -1.0, None, ALU.mult).then_inc(S["nmax_ready"], 1)
                        gate_mul(idx)
                        if g is not None and g < len(ATT):
                            dve.wait_ge(S["exps_done"], g + 2)
                            if br == "c":
                                step(nc.vector.tensor_tensor(SM, SM, ES, ALU.add))
                                settle()
                            step(nc.vector.reciprocal(RI, SM))
                            settle()
                            nc.vector.tensor_tensor(SCB[:, :, 0:w], SCB[:, :, 0:w], RI.unsqueeze(2).broadcast_to((P, 4, w)),
                                                    ALU.mult).then_inc(S["p_ready"], 1)
                        if idx % 4 == 0 and idx:
                            ada_end(3 + idx // 4)
                    ada_end(NADA - 1)
                    dve.wait_ge(S["gate_add"], 3 * KT)
                    for i, (t, half) in enumerate((t, h) for t in range(TT) for h in range(2)):
                        ps = take(dve, f"wo{t}_{half}")
                        if i == 0:
                            for c in (4, 5):
                                for gi in range(2):
                                    copied(dve, f"gr{c}_{gi}")
                        cols = slice(half * CH, (half + 1) * CH)
                        if i:
                            settle()
                        release(nc.vector.tensor_tensor(WOT[:, i % 2, :], ps, GROW[:, 0, min(t, 1), cols], ALU.mult), f"wo{t}_{half}")
                        copied(dve, f"wo{t}_{half}")
                        step(nc.vector.tensor_tensor(X[:, t, cols], X[:, t, cols], WOT[:, i % 2, :], ALU.add))
                    settle()

            with nc.Block() as block:
                @block.sync
                def _(sp):
                    def load(g, j, e):
                        done = 4 * g + j + 1
                        for name, half, s in E_SRC:
                            if s == 0:
                                sp.wait_ge(S["e_half"], done)
                            elif s == 1:
                                e_take(sp, g, f"gu{j}_1")
                            elif s == 4:
                                sp.wait_ge(S["e_down_half"], done)
                            elif s == 5:
                                e_take(sp, g, f"y{j}")
                            sp.dma_start(e_dst(s), e_unit(l, e, name, half)).then_inc(e_land[s], 16)

                    with sp.Fori(0, NE // GRP - 1) as g:
                        for j in range(GRP):
                            load(g, j, g * GRP + (j + 1))
                    last = NE // GRP - 1
                    for j in range(GRP - 1):
                        load(last, j, last * GRP + j + 1)

                @block.tensor
                def _(pe):
                    for b in range(8):
                        pe.sem_inc(e_free[b], 1)
                    pe.wait_ge(S["n2_xn"], TT)
                    for k in range(KT):
                        ps = open_tile(pe, f"yt{k}")
                        for t in range(TT):
                            ins = nc.tensor.transpose(ps[:, t * P:(t + 1) * P], XN[:, t, k * P:(k + 1) * P], ident)
                        close_tile(ins, f"yt{k}")
                    ps = open_tile(pe, "rt")
                    pe.wait_ge(S["wr_in"], 16)
                    for k in range(KT):
                        copied(pe, f"yt{k}")
                    for t in range(TT):
                        for k in range(KT):
                            ins = nc.tensor.matmul(ps[:, t * NE:(t + 1) * NE], HT[:, k, t * P:(t + 1) * P], WR[:, k, :],
                                                   start=(k == 0), stop=(k == KT - 1))
                    close_tile(ins, "rt")
                    ps = open_tile(pe, "aft")
                    pe.wait_ge(S["aff_ready"], 1)
                    for t in range(TT):
                        ins = nc.tensor.transpose(ps[0:NE, t * P:(t + 1) * P], AFF[:, t, :], ident)
                    close_tile(ins, "aft")
                    ps = open_tile(pe, "post")
                    pe.wait_ge(S["cum_ready"], 1)
                    for t in range(TT):
                        ins = nc.tensor.transpose(ps[:, t * NE:(t + 1) * NE], CUM[0:NE, t * P:(t + 1) * P], ident[0:NE, 0:NE])
                    close_tile(ins, "post")

                    with pe.Fori(0, NE // GRP) as g:
                        pe.wait_ge(S["sel_ready"], g + 1)
                        for k in range(KT):
                            ps = e_open(pe, g, f"xe{k}")
                            for t in (1, 2, 0):
                                c0 = 0 if t else P
                                ins = nc.tensor.matmul(ps[:, c0:c0 + P], XN[:, t, k * P:(k + 1) * P],
                                                       SEL[:, t].rearrange("p e s -> p (e s)"), start=(t != 2), stop=(t != 1))
                            e_close(ins, f"xe{k}")
                        ps = e_open(pe, g, "pg")
                        pe.wait_ge(S["selg_ready"], g + 1)
                        for t in range(TT):
                            ins = nc.tensor.transpose(ps[:, t * P:(t + 1) * P], SELG[:, t].rearrange("p e s -> p (e s)"), ident)
                        e_close(ins, "pg")

                        def gate_up(j):
                            pb = [e_open(pe, g, f"gu{j}_{half}") for half in range(2)]
                            n_landed = 16 * (j + 1)
                            for k in range(KT):
                                if k % 4 == 0:
                                    pe.wait_ge(e_land[k // 4], g * 64 + n_landed)
                                    pe.wait_ge(e_land[2 + k // 4], g * 64 + n_landed)
                                if j == 0:
                                    e_copied(pe, g, f"xe{k}")
                                for half in range(2):
                                    for m in range(2):
                                        w = e_dst(2 * m + k // 4)
                                        ins = nc.tensor.matmul(pb[half][64 * m:64 * m + 64, :], XE[:, k, j, :],
                                                               w[:, k % 4, half * CH:(half + 1) * CH], start=(k == 0), stop=(k == KT - 1))
                                    if k == KT - 1:
                                        e_close(ins, f"gu{j}_{half}")
                                if k == 3:
                                    ins.then_inc(S["e_half"], 1)

                        def down(j):
                            ps = e_open(pe, g, f"at{j}")
                            for k in range(KT):
                                if k % 4 == 0:
                                    e_copied(pe, g, f"gu{j}_{k // 4}")
                                    ins = nc.tensor.matmul(ps[:, k * 64:(k + 1) * 64], AA[0:64, k * P:(k + 1) * P],
                                                           ident[0:64, 0:64], start=True, stop=True)
                                else:
                                    ins = nc.tensor.transpose(ps[:, k * 64:(k + 1) * 64], AA[0:64, k * P:(k + 1) * P],
                                                              ident[0:64, 0:64])
                            e_close(ins, f"at{j}")
                            ps = e_open(pe, g, f"y{j}")
                            e_copied(pe, g, f"at{j}")
                            for k in range(KT):
                                if k % 4 == 0:
                                    pe.wait_ge(e_land[4 + k // 4], g * 64 + 16 * (j + 1))
                                for half in range(2):
                                    ins = nc.tensor.matmul(ps[64 * half:64 * half + 64, :], AT[:, k, :],
                                                           e_dst(4 + k // 4)[:, k % 4, half * CH:(half + 1) * CH],
                                                           start=(k == 0), stop=(k == KT - 1))
                                if k == 3:
                                    ins.then_inc(S["e_down_half"], 1)
                            e_close(ins, f"y{j}")

                        for j in range(GRP):
                            gate_up(j)
                            down(j)
                        e_copied(pe, g, "pg")
                        e_copied(pe, g, f"y{GRP-2}")
                        e_copied(pe, g, f"y{GRP-1}")
                        for i, (t, half) in enumerate((t, h) for t in range(TT) for h in range(2)):
                            ps = e_open(pe, g, f"cm{i}")
                            e_close(nc.tensor.matmul(ps, PG[:, t, :], (YS if t else YP)[:, half * CH:(half + 1) * CH],
                                                     start=True, stop=True), f"cm{i}")

                @block.scalar
                def _(act):
                    rms_part_act(act, S["n2_sq"], S["n2_ms"], S["n2_sd"])
                    for k in range(0, KT, 2):
                        ps = take(act, f"yt{k}")
                        modulate_act(HT[:, k, 0:P], ps[:, 0:P], 1, 3, k, 0)
                        release(modulate_act(HT[:, k, P:TOK], ps[:, P:TOK], 1, 3, k, 1), f"yt{k}")
                    ps = take(act, "rt")
                    act.wait_ge(S["router_max"], 1)
                    for t in range(TT):
                        ins = nc.scalar.activation(AFF[:, t, :], ps[:, t * NE:(t + 1) * NE], ACT.Exp, bias=RMX[:, t:t + 1],
                                                   accum_out=RSM[:, t:t + 1])
                    release(ins, "rt")
                    act.wait_ge(S["aff_ready"], 1)
                    nc.scalar.activation(AFFG.rearrange("p g (t e) -> p g t e", t=TT),
                                         AFF.rearrange("p t (g e) -> p g t e", g=NE // GRP), ACT.Copy).then_inc(S["affg_ready"], 1)
                    with act.Fori(0, NE // GRP) as g:
                        for k in range(0, KT, 2):
                            ps = e_take(act, g, f"xe{k}")[:, 0:2 * P].rearrange("p (x e s) -> p x e s", x=2, e=GRP)
                            modulate_act(XE[:, k, :, 0:SLOTS], ps[:, 0], 1, 3, k, 1)
                            e_release(modulate_act(XE[:, k, :, SLOTS:2 * SLOTS], ps[:, 1], 1, 3, k, 0), f"xe{k}")
                        ps = e_take(act, g, "pg")
                        e_release(nc.scalar.activation(PG, ps[:, 0:384].rearrange("p (t n) -> p t n", t=TT), ACT.Copy), "pg")

                        def at_copy(j):
                            ps = e_take(act, g, f"at{j}")
                            e_release(nc.scalar.activation(AT.rearrange("p k s -> p (k s)"), ps, ACT.Copy), f"at{j}")

                        def y_copy(j):
                            ps = e_take(act, g, f"y{j}")
                            rows = slice(32 * j, 32 * j + 32)
                            nc.scalar.activation(YS[rows, CH:D], ps[64:96, :], ACT.Copy)
                            e_release(nc.scalar.activation(YP[rows, CH:D], ps[96:128, :], ACT.Copy), f"y{j}")

                        for j in range(GRP):
                            for half in range(2):
                                ps = e_take(act, g, f"gu{j}_{half}")
                                if j:
                                    e_copied(act, g, f"gu{j-1}_{half}")
                                nc.scalar.activation(TMP[64:128, half * CH:(half + 1) * CH], ps[0:64, :], ACT.Silu).then_inc(
                                    S["silu_done"], 1)
                            at_copy(j)
                            y_copy(j)

                @block.vector
                def _(dve):
                    rms_part_dve(dve, S["n2_sq"], S["n2_ms"], S["n2_sd"], S["n2_rs"], S["n2_xn"])
                    steps = [0]

                    def step(ins):
                        steps[0] += 1
                        ins.then_inc(S["route_step"], 1)

                    def settle():
                        dve.wait_ge(S["route_step"], steps[0])

                    step(nc.vector.memset(ONE[0:NE, :], 1.0))
                    for k in range(1, KT, 2):
                        ps = take(dve, f"yt{k}")
                        modulate_dve(HT[:, k, 0:P], ps[:, 0:P], 1, 3, k, 0)
                        release(modulate_dve(HT[:, k, P:TOK], ps[:, P:TOK], 1, 3, k, 1), f"yt{k}")
                    ps = take(dve, "rt")
                    step(nc.vector.tensor_reduce(RRI[:, 0:TT], ps[:, 0:TT * NE].rearrange("p (t e) -> p t e", t=TT), AX_X, ALU.max))
                    settle()
                    nc.vector.tensor_scalar(RMX[:, 0:TT], RRI[:, 0:TT], -1.0, None, ALU.mult).then_inc(S["router_max"], 1)
                    dve.wait_ge(S["router_max"], 1)
                    copied(dve, "rt")
                    step(nc.vector.reciprocal(RRI[:, 0:TT], RSM[:, 0:TT]))
                    settle()
                    nc.vector.tensor_tensor(AFF, AFF, RRI[:, 0:TT].unsqueeze(2).broadcast_to((P, TT, NE)), ALU.mult).then_inc(
                        S["aff_ready"], 1)
                    ps = take(dve, "aft")
                    step(nc.vector.tensor_copy(WK[0:NE, :], ps[0:NE, 0:TOK]))
                    settle()
                    for lo, hi, cap in ((0, SEQ, CAP_P), (SEQ, TOK, CAP_S)):
                        for r in range(cap // 8):
                            step(nc.vector.max(M8[0:NE, :], WK[0:NE, lo:hi]))
                            settle()
                            step(nc.vector.match_replace(WK[0:NE, lo:hi], M8[0:NE, :], WK[0:NE, lo:hi], -1.0))
                            settle()
                    release(nc.vector.tensor_scalar(MSK[0:NE, :], WK[0:NE, :], 0.0, None, ALU.is_lt), "aft")
                    copied(dve, "aft")
                    for lo, hi in ((0, SEQ), (SEQ, TOK)):
                        step(nc.vector.tensor_tensor_scan(CUM[0:NE, lo:hi], ONE[0:NE, lo:hi], MSK[0:NE, lo:hi], 0.0, ALU.mult, ALU.add))
                    settle()
                    nc.vector.tensor_tensor(CUM[0:NE, :], CUM[0:NE, :], MSK[0:NE, :], ALU.mult).then_inc(S["cum_ready"], 1)
                    ps = take(dve, "post")
                    release(nc.vector.tensor_scalar(POSG.rearrange("p g (t e) -> p g t e", t=TT),
                                                    ps[:, 0:TT * NE].rearrange("p (t g e) -> p g t e", t=TT, g=NE // GRP),
                                                    -1.0, None, ALU.add), "post")
                    copied(dve, "post")
                    dve.wait_ge(S["affg_ready"], 1)
                    with dve.Fori(0, NE // GRP) as g:
                        sel = SEL.rearrange("p t e s -> p (t e) s")
                        n = TT * GRP
                        nc.vector.tensor_tensor(sel, iota.unsqueeze(1).broadcast_to((P, n, SLOTS)),
                                                POSG[:, bass.ds(g, 1), :].rearrange("p o n -> p (o n)").unsqueeze(2).broadcast_to((P, n, SLOTS)),
                                                ALU.is_equal).then_inc(S["sel_ready"], 1)
                        dve.wait_ge(S["sel_ready"], g + 1)
                        nc.vector.tensor_tensor(SELG.rearrange("p t e s -> p (t e) s"), sel,
                                                AFFG[:, bass.ds(g, 1), :].rearrange("p o n -> p (o n)").unsqueeze(2).broadcast_to((P, n, SLOTS)),
                                                ALU.mult).then_inc(S["selg_ready"], 1)
                        for k in range(1, KT, 2):
                            ps = e_take(dve, g, f"xe{k}")[:, 0:2 * P].rearrange("p (x e s) -> p x e s", x=2, e=GRP)
                            modulate_dve(XE[:, k, :, 0:SLOTS], ps[:, 0], 1, 3, k, 1)
                            e_release(modulate_dve(XE[:, k, :, SLOTS:2 * SLOTS], ps[:, 1], 1, 3, k, 0), f"xe{k}")

                        def y_copy(j):
                            ps = e_take(dve, g, f"y{j}")
                            rows = slice(32 * j, 32 * j + 32)
                            nc.vector.tensor_copy(YS[rows, 0:CH], ps[0:32, :])
                            e_release(nc.vector.tensor_copy(YP[rows, 0:CH], ps[32:64, :]), f"y{j}")

                        for j in range(GRP):
                            for half in range(2):
                                ps = e_take(dve, g, f"gu{j}_{half}")
                                dve.wait_ge(S["silu_done"], g * 8 + 2 * j + half + 1)
                                if j and half == 0:
                                    e_take(dve, g, f"at{j-1}")
                                cols = slice(half * CH, (half + 1) * CH)
                                e_release(nc.vector.tensor_tensor(AA[0:64, cols], TMP[64:128, cols], ps[64:128, :], ALU.mult),
                                          f"gu{j}_{half}")
                            y_copy(j)
                        for i, (t, half) in enumerate((t, h) for t in range(TT) for h in range(2)):
                            ps = e_take(dve, g, f"cm{i}")
                            cols = slice(half * CH, (half + 1) * CH)
                            e_release(nc.vector.tensor_tensor(CMB[:, i % 2, :], ps, GROW[:, 1, min(t, 1), cols], ALU.mult), f"cm{i}")
                            e_copied(dve, g, f"cm{i}")
                            nc.vector.tensor_tensor(X[:, t, cols], X[:, t, cols], CMB[:, i % 2, :], ALU.add).then_inc(S["x_done"], 1)
                            dve.wait_ge(S["x_done"], g * 6 + (i + 1))

            nums = [s.num for s in sems]
            assert max(nums) - min(nums) == len(nums) - 1
            nc.all_engine_barrier(sems_to_clear=range(min(nums), max(nums) + 1))

        with nc.Block() as block:
            @block.sync
            def _(sp):
                sp.dma_start(GROW[:, 0, 0, :], A["final_norm_g"].rearrange("(o d) -> o d", o=1).broadcast_to((P, D))).then_inc(
                    once["fin_g_in"], 16)
                sp.wait_ge(once["fin_y"], 1)
                sp.dma_start(A["y_prompt"].rearrange("b s d -> (b s) d"), XN[:, 0, :]).then_inc(once["fin_out"], 16)
                sp.wait_ge(once["fin_y"], TT)
                sp.dma_start(A["y_sample"].rearrange("b (t p) d -> p (b t) d", p=P), XN[:, 1:3, :]).then_inc(once["fin_out"], 16)
                sp.wait_ge(once["fin_out"], 32)

            @block.scalar
            def _(act):
                rms_part_act(act, once["fin_sq"], once["fin_ms"], once["fin_sd"])

            @block.vector
            def _(dve):
                rms_part_dve(dve, once["fin_sq"], once["fin_ms"], once["fin_sd"], once["fin_rs"], once["fin_n"])
                dve.wait_ge(once["fin_g_in"], 16)
                for t in range(TT):
                    dve.wait_ge(once["fin_n"], t + 1)
                    nc.vector.tensor_tensor(XN[:, t, :], XN[:, t, :], GROW[:, 0, 0, :], ALU.mult).then_inc(once["fin_y"], 1)


INS = ["x_prompt", "x_sample", "cache_win_k", "cache_win_v", "cache_nat_k", "cache_nat_v", "c", "c_ctx", "norm1_g", "norm2_g",
       "w_ada", "b_ada", "w_in", "conv_w", "conv_b", "conv_ln_g", "conv_ln_b", "win_sink", "w_branch", "w_out", "w_router",
       "w_e_gate", "w_e_up", "w_e_down", "final_norm_g"]
OUTS = [("y_prompt", (1, SEQ, D)), ("y_sample", (1, DEC, D)), ("new_win_k", (1, DEPTH, 2, SEQ, HD)),
        ("new_win_v", (1, DEPTH, 2, SEQ, HD)), ("new_nat_k", (1, DEPTH, 4, SEQ, HD)), ("new_nat_v", (1, DEPTH, 4, SEQ, HD))]


def bias_grid(na_bias):
    t = np.arange(DEC)
    row, col = t // 64, t % 64
    dr = row[None, :] - row[:, None] + 7
    dc = np.clip(col[None, :] - col[:, None] + 15, 0, 30)
    g = na_bias[:, :, dr, dc]
    return np.ascontiguousarray(g.reshape(DEPTH, 4, 2, P, DEC).transpose(0, 2, 3, 1, 4).reshape(DEPTH, 2, P, 4 * DEC))


def kernel(**inputs):
    import numpy as _np
    import concourse.bacc as _bacc
    from concourse import mybir as _mybir
    from concourse.bass_utils import run_bass_kernel_spmd as _run

    nc = _bacc.Bacc("TRN2", target_bir_lowering=False, num_devices=1)
    arrays, A = {}, {}
    data = {n: _np.asarray(inputs[n]) for n in INS}
    data["na_grid"] = bias_grid(_np.asarray(inputs["na_bias"]))
    data["const"] = constants()
    for name, a in data.items():
        a = _np.ascontiguousarray(a)
        arrays[f"in_{name}"] = a
        A[name] = nc.dram_tensor(f"in_{name}", a.shape, _mybir.dt.from_np(a.dtype), kind="ExternalInput").ap()
    for name, shape in OUTS:
        A[name] = nc.dram_tensor(f"out_{name}", shape, F32, kind="ExternalOutput").ap()
    build(nc, A)
    r = _run(nc, [arrays], core_ids=[0])
    return tuple(r.results[0][f"out_{name}"] for name, _ in OUTS)
```

```python
from contextlib import ExitStack

import numpy as np

import concourse.bass as bass
from concourse import mybir

F32 = mybir.dt.float32
F32R = mybir.dt.float32r
ALU = mybir.AluOpType
ACT = mybir.ActivationFunctionType
AX_X = mybir.AxisListType.X

P = 128
D = 1024
KT = D // P
SEQ, DEC = 128, 256
TOK = SEQ + DEC
TT = TOK // P
DEPTH = 2
BW = 256
HD = 64
CONV_K = 31
NE, FF = 16, 1024
CAP_P, CAP_S = 2 * SEQ // NE, 2 * DEC // NE
SLOTS = 32
GRP = 4
EPS = 1e-6
NEG = -1e30
SCALE = HD ** -0.5
CH = 512
NADA = 6 * D // CH
PADC = CONV_K // 2
UW = PADC + SEQ + 2 * PADC + DEC + PADC
AW = UW - CONV_K + 1
USAMP = PADC + SEQ + 2 * PADC
NSLOT = 6
ARENA = 15600

CONST_COLS = dict(ident=128, cos=256, sin=256, rot=128, winmask=512, iota=32, esum=256,
                  namask=512, dft_s=1024, dft_p=256, dftc=256)
HELD = 1568


def const_at(name):
    at = 0
    for n, w in CONST_COLS.items():
        if n == name:
            return at, at + w
        at += w


def constants():
    c = np.zeros((P, sum(CONST_COLS.values())), np.float32)

    def put(name, a):
        lo, hi = const_at(name)
        c[:, lo:hi] = np.asarray(a, np.float64).reshape(P, hi - lo)

    put("ident", np.eye(P))

    def dft(n):
        k = np.outer(np.arange(n), np.arange(n)) % n
        return np.cos(2 * np.pi * k / n), np.sin(2 * np.pi * k / n)

    cs, ss = dft(DEC)
    both = np.concatenate([cs, ss], 1) / np.sqrt(DEC)
    put("dft_s", both.reshape(2, P, 2 * DEC).transpose(1, 0, 2))
    cp, sp = dft(SEQ)
    put("dft_p", np.concatenate([cp, sp], 1) / np.sqrt(SEQ))
    cc, sc = dft(HD)
    eye2 = np.eye(2)
    put("dftc", np.concatenate([np.kron(eye2, cc), -np.kron(eye2, sc)], 1) / np.sqrt(HD))
    t = np.arange(DEC)
    row, col = t // 64, t % 64
    d = np.arange(P) % HD
    freqs = (1.0 / (np.float32(10000.0) ** (np.arange(16, dtype=np.float32) / np.float32(16)))).astype(np.float32)
    pos = np.where((d // 32 == 0)[:, None], row[None], col[None]).astype(np.float32)
    ang = pos * freqs[d % 16][:, None]
    put("cos", np.cos(ang))
    put("sin", np.sin(ang))
    r = np.zeros((P, P))
    for m in range(P):
        if m % 32 < 16:
            r[m + 16, m] = -1.0
        else:
            r[m - 16, m] = 1.0
    put("rot", r)
    q, k = np.arange(DEC)[:, None], np.arange(DEC)[None]
    win = np.where(np.abs(k - q) <= 128, 0.0, NEG)
    put("winmask", win.reshape(2, P, DEC).transpose(1, 0, 2))
    start = np.clip(q % 64 - 8, 0, 48)
    na = np.where((k % 64 >= start) & (k % 64 < start + 16), 0.0, NEG)
    put("namask", na.reshape(2, P, DEC).transpose(1, 0, 2))
    put("iota", np.tile(np.arange(SLOTS), (P, 1)))
    e = np.zeros((P, 2, P))
    for i in range(2):
        e[i::32, i, :] = 1.0
    put("esum", e)
    return c


class BankTurns:

    def __init__(self):
        self.at, self.turns, self.copies = {}, [0] * 8, [0] * 8

    def add(self, name, bank, copies=1):
        self.at[name] = (bank, self.turns[bank], self.copies[bank], copies)
        self.turns[bank] += 1
        self.copies[bank] += copies


def build(nc, A):
    ctx = ExitStack()
    with ctx:
        def sb(name, shape):
            return ctx.enter_context(nc.sbuf_tensor(name, shape, F32))

        sems = []

        def sem(name):
            s = ctx.enter_context(nc.semaphore(name))
            sems.append(s)
            return s

        once = {n: ctx.enter_context(nc.semaphore(n)) for n in
                ("x_in", "const_in", "ada_in0", "ada_in1", "ada_in2", "ada_in3", "cond_in", "cond_t", "cond_zero", "cond_ready",
                 "fin_g_in", "fin_sq", "fin_ms", "fin_sd", "fin_rs", "fin_n", "fin_y", "fin_out")}

        starts = {}

        def slab(name, shape):
            t = sb(name, shape)
            starts[name] = nc.sbuf_base - 4 * int(np.prod(shape[1:]))
            return t

        def over(name, host, word, words):
            return nc.alloc_sbuf_tensor_at(name, [P, words], F32R, offset=starts[host] + 4 * word)

        ring = slab("ring", [P, NSLOT, KT // 2 * D])
        X = sb("X", [P, TT, D])
        XN = sb("XN", [P, TT, D])
        C = sb("C", [P, HELD])
        assert const_at("esum")[1] == HELD
        GROW = sb("GROW", [P, 2, 2, D])
        condT = sb("condT", [P, KT, 32])
        MOD = sb("MOD", [P, 48, 2])
        SC = sb("SC", [P, 2, KT, 2])
        PRM = sb("PRM", [P, 132])
        SS = sb("SS", [P, 4])
        MS = sb("MS", [P, 4])
        SD = sb("SD", [P, 4])
        RS = sb("RS", [P, 4])
        WR = sb("WR", [P, KT, NE])
        arena = slab("arena", [P, ARENA])
        psum = ctx.enter_context(nc.psum_tensor("psum", [P, 8, 512], F32))

        def cst(name, **kw):
            lo, hi = const_at(name)
            return C[:, lo:hi]

        ident = cst("ident")
        cosT, sinT, rot = cst("cos"), cst("sin"), cst("rot")
        winmask = cst("winmask").rearrange("p (q n) -> p q n", q=2)
        iota = cst("iota")
        esum = cst("esum").rearrange("p (i n) -> p i n", i=2)

        cursor = [0]

        def part(n, base=None):
            lo = cursor[0] if base is None else base
            if base is None:
                cursor[0] += n
            return arena[:, lo:lo + n]

        HT = part(KT * TOK).rearrange("p (k t) -> p k t", k=KT)
        part(KT * TOK)
        HTH = over("HTH", "arena", 0, KT * TOK)[:, :].rearrange("p (k t) -> p k t", k=KT)
        HTL = over("HTL", "arena", KT * TOK, KT * TOK)[:, :].rearrange("p (k t) -> p k t", k=KT)
        mrg_at = cursor[0]
        MRG = part(KT * TOK).rearrange("p (k t) -> p k t", k=KT)
        ADAS = part(2 * CH, mrg_at + 768).rearrange("p (b n) -> p b n", b=2)
        ZF = part(2 * TOK, mrg_at + 1792).rearrange("p (c t) -> p c t", c=2)
        VT = part(3 * TOK, mrg_at + 1792).rearrange("p (c t) -> p c t", c=3)
        U = part(2 * UW).rearrange("p (c n) -> p c n", c=2)
        ACC = part(2 * AW).rearrange("p (c n) -> p c n", c=2)
        LATE = part(2 * CH, cursor[0] - 2 * AW - 2 * UW).rearrange("p (b n) -> p b n", b=2)

        def adas(c):
            return ADAS[:, c // 2, :] if c < 4 else LATE[:, c % 2, :]

        CT = part(3 * P).rearrange("p (c n) -> p c n", c=3)
        kc_at = cursor[0]
        KC = part(6 * HD).rearrange("p (h d) -> p h d", h=6)
        KO = part(384)
        GP = part(2 * TOK, kc_at).rearrange("p (b n) -> p b n", b=2)
        VC = part(6 * HD).rearrange("p (h d) -> p h d", h=6)
        ZV = part(TT * 384).rearrange("p (t c) -> p t c", t=TT)
        SIG = part(2 * TOK).rearrange("p (b n) -> p b n", b=2)
        PTB = part(2 * 384).rearrange("p (b n) -> p b n", b=2)
        WOT = part(2 * CH, cursor[0] - 4 * TOK).rearrange("p (b n) -> p b n", b=2)
        PR = part(2 * P).rearrange("p (b n) -> p b n", b=2)
        BN = part(TT * 6).rearrange("p (t n) -> p t n", t=TT)
        MV = part(TT * 2).rearrange("p (t n) -> p t n", t=TT)
        LSD = part(TT)
        LRS = part(TT)
        SINK = part(4)
        MX = part(4)
        NM = part(4)
        DS = part(4)
        ES = part(4)
        SM = part(4)
        RI = part(4)
        assert cursor[0] <= ARENA, cursor[0]
        tmp = ring[:, 4:6, :].rearrange("p s n -> p (s n)")
        QC = tmp[:, 0:768].rearrange("p (a t) -> p a t", a=2)
        KTC = tmp[:, 768:1152]
        DQ = tmp[:, 1152:1920].rearrange("p (a t) -> p a t", a=2)
        DK = tmp[:, 1920:2688].rearrange("p (a t) -> p a t", a=2)
        NAB = tmp[:, 2688:4736].rearrange("p (q h n) -> p q h n", q=2, h=4)
        SCB = tmp[:, 4736:6272].rearrange("p (h n) -> p h n", h=4)
        FG = tmp[:, 6272:7808].rearrange("p (t c x n) -> p t c x n", t=TT, c=2, x=2)
        LNX = tmp[:, 6272:7040].rearrange("p (t c) -> p t c", t=TT)
        ROTT = tmp[:, 7808:8064]
        NAM = tmp[:, 1152:1664]
        namask = NAM.rearrange("p (q n) -> p q n", q=2)
        DFT = tmp[:, 4736:6272]
        dft_s = DFT[:, 0:1024].rearrange("p (k n) -> p k n", k=2)
        dft_p = DFT[:, 1024:1280]
        dftc = DFT[:, 1280:1536]
        WSR = over("WSR", "ring", 3 * 4 * D, 4 * D)[:, :].rearrange("p (x b k n) -> p x b k n", x=2, b=2, k=KT)
        BRT = XN[:, :, :].rearrange("p t n -> p (t n)").rearrange("p (b c t) -> p b c t", b=4, c=2)
        cursor[0] = KT * TOK
        XE = part(KT * GRP * 64).rearrange("p (k e s) -> p k e s", k=KT, e=GRP)
        SEL = part(TT * P).rearrange("p (t e s) -> p t e s", t=TT, e=GRP)
        SELG = part(TT * P).rearrange("p (t e s) -> p t e s", t=TT, e=GRP)
        PG = part(TT * P).rearrange("p (t n) -> p t n", t=TT)
        TMP = part(FF)
        AA = part(FF)
        AT = part(KT * 64).rearrange("p (k s) -> p k s", k=KT)
        YS = part(D)
        YP = part(D)
        CMB = part(2 * CH).rearrange("p (b n) -> p b n", b=2)
        AFF = part(TT * NE).rearrange("p (t e) -> p t e", t=TT)
        POSG = part(TT * NE).rearrange("p (g n) -> p g n", g=NE // GRP)
        AFFG = part(TT * NE).rearrange("p (g n) -> p g n", g=NE // GRP)
        WK = part(TOK)
        MSK = part(TOK)
        ONE = part(TOK)
        CUM = part(TOK)
        M8 = part(8)
        RMX = part(4)
        RSM = part(4)
        RRI = part(4)
        assert cursor[0] <= ARENA, cursor[0]

        land = [sem(f"land{s}") for s in range(NSLOT)]
        e_land = [sem(f"e_land{s}") for s in range(NSLOT)]
        full = [sem(f"full{b}") for b in range(8)]
        free = [sem(f"free{b}") for b in range(8)]
        e_full = [sem(f"e_full{b}") for b in range(8)]
        e_free = [sem(f"e_free{b}") for b in range(8)]
        names = ("x_mixed prm_in grow_in sink_in cache_in nab_in nab_ready u_zero sq_done ms_ready sd_ready rs_ready xn_ready "
                 "sc_ready dve_step route_step conv_step rope_ready scores_done scores_read nmax_ready exps_done p_ready "
                 "pv0 pv1 high_act rest_pool high_dve rest_dve w_high w_rest mask_in dft_in gate_add out_kv n2_sq n2_ms n2_sd n2_rs n2_xn wr_in router_max router_exp aff_ready affg_ready "
                 "cum_ready sel_ready selg_ready e_half e_down_half silu_done x_done").split()
        S = {n: sem(n) for n in names}

        GATE_ORDER = [1, 0, 2, 3]
        ADA_AT = {0: 4, 4: 5, 8: 6, 11: 7, 20: 8, 24: 9, 28: 10, 30: 11}

        order = ["ada0", "ada1", "ada2", "ada3", "w0", "w1", "w2", "w3", "w6", "wb01", "ada4", "w7", "ada5", "w4", "ada6",
                 "w5", "ada7", "w8", "wb23", "w9", "ada8", "w10", "ada9", "w11", "ada10", "ada11", "wo0", "wo1"]
        done_at = {n: i - 8 for i, n in enumerate(order[:8])}
        done_at.update(wb01=15, wb23=31, wo0=32, wo1=32)
        done_at.update({f"w{4 + 2 * n + h}": 4 * (2 * GATE_ORDER.index(n) + h) + 1.6 for n in range(4) for h in range(2)})
        done_at.update({f"ada{c}": idx + 0.5 for idx, c in ADA_AT.items()})
        unit_at, used, before, latest, units = {}, [0] * NSLOT, {}, {}, []
        for name in order:
            s = min(range(4 if name == "ada3" else 3), key=lambda x: done_at[latest[x]] if x in latest else x - 100)
            units.append((name, s))
            unit_at[name] = (s, used[s])
            before[name] = latest.get(s)
            latest[s] = name
            used[s] += name not in order[:4]

        def slot(name, cols):
            return ring[:, unit_at[name][0], :].rearrange("p (k n) -> p k n", n=cols)

        parts = [("gb0", "w0", 256), ("ga0", "w0", 0), ("gb1", "w0", 384), ("ga1", "w0", 128),
                 ("zf0", "w1", 0), ("zf1", "w1", 128), ("cq0", "w1", 256), ("cq1", "w1", 384),
                 ("ck", "w2", 0), ("dq0", "w2", 256), ("dq1", "w2", 384), ("zcv", "w2", 128),
                 ("dk0", "w3", 0), ("dk1", "w3", 128), ("dv0", "w3", 256), ("dv1", "w3", 384)]
        EARLY = len(parts)
        for n in GATE_ORDER:
            for k in range(KT):
                parts.append((f"g{n}_{k}", f"w{4 + 2 * n + k // 4}", (k % 4) * P))
        part_of = {tile: i for i, (tile, _, _) in enumerate(parts)}

        ln_var_step = [2 + 3 + 3 + 3 + 1]

        T = BankTurns()
        seq = {"a": 0, "b": 0}

        def tile_a(name):
            T.add(name, seq["a"] % 4)
            seq["a"] += 1

        def tile_b(name):
            T.add(name, 4 + seq["b"] % 4)
            seq["b"] += 1

        for half in range(2):
            for c in (half, half + 2):
                tile_a(f"ada{c}")
                tile_b(f"md{c}")
            if half == 0:
                tile_b("prm")
            for k in range(4 * half, 4 * half + 4):
                tile_a(f"xt{k}")
        for n, _, _ in parts[:EARLY]:
            tile_a(n)
        for n in ("fa0", "fa1", "fa2", "ctxT", "fo0", "fo1", "ko", "vt0", "vt1", "vt2", "rot0", "rot1", "rotk"):
            tile_b(n)
        for n in ("lt0", "lt1", "lt2"):
            tile_b(n)
        GATE_CHUNKS = (4, 5, 10, 11)

        def ada_small_tiles(c):
            for n in ([f"gr{c}_0", f"gr{c}_1"] if c in GATE_CHUNKS else [f"md{c}"]):
                tile_a(n)

        ATT = [("c", 0), ("c", 1), ("c", None), ("d", 0), ("d", 1), ("d", None)]
        OUT_OF = {"c": ("o0", "o1", "o2"), "d": ("o3", "o4", "o5")}

        def scores_at(idx):
            return (idx - 1) // 3 if idx % 3 == 1 and (idx - 1) // 3 < len(ATT) else None

        def out_at(idx):
            return (idx - 4) // 3 if idx % 3 == 1 and 0 <= (idx - 4) // 3 < len(ATT) else None

        for n in GATE_ORDER:
            for k in range(KT):
                idx = GATE_ORDER.index(n) * KT + k
                g = out_at(idx)
                if g is not None:
                    for h in range(4):
                        tile_b(f"pt{g}_{h}")
                tile_a(f"g{n}_{k}")
                if g is not None:
                    tile_a(f"o{g}")
                tile_a(f"p{n}_{k}")
                if idx == 0:
                    tile_b("lb0")
                    tile_b("lb1")
                    while seq["b"] % 4:
                        seq["b"] += 1
                if idx in ADA_AT:
                    tile_a(f"ada{ADA_AT[idx]}")
                if idx - 1 in ADA_AT:
                    ada_small_tiles(ADA_AT[idx - 1])
        for t in range(TT):
            for half in range(2):
                tile_a(f"wo{t}_{half}")

        for k in range(KT):
            (tile_a if k < 4 else tile_b)(f"ya{k}")
        tile_a("yb0")
        tile_b("yb1")
        for n in ("rt", "aft", "post"):
            tile_b(n)

        def open_tile(pe, name):
            b, _, copies_before, _ = T.at[name]
            if copies_before:
                pe.wait_ge(free[b], copies_before)
            return psum[:, b, :]

        def close_tile(ins, name):
            ins.then_inc(full[T.at[name][0]], 1)

        def take(eng, name):
            b, n, _, _ = T.at[name]
            eng.wait_ge(full[b], n + 1)
            return psum[:, b, :]

        def release(ins, name):
            ins.then_inc(free[T.at[name][0]], 1)

        def copied(eng, name):
            b, _, copies_before, copies = T.at[name]
            eng.wait_ge(free[b], copies_before + copies)

        last_tile = {f"ada{c}": f"ada{c}" for c in range(NADA)}
        last_tile.update(wb01="p0_7", wb23="p3_7", wo0="wo2_1", wo1="wo2_1")
        last_part = {unit: i for i, (_, unit, _) in enumerate(parts)}

        def used_up(eng, name):
            if name in last_part:
                eng.wait_ge(S["w_rest"], last_part[name] + 1)
            else:
                take(eng, last_tile[name])

        def landed(eng, name):
            s, n = unit_at[name]
            eng.wait_ge(land[s], 16 * (n + 1))

        def part_src(i):
            _, unit, c0 = parts[i]
            return slot(unit, CH)[:, :, c0:c0 + P]

        def w_unit(l, name):
            kind = name[:3]
            if kind == "ada":
                c = int(name[3:])
                return A["w_ada"][bass.ds(l, 1), :, c * CH:(c + 1) * CH].rearrange("o (k p) n -> p (o k) n", p=P)
            if name[:2] == "wb":
                b = int(name[2])
                return A["w_branch"][bass.ds(l, 1), b:b + 2].rearrange("o b (c p) n -> p (o b c) n", p=P)
            if name[:2] == "wo":
                h = int(name[2])
                return A["w_out"][bass.ds(l, 1), h * 512:(h + 1) * 512, :].rearrange("o (k p) n -> p (o k) n", p=P)
            c = int(name[1:])
            return A["w_in"][bass.ds(l, 1), :, c * CH:(c + 1) * CH].rearrange("o (k p) n -> p (o k) n", p=P)

        E_SRC = (("w_e_gate", 0, 0), ("w_e_up", 0, 2), ("w_e_gate", 1, 1), ("w_e_up", 1, 3), ("w_e_down", 0, 4), ("w_e_down", 1, 5))

        def e_unit(l, e, name, half):
            return A[name][bass.ds(l, 1), bass.ds(e, 1), half * 512:(half + 1) * 512, :].rearrange(
                "o e (k p) n -> p (o e k) n", p=P)

        def e_dst(s):
            return ring[:, s, :].rearrange("p (k n) -> p k n", n=D)

        E = BankTurns()
        for k in range(KT):
            E.add(f"xe{k}", 6 + k % 2)
        E.add("pg", 7)
        for j in range(GRP):
            for half in range(2):
                E.add(f"gu{j}_{half}", 2 * (j % 2) + half)
            E.add(f"at{j}", 6)
            E.add(f"y{j}", 4 + j % 2, 2)
        for i in range(6):
            E.add(f"cm{i}", (7, 0, 1, 2, 3, 6)[i])

        def e_open(pe, g, name):
            b, _, copies_before, _ = E.at[name]
            pe.wait_ge(e_free[b], g * E.copies[b] + copies_before + 1)
            return psum[:, b, :]

        def e_close(ins, name):
            ins.then_inc(e_full[E.at[name][0]], 1)

        def e_take(eng, g, name):
            b, n, _, _ = E.at[name]
            eng.wait_ge(e_full[b], g * E.turns[b] + n + 1)
            return psum[:, b, :]

        def e_release(ins, name):
            ins.then_inc(e_free[E.at[name][0]], 1)

        def e_copied(eng, g, name):
            b, _, copies_before, copies = E.at[name]
            eng.wait_ge(e_free[b], g * E.copies[b] + copies_before + copies + 1)

        def modulate_act(dst, src, which, sec, k, i):
            return nc.scalar.activation(dst, src, ACT.Identity, scale=SC[:, which, k, i:i + 1], bias=MOD[:, sec * KT + k, i:i + 1])

        def modulate_dve(dst, src, which, sec, k, i):
            return nc.vector.tensor_scalar(dst, src, SC[:, which, k, i:i + 1], MOD[:, sec * KT + k, i:i + 1], ALU.mult, ALU.add)

        def rms_part_act(act, sq_sem, ms_sem, sd_sem):
            for t in range(TT):
                nc.scalar.activation(XN[:, t, :], X[:, t, :], ACT.Square, accum_out=SS[:, t:t + 1]).then_inc(sq_sem, 1)
            act.wait_ge(ms_sem, 1)
            nc.scalar.activation(SD[:, 0:TT], MS[:, 0:TT], ACT.Sqrt).then_inc(sd_sem, 1)

        def rms_part_dve(dve, sq_sem, ms_sem, sd_sem, rs_sem, xn_sem):
            dve.wait_ge(sq_sem, TT)
            nc.vector.tensor_scalar(MS[:, 0:TT], SS[:, 0:TT], 1.0 / D, EPS, ALU.mult, ALU.add).then_inc(ms_sem, 1)
            dve.wait_ge(sd_sem, 1)
            nc.vector.reciprocal(RS[:, 0:TT], SD[:, 0:TT]).then_inc(rs_sem, 1)
            dve.wait_ge(rs_sem, 1)
            for t in range(TT):
                nc.vector.tensor_scalar(XN[:, t, :], X[:, t, :], RS[:, t:t + 1], None, ALU.mult).then_inc(xn_sem, 1)

        def load_ada(eng, layer, c):
            eng.dma_start(slot(f"ada{c}", CH), w_unit(layer, f"ada{c}")).then_inc(once[f"ada_in{c}"], 16)

        with nc.Block() as block:
            @block.sync
            def _(sp):
                sp.dma_start(XN[0:8, 0, 0:P], A["c_ctx"].rearrange("(k p) -> k p", p=P)).then_inc(once["cond_in"], 16)
                sp.dma_start(XN[8:16, 0, 0:P], A["c"].rearrange("b (k p) -> (b k) p", p=P)).then_inc(once["cond_in"], 16)
                sp.dma_start(C[:, :], A["const"][:, 0:HELD]).then_inc(once["const_in"], 16)
                load_ada(sp, 0, 0)
                sp.dma_start(X[:, 0, :], A["x_prompt"].rearrange("b s d -> (b s) d")).then_inc(once["x_in"], 16)
                sp.dma_start(X[:, 1:3, :], A["x_sample"].rearrange("b (t p) d -> p (b t) d", p=P)).then_inc(once["x_in"], 16)
                for c in (2, 1, 3):
                    load_ada(sp, 0, c)
                sp.wait_ge(once["x_in"], 32)

            @block.vector
            def _(dve):
                nc.vector.memset(condT[:, :, :], 0.0).then_inc(once["cond_zero"], 1)

            @block.tensor
            def _(pe):
                pe.wait_ge(once["cond_in"], 32)
                pe.wait_ge(once["const_in"], 16)
                nc.tensor.transpose(psum[:, 0, 0:16], XN[0:16, 0, 0:P], ident[0:16, 0:16]).then_inc(once["cond_t"], 1)

            @block.scalar
            def _(act):
                act.wait_ge(once["cond_zero"], 1)
                act.wait_ge(once["cond_t"], 1)
                nc.scalar.activation(condT[:, :, 0:2], psum[:, 0, 0:16].rearrange("p (i k) -> p k i", i=2),
                                     ACT.Silu).then_inc(once["cond_ready"], 1)
                act.wait_ge(once["cond_ready"], 1)

        with nc.Fori(0, DEPTH) as l:
            with nc.Block() as block:
                @block.sync
                def _(sp):
                    def parameters():
                        for dst, src in (
                            (PR[0:48, 0, :], A["b_ada"][bass.ds(l, 1)].rearrange("o (r p) -> (o r) p", p=P)),
                            (PR[48:56, 0, :], A["norm1_g"][bass.ds(l, 1)].rearrange("o (r p) -> (o r) p", p=P)),
                            (PR[56:64, 0, :], A["norm2_g"][bass.ds(l, 1)].rearrange("o (r p) -> (o r) p", p=P)),
                            (PR[0:62, 1, :], A["conv_w"][bass.ds(l, 1)].rearrange("o k (c p) -> (o k c) p", p=P)),
                            (PR[62:64, 1, :], A["conv_b"][bass.ds(l, 1)].rearrange("o (r p) -> (o r) p", p=P)),
                            (PR[64:66, 1, :], A["conv_ln_g"][bass.ds(l, 1)].rearrange("o (r p) -> (o r) p", p=P)),
                            (PR[66:68, 1, :], A["conv_ln_b"][bass.ds(l, 1)].rearrange("o (r p) -> (o r) p", p=P)),
                        ):
                            sp.dma_start(dst, src).then_inc(S["prm_in"], 16)
                        sp.dma_start(SINK, A["win_sink"][bass.ds(l, 1)].broadcast_to((P, 4))).then_inc(S["sink_in"], 16)
                        for name, h0, nh in (("cache_win", 0, 2), ("cache_nat", 2, 4)):
                            for kv, dst in (("k", KC), ("v", VC)):
                                sp.dma_start(dst[:, h0:h0 + nh, :], A[f"{name}_{kv}"][:, bass.ds(l, 1)].rearrange(
                                    "b o h t d -> t (b o h) d")).then_inc(S["cache_in"], 16)

                    def late_constants():
                        sp.dma_start(DFT, A["const"][:, const_at("dft_s")[0]:]).then_inc(S["dft_in"], 16)
                        sp.dma_start(NAM, A["const"][:, const_at("namask")[0]:const_at("namask")[1]]).then_inc(S["mask_in"], 16)
                        sp.dma_start(NAB[:, :, :, :].rearrange("p q h n -> p q (h n)"),
                                     A["na_grid"][bass.ds(l, 1)].rearrange("o q p n -> p (o q) n")).then_inc(S["nab_in"], 16)

                    def gate_biases():
                        sp.dma_start(WR[:, :, :], A["w_router"][bass.ds(l, 1)].rearrange("o (k p) e -> p (o k) e", p=P)).then_inc(
                            S["wr_in"], 16)
                        for gate, sec in ((0, 2), (1, 5)):
                            for i in range(2):
                                sp.dma_start(GROW[:, gate, i, :], A["b_ada"][bass.ds(l, 1), sec * D:(sec + 1) * D].broadcast_to(
                                    (P, D))).then_inc(S["grow_in"], 16)

                    def prompt_kv():
                        copied(sp, "ko")
                        copied(sp, "vt0")
                        for name, src, h0, nh in (("new_win_k", KO, 0, 2), ("new_nat_k", KO, 2, 4),
                                                  ("new_win_v", ZV[:, 0, :], 0, 2), ("new_nat_v", ZV[:, 0, :], 2, 4)):
                            sp.dma_start(A[name][:, bass.ds(l, 1)].rearrange("b o h t d -> t (b o h) d"),
                                         src[:, h0 * HD:(h0 + nh) * HD].rearrange("p (h d) -> p h d", d=HD)).then_inc(S["out_kv"], 16)

                    parameters()
                    for name, s in units[4:]:
                        cols = D if name[:2] in ("wb", "wo") else CH
                        used_up(sp, before[name])
                        sp.dma_start(slot(name, cols), w_unit(l, name)).then_inc(land[s], 16)
                        if name == "w1":
                            late_constants()
                        elif name == "w3":
                            gate_biases()
                        elif name == "w7":
                            prompt_kv()
                    sp.wait_ge(S["out_kv"], 64)
                    for name, half, s in E_SRC:
                        if s == 3:
                            take(sp, parts[-1][0])
                        elif s in latest:
                            used_up(sp, latest[s])
                        elif s == NSLOT - 2:
                            copied(sp, f"o{len(ATT) - 1}")
                        sp.dma_start(e_dst(s), e_unit(l, 0, name, half)).then_inc(e_land[s], 16)

                @block.gpsimd
                def _(pool):
                    nc.gpsimd.memset(U[:, :, :], 0.0).then_inc(S["u_zero"], 1)
                    for k in range(0, KT, 2):
                        pool.wait_ge(S["high_act"], k // 2 + 1)
                        nc.gpsimd.tensor_tensor(HTL[:, k, :], SIG[:, (k // 2) % 2, :], HTH[:, k, :].bitcast(F32),
                                                ALU.subtract).then_inc(S["rest_pool"], 1)
                    for i in range(len(parts)):
                        src = part_src(i)
                        pool.wait_ge(S["w_high"], i + 1)
                        nc.gpsimd.tensor_tensor(WSR[:, 1, i % 2], src, WSR[:, 0, i % 2].bitcast(F32), ALU.subtract).then_inc(S["w_rest"], 1)
                        if i == 5:
                            pool.wait_ge(S["nab_in"], 16)
                            pool.wait_ge(S["mask_in"], 16)
                            nc.gpsimd.tensor_tensor(NAB, NAB, namask.unsqueeze(2).broadcast_to((P, 2, 4, DEC)),
                                                    ALU.add).then_inc(S["nab_ready"], 1)

                @block.tensor
                def _(pe):
                    def ada_main(c):
                        name = f"ada{c}"
                        ps = open_tile(pe, name)
                        if c < 4:
                            pe.wait_ge(once[f"ada_in{c}"], l * 16 + 16)
                        else:
                            landed(pe, name)
                        w = slot(name, CH)
                        for k2 in range(2):
                            for j in range(4):
                                ins = nc.tensor.matmul(ps[32 * j:32 * j + 32, :], condT[:, 4 * k2 + j, :], w[:, 4 * k2 + j, :],
                                                       start=(k2 == 0), stop=(k2 == 1))
                        close_tile(ins, name)

                    def ada_mod(c):
                        ps = open_tile(pe, f"md{c}")
                        copied(pe, f"ada{c}")
                        for s in range(4):
                            ins = nc.tensor.matmul(ps[:, 2 * s:2 * s + 2], adas(c)[:, s * P:(s + 1) * P], esum[:, :, 0],
                                                   start=True, stop=True)
                        close_tile(ins, f"md{c}")

                    def ada_gate(c):
                        for i in range(2):
                            ps = open_tile(pe, f"gr{c}_{i}")
                            copied(pe, f"ada{c}")
                            ins = nc.tensor.matmul(ps[:, :], esum[:, i, :], adas(c), start=True, stop=True)
                            close_tile(ins, f"gr{c}_{i}")

                    def ada_small(c):
                        (ada_gate if c in GATE_CHUNKS else ada_mod)(c)

                    for half in range(2):
                        for c in (half, half + 2):
                            ada_main(c)
                        for c in (half, half + 2):
                            ada_mod(c)
                        if half == 0:
                            ps = open_tile(pe, "prm")
                            pe.wait_ge(S["prm_in"], 7 * 16)
                            nc.tensor.transpose(ps[:, 0:64], PR[0:64, 0, :], ident[0:64, 0:64])
                            close_tile(nc.tensor.transpose(ps[:, 64:132], PR[0:68, 1, :], ident[0:68, 0:68]), "prm")
                            pe.wait_ge(S["xn_ready"], TT)
                        for k in range(4 * half, 4 * half + 4):
                            ps = open_tile(pe, f"xt{k}")
                            for t in range(TT):
                                ins = nc.tensor.transpose(ps[:, t * P:(t + 1) * P], XN[:, t, k * P:(k + 1) * P], ident)
                            close_tile(ins, f"xt{k}")

                    def zt(tile):
                        i = part_of[tile]
                        ps = open_tile(pe, tile)
                        pe.wait_ge(S["w_rest"], i + 1)
                        for k in range(KT):
                            if i == 0:
                                pe.wait_ge(S["rest_dve" if k % 2 else "rest_pool"], k // 2 + 1)
                            for w, x in ((0, HTH), (0, HTL), (1, HTH)):
                                ins = nc.tensor.matmul(ps[:, 0:TOK], WSR[:, w, i % 2, k, :], x[:, k, :],
                                                       start=(k == 0 and w == 0 and x is HTH), stop=(k == KT - 1 and w == 1))
                        close_tile(ins, tile)

                    for n in ("gb0", "ga0", "gb1", "ga1", "zf0", "zf1", "cq0"):
                        zt(n)
                    pe.wait_ge(S["dft_in"], 16)
                    for c in range(2):
                        copied(pe, f"zf{c}")
                    for t in range(TT):
                        ps = open_tile(pe, f"fa{t}")
                        for c in range(2):
                            ins = nc.tensor.matmul(ps[:, c * 256:(c + 1) * 256], ZF[:, c, t * P:(t + 1) * P], dftc,
                                                   start=True, stop=True)
                        close_tile(ins, f"fa{t}")
                    zt("cq1")
                    ps = open_tile(pe, "ctxT")
                    pe.wait_ge(S["cache_in"], 64)
                    for c in range(3):
                        ins = nc.tensor.transpose(ps[:, c * P:(c + 1) * P],
                                                  KC[:, 2 * c:2 * c + 2, :].rearrange("p h d -> p (h d)"), ident)
                    close_tile(ins, "ctxT")
                    zt("ck")
                    for t in range(TT):
                        copied(pe, f"fa{t}")
                    for c in range(2):
                        ps = open_tile(pe, f"fo{c}")
                        for x in range(2):
                            for t in (1, 2):
                                ins = nc.tensor.matmul(ps[:, P:TOK], FG[:, t, c, x, :], dft_s[:, t - 1, x * DEC:(x + 1) * DEC],
                                                       start=(x == 0 and t == 1), stop=(x == 1 and t == 2))
                        for x in range(2):
                            ins = nc.tensor.matmul(ps[:, 0:P], FG[:, 0, c, x, :], dft_p[:, x * SEQ:(x + 1) * SEQ],
                                                   start=(x == 0), stop=(x == 1))
                        close_tile(ins, f"fo{c}")
                    for n in ("dq0", "dq1", "zcv", "dk0", "dk1", "dv0", "dv1"):
                        zt(n)
                    ps = open_tile(pe, "ko")
                    for n in ("cq0", "cq1", "ck", "dk0", "dk1"):
                        copied(pe, n)
                    for c, src in enumerate((KTC[:, 0:P], DK[:, 0, 0:P], DK[:, 1, 0:P])):
                        ins = nc.tensor.transpose(ps[:, c * P:(c + 1) * P], src, ident)
                    close_tile(ins, "ko")
                    for n in ("zcv", "dv0", "dv1"):
                        copied(pe, n)
                    for t in range(TT):
                        ps = open_tile(pe, f"vt{t}")
                        for c in range(3):
                            ins = nc.tensor.transpose(ps[:, c * P:(c + 1) * P], VT[:, c, t * P:(t + 1) * P], ident)
                        close_tile(ins, f"vt{t}")
                    for n, src in (("rot0", QC[:, 0, P:TOK]), ("rot1", QC[:, 1, P:TOK]), ("rotk", KTC[:, P:TOK])):
                        ps = open_tile(pe, n)
                        close_tile(nc.tensor.matmul(ps[:, 0:DEC], rot, src, start=True, stop=True), n)
                    pe.wait_ge(S["conv_step"], 2 * CONV_K)
                    for t in range(TT):
                        ps = open_tile(pe, f"lt{t}")
                        a0 = 0 if t == 0 else USAMP - PADC + (t - 1) * P
                        for c in range(2):
                            ins = nc.tensor.transpose(ps[:, c * P:(c + 1) * P], ACC[:, c, a0:a0 + P], ident)
                        close_tile(ins, f"lt{t}")
                    def normed_back():
                        for t in range(TT):
                            copied(pe, f"lt{t}")
                        for c in range(2):
                            ps = open_tile(pe, f"lb{c}")
                            for t in range(TT):
                                ins = nc.tensor.transpose(ps[:, t * P:(t + 1) * P], LNX[:, t, c * P:(c + 1) * P], ident)
                            close_tile(ins, f"lb{c}")

                    def att_scores(g):
                        br, qt = ATT[g]
                        if g == 0:
                            pe.wait_ge(S["rope_ready"], 3)
                            for n in ("ctxT", "dq0", "dq1", "vt0", "vt1", "vt2"):
                                copied(pe, n)
                        q0 = 0 if qt is None else P + qt * P
                        for h in range(4):
                            b = 4 + h
                            pe.wait_ge(free[b], T.at[f"pt{g}_{h}"][2])
                            if br == "c":
                                r = slice(64 * (h // 2), 64 * (h // 2) + 64)
                                q, kk, ct = QC[r, h % 2, q0:q0 + P], KTC[r, :], CT[r, 0, :]
                            else:
                                r = slice(64 * (h % 2), 64 * (h % 2) + 64)
                                q, kk, ct = DQ[r, h // 2, q0:q0 + P], DK[r, h // 2, :], CT[r, 1 + h // 2, :]
                            if qt is None:
                                ins = nc.tensor.matmul(psum[:, b, 0:P], q, kk[:, 0:P], start=True, stop=True)
                            else:
                                nc.tensor.matmul(psum[:, b, 0:DEC], q, kk[:, P:TOK], start=True, stop=True)
                                ins = nc.tensor.matmul(psum[:, b, DEC:DEC + P], q, ct, start=True, stop=True)
                        ins.then_inc(S["scores_done"], 1)

                    def probs_t(g, h):
                        if h == 0:
                            pe.wait_ge(S["scores_read"], g + 1)
                            pe.wait_ge(S["p_ready"], g + 1)
                        name = f"pt{g}_{h}"
                        b = T.at[name][0]
                        for j in range(1 if ATT[g][1] is None else 3):
                            ins = nc.tensor.transpose(psum[:, b, j * P:(j + 1) * P], SCB[:, h, j * P:(j + 1) * P], ident)
                        close_tile(ins, name)

                    def pv(g, h):
                        br, qt = ATT[g]
                        if h == 0:
                            open_tile(pe, f"o{g}")
                        po = psum[:, T.at[f"o{g}"][0], :]
                        copied(pe, f"pt{g}_{h}")
                        if br == "c":
                            kv = h // 2
                            vl, vc = slice(kv * HD, (kv + 1) * HD), kv
                        else:
                            vl, vc = slice(P + h * HD, P + (h + 1) * HD), 2 + h
                        vs = [ZV[:, 0, vl]] if qt is None else [ZV[:, 1, vl], ZV[:, 2, vl], VC[:, vc, :]]
                        for j, v in enumerate(vs):
                            ins = nc.tensor.matmul(po[64 * (h % 2):64 * (h % 2) + 64, (h // 2) * P:(h // 2 + 1) * P],
                                                   v, PTB[:, h % 2, j * P:(j + 1) * P],
                                                   start=(j == 0), stop=(j == len(vs) - 1))
                        if h < 2:
                            ins.then_inc(S[f"pv{h}"], 1)
                        elif h == 3:
                            close_tile(ins, f"o{g}")

                    for n in GATE_ORDER:
                        wb = slot("wb01" if n < 2 else "wb23", D)
                        landed(pe, "wb01" if n < 2 else "wb23")
                        for k in range(KT):
                            idx = GATE_ORDER.index(n) * KT + k
                            go, gs = out_at(idx), scores_at(idx)
                            if go is not None:
                                probs_t(go, 0)
                                probs_t(go, 1)
                            zt(f"g{n}_{k}")
                            if go is not None:
                                pv(go, 0)
                                probs_t(go, 2)
                                pv(go, 1)
                                probs_t(go, 3)
                            ps = open_tile(pe, f"p{n}_{k}")
                            if k == 0:
                                for x in {1: ("fo0", "fo1"), 0: ("lb0", "lb1"), 2: OUT_OF["c"], 3: OUT_OF["d"]}[n]:
                                    copied(pe, x)
                            for c in range(2):
                                ins = nc.tensor.matmul(ps[:, 0:TOK], wb[:, 2 * (n % 2) + c, k * P:(k + 1) * P], BRT[:, n, c, :],
                                                       start=(c == 0), stop=(c == 1))
                            close_tile(ins, f"p{n}_{k}")
                            if idx == 0:
                                normed_back()
                            if go is not None:
                                pv(go, 2)
                                pv(go, 3)
                            if gs is not None:
                                att_scores(gs)
                            if idx in ADA_AT:
                                ada_main(ADA_AT[idx])
                            if idx - 1 in ADA_AT:
                                ada_small(ADA_AT[idx - 1])

                    landed(pe, "wo0")
                    landed(pe, "wo1")
                    pe.wait_ge(S["gate_add"], 3 * KT)
                    for t in range(TT):
                        for half in range(2):
                            ps = open_tile(pe, f"wo{t}_{half}")
                            for k in range(KT):
                                wo = slot(f"wo{k // 4}", D)
                                ins = nc.tensor.matmul(ps[:, :], MRG[:, k, t * P:(t + 1) * P],
                                                       wo[:, k % 4, half * CH:(half + 1) * CH], start=(k == 0), stop=(k == KT - 1))
                            close_tile(ins, f"wo{t}_{half}")
                    pe.wait_ge(S["n2_xn"], 2)
                    for k in range(KT):
                        ps = open_tile(pe, f"ya{k}")
                        for t in range(2):
                            ins = nc.tensor.transpose(ps[:, t * P:(t + 1) * P], XN[:, t, k * P:(k + 1) * P], ident)
                        close_tile(ins, f"ya{k}")
                    pe.wait_ge(S["n2_xn"], TT)
                    for j in range(2):
                        ps = open_tile(pe, f"yb{j}")
                        for k in range(4):
                            ins = nc.tensor.transpose(ps[:, k * P:(k + 1) * P], XN[:, 2, (4 * j + k) * P:(4 * j + k + 1) * P], ident)
                        close_tile(ins, f"yb{j}")

                @block.scalar
                def _(act):
                    rms_part_act(act, S["sq_done"], S["ms_ready"], S["sd_ready"])

                    def copy_out(name, dst, src):
                        ps = take(act, name)
                        release(nc.scalar.activation(dst, src(ps), ACT.Copy), name)

                    for k in range(0, KT, 2):
                        if k % 4 == 0:
                            for c in (k // 4, k // 4 + 2):
                                if k:
                                    copied(act, f"md{c - 1}")
                                copy_out(f"ada{c}", adas(c), lambda ps: ps)
                            act.wait_ge(S["sc_ready"], k // 4 + 1)
                        ps = take(act, f"xt{k}")
                        hx = SIG[:, (k // 2) % 2, :]
                        if k >= 4:
                            act.wait_ge(S["rest_pool"], k // 2 - 1)
                        modulate_act(hx[:, 0:P], ps[:, 0:P], 0, 0, k, 0)
                        release(modulate_act(hx[:, P:TOK], ps[:, P:TOK], 0, 0, k, 1), f"xt{k}")
                        copied(act, f"xt{k}")
                        nc.scalar.activation(HTH[:, k, :], hx, ACT.Copy).then_inc(S["high_act"], 1)

                    def w_high(i):
                        if i < len(parts):
                            if i < 2:
                                take(act, "ada3")
                            landed(act, parts[i][1])
                            nc.scalar.activation(WSR[:, 0, i % 2], part_src(i), ACT.Copy).then_inc(S["w_high"], 1)

                    w_high(0)
                    w_high(1)
                    for c in range(2):
                        ps = take(act, f"gb{c}")
                        w_high(part_of[f"gb{c}"] + 2)
                        if c == 0:
                            act.wait_ge(S["rest_pool"], KT // 2)
                        release(nc.scalar.activation(SIG[:, c, :], ps[:, 0:TOK], ACT.Sigmoid), f"gb{c}")
                        take(act, f"ga{c}")
                        w_high(part_of[f"ga{c}"] + 2)

                    def copy_z(name, dst):
                        ps = take(act, name)
                        w_high(part_of[name] + 2)
                        release(nc.scalar.activation(dst, ps[:, 0:TOK], ACT.Copy), name)

                    for c in range(2):
                        copy_z(f"zf{c}", ZF[:, c, :])

                    def query(a):
                        ps = take(act, f"cq{a}")
                        w_high(part_of[f"cq{a}"] + 2)
                        nc.scalar.activation(QC[64 * a:64 * a + 64, 0, :], ps[0:64, 0:TOK], ACT.Copy)
                        release(nc.scalar.activation(QC[64 * a:64 * a + 64, 1, :], ps[64:128, 0:TOK], ACT.Copy), f"cq{a}")

                    query(0)
                    for t in range(TT):
                        copy_out(f"fa{t}", FG[:, t].rearrange("p c x n -> p (c x n)"), lambda ps: ps)
                    query(1)
                    copy_out("ctxT", CT, lambda ps: ps[:, 0:384].rearrange("p (c n) -> p c n", c=3))
                    copy_z("ck", KTC)
                    for c in range(2):
                        copy_out(f"fo{c}", BRT[:, 1, c, :], lambda ps: ps[:, 0:TOK])
                    act.wait_ge(S["nab_ready"], 1)
                    for n, dst in (("dq0", DQ[:, 0, :]), ("dq1", DQ[:, 1, :]), ("zcv", VT[:, 0, :]), ("dk0", DK[:, 0, :]),
                                   ("dk1", DK[:, 1, :]), ("dv0", VT[:, 1, :]), ("dv1", VT[:, 2, :])):
                        copy_z(n, dst)
                    copy_out("ko", KO, lambda ps: ps[:, 0:384])
                    for t in range(TT):
                        copy_out(f"vt{t}", ZV[:, t, :], lambda ps: ps[:, 0:384])
                    act.wait_ge(S["dve_step"], ln_var_step[0])
                    nc.scalar.activation(LSD, MV[:, :, 1], ACT.Sqrt).then_inc(S["exps_done"], 1)
                    for idx in range(4 * KT):
                        n, k = GATE_ORDER[idx // KT], idx % KT
                        go, ge = out_at(idx), scores_at(idx - 1)
                        nk = 1 if go is not None and ATT[go][1] is None else 3
                        if go is not None:
                            copy_out(f"pt{go}_0", PTB[:, 0, 0:nk * P], lambda ps: ps[:, 0:nk * P])
                        ps = take(act, f"g{n}_{k}")
                        w_high(EARLY + idx + 2)
                        if idx == 0:
                            copied(act, "ga0")
                            copied(act, "ga1")
                        if idx >= 2:
                            m, kk = GATE_ORDER[(idx - 2) // KT], (idx - 2) % KT
                            copied(act, f"p{m}_{kk}")
                        release(nc.scalar.activation(SIG[:, idx % 2, :], ps[:, 0:TOK], ACT.Sigmoid), f"g{n}_{k}")
                        if idx == 0:
                            for c in range(2):
                                ps = take(act, f"lb{c}")
                                release(nc.scalar.activation(BRT[:, 0, c, :], ps[:, 0:TOK], ACT.Silu, scale=PRM[:, 128 + c:129 + c],
                                                             bias=PRM[:, 130 + c:131 + c]), f"lb{c}")
                        if go is not None:
                            act.wait_ge(S["pv0"], go + 1)
                            copy_out(f"pt{go}_2", PTB[:, 0, 0:nk * P], lambda ps: ps[:, 0:nk * P])
                        if ge is not None:
                            w = P if ATT[ge][1] is None else TOK
                            act.wait_ge(S["nmax_ready"], ge + 1)
                            if ATT[ge][0] == "c":
                                nc.scalar.activation(ES, DS, ACT.Exp)
                            for h in range(4):
                                ins = nc.scalar.activation(SCB[:, h, 0:w], SCB[:, h, 0:w], ACT.Exp, bias=NM[:, h:h + 1],
                                                           accum_out=SM[:, h:h + 1])
                            ins.then_inc(S["exps_done"], 1)
                        if idx in ADA_AT:
                            copy_out(f"ada{ADA_AT[idx]}", adas(ADA_AT[idx]), lambda ps: ps)
                    for t in range(TT):
                        act.wait_ge(S["x_mixed"], 2 * t + 2)
                        nc.scalar.activation(XN[:, t, :], X[:, t, :], ACT.Square, accum_out=SS[:, t:t + 1]).then_inc(S["n2_sq"], 1)
                        act.wait_ge(S["n2_ms"], t + 1)
                        nc.scalar.activation(SD[:, t:t + 1], MS[:, t:t + 1], ACT.Sqrt).then_inc(S["n2_sd"], 1)
                    act.wait_ge(S["sc_ready"], 4)
                    for c in (6, 7):
                        copied(act, f"md{c}")
                    for k in range(0, KT, 2):
                        ps = take(act, f"ya{k}")
                        modulate_act(HT[:, k, 0:P], ps[:, 0:P], 1, 3, k, 0)
                        release(modulate_act(HT[:, k, P:2 * P], ps[:, P:2 * P], 1, 3, k, 1), f"ya{k}")
                    ps = take(act, "yb0")
                    for k in range(4):
                        ins = modulate_act(HT[:, k, 2 * P:TOK], ps[:, k * P:(k + 1) * P], 1, 3, k, 1)
                    release(ins, "yb0")

                @block.vector
                def _(dve):
                    steps = [0]

                    def step(ins):
                        steps[0] += 1
                        ins.then_inc(S["dve_step"], 1)

                    def settle():
                        dve.wait_ge(S["dve_step"], steps[0])

                    rms_part_dve(dve, S["sq_done"], S["ms_ready"], S["sd_ready"], S["rs_ready"], S["xn_ready"])
                    ps = take(dve, "prm")
                    release(nc.vector.tensor_copy(PRM[:, :], ps[:, 0:132]), "prm")

                    def shift_scale(c):
                        ps = take(dve, f"md{c}")
                        release(nc.vector.tensor_tensor(MOD[:, 4 * c:4 * c + 4, :], ps[:, 0:8].rearrange("p (n i) -> p n i", i=2),
                                                        PRM[:, 4 * c:4 * c + 4].unsqueeze(2).broadcast_to((P, 4, 2)), ALU.add), f"md{c}")

                    def gain(which, scale_sec, col, half):
                        ks = slice(4 * half, 4 * half + 4)
                        copied(dve, f"md{2 * scale_sec + half}")
                        nc.vector.scalar_tensor_tensor(
                            SC[:, which, ks, :], MOD[:, scale_sec * KT + 4 * half:scale_sec * KT + 4 * half + 4, :], 1.0,
                            PRM[:, col + 4 * half:col + 4 * half + 4].unsqueeze(2).broadcast_to((P, 4, 2)), ALU.add,
                            ALU.mult).then_inc(S["sc_ready"], 1)

                    copied(dve, "prm")
                    for k in range(1, KT, 2):
                        if k % 4 == 1:
                            half = k // 4
                            shift_scale(half)
                            shift_scale(half + 2)
                            gain(0, 1, 48, half)
                            dve.wait_ge(S["sc_ready"], half + 1)
                        ps = take(dve, f"xt{k}")
                        hx = PTB[:, (k // 2) % 2, :]
                        if k >= 4:
                            dve.wait_ge(S["rest_dve"], k // 2 - 1)
                        modulate_dve(hx[:, 0:P], ps[:, 0:P], 0, 0, k, 0)
                        release(modulate_dve(hx[:, P:TOK], ps[:, P:TOK], 0, 0, k, 1), f"xt{k}")
                        copied(dve, f"xt{k}")
                        nc.vector.tensor_copy(HTH[:, k, :], hx).then_inc(S["high_dve"], 1)
                        dve.wait_ge(S["high_dve"], k // 2 + 1)
                        nc.vector.tensor_tensor(HTL[:, k, :], hx, HTH[:, k, :].bitcast(F32), ALU.subtract).then_inc(S["rest_dve"], 1)
                    dve.wait_ge(S["u_zero"], 1)
                    for c in range(2):
                        ps = take(dve, f"ga{c}")
                        copied(dve, f"gb{c}")
                        step(nc.vector.tensor_tensor(U[:, c, PADC:PADC + SEQ], ps[:, 0:P], SIG[:, c, 0:P], ALU.mult))
                        release(nc.vector.tensor_tensor(U[:, c, USAMP:USAMP + DEC], ps[:, P:TOK], SIG[:, c, P:TOK], ALU.mult),
                                f"ga{c}")
                    settle()
                    copied(dve, "ga0")
                    copied(dve, "ga1")
                    for k in range(CONV_K):
                        for c in range(2):
                            w = PRM[:, 64 + 2 * k + c:65 + 2 * k + c]
                            if k == 0:
                                ins = nc.vector.tensor_scalar(ACC[:, c, :], U[:, c, 0:AW], w, PRM[:, 126 + c:127 + c],
                                                              ALU.mult, ALU.add)
                            else:
                                dve.wait_ge(S["conv_step"], 2 * (k - 1) + c + 1)
                                ins = nc.vector.scalar_tensor_tensor(ACC[:, c, :], U[:, c, k:k + AW], w, ACC[:, c, :],
                                                                     ALU.mult, ALU.add)
                            ins.then_inc(S["conv_step"], 1)
                    for i, (n, x) in enumerate((("rot0", QC[:, 0, P:TOK]), ("rot1", QC[:, 1, P:TOK]), ("rotk", KTC[:, P:TOK]))):
                        ps = take(dve, n)
                        step(nc.vector.tensor_tensor(x, x, cosT, ALU.mult))
                        release(nc.vector.tensor_tensor(ROTT, ps[:, 0:DEC], sinT, ALU.mult), n)
                        settle()
                        copied(dve, n)
                        nc.vector.tensor_tensor(x, x, ROTT, ALU.add).then_inc(S["rope_ready"], 1)
                        dve.wait_ge(S["rope_ready"], i + 1)
                    dve.wait_ge(S["grow_in"], 64)

                    def gate_rows(c):
                        gate, half = (0, c - 4) if c < 6 else (1, c - 10)
                        for i in range(2):
                            ps = take(dve, f"gr{c}_{i}")
                            dst = GROW[:, gate, i, half * CH:(half + 1) * CH]
                            release(nc.vector.tensor_tensor(dst, dst, ps, ALU.add), f"gr{c}_{i}")

                    def ada_end(c):
                        if c in GATE_CHUNKS:
                            gate_rows(c)
                        else:
                            shift_scale(c)
                        if c in (8, 9):
                            gain(1, 4, 56, c - 8)

                    for t in range(TT):
                        ps = take(dve, f"lt{t}")
                        step(nc.vector.bn_stats(BN[:, t, :], ps[:, 0:BW]))
                    settle()
                    for t in range(TT):
                        step(nc.vector.bn_aggr(MV[:, t, :], BN[:, t, :]))
                    settle()
                    step(nc.vector.tensor_scalar(MV[:, :, 1], MV[:, :, 1], EPS, None, ALU.add))
                    assert steps[0] == ln_var_step[0], steps[0]
                    dve.wait_ge(S["exps_done"], 1)
                    step(nc.vector.reciprocal(LRS, LSD))
                    settle()
                    for t in range(TT):
                        release(nc.vector.tensor_scalar(LNX[:, t, :], psum[:, T.at[f"lt{t}"][0], 0:BW], MV[:, t, 0:1],
                                                        LRS[:, t:t + 1], ALU.subtract, ALU.mult), f"lt{t}")
                    dve.wait_ge(S["sink_in"], 16)
                    dve.wait_ge(S["nab_ready"], 1)
                    adds = [0]

                    def gate_mul(idx):
                        n, k = GATE_ORDER[idx // KT], idx % KT
                        copied(dve, f"g{n}_{k}")
                        ps = take(dve, f"p{n}_{k}")
                        if idx == KT:
                            dve.wait_ge(S["out_kv"], 64)
                        if idx < KT:
                            release(nc.vector.tensor_tensor(MRG[:, k, :], SIG[:, idx % 2, :], ps[:, 0:TOK], ALU.mult), f"p{n}_{k}")
                        else:
                            if adds[0]:
                                dve.wait_ge(S["gate_add"], adds[0])
                            release(nc.vector.tensor_tensor(GP[:, idx % 2, :], SIG[:, idx % 2, :], ps[:, 0:TOK], ALU.mult),
                                    f"p{n}_{k}")
                            copied(dve, f"p{n}_{k}")
                            nc.vector.tensor_tensor(MRG[:, k, :], MRG[:, k, :], GP[:, idx % 2, :], ALU.add).then_inc(S["gate_add"], 1)
                            adds[0] += 1

                    for idx in range(4 * KT):
                        go, gs, ge = out_at(idx), scores_at(idx), scores_at(idx - 1)
                        if go is not None:
                            nk = 1 if ATT[go][1] is None else 3
                            for h in (1, 3):
                                ps = take(dve, f"pt{go}_{h}")
                                if h == 3:
                                    dve.wait_ge(S["pv1"], go + 1)
                                release(nc.vector.tensor_copy(PTB[:, 1, 0:nk * P], ps[:, 0:nk * P]), f"pt{go}_{h}")
                        gate_mul(idx)
                        if go is not None:
                            br, qt = ATT[go]
                            ps = take(dve, f"o{go}")
                            t0 = 0 if qt is None else P + qt * P
                            release(nc.vector.tensor_copy(BRT[:, 2 if br == "c" else 3, :, t0:t0 + P],
                                                          ps[:, 0:2 * P].rearrange("p (c n) -> p c n", c=2)), f"o{go}")
                        if gs is not None:
                            br, qt = ATT[gs]
                            w = P if qt is None else TOK
                            dve.wait_ge(S["scores_done"], gs + 1)
                            if qt is None:
                                nc.vector.tensor_scalar(SCB[:, :, 0:P], psum[:, 4:8, 0:P], SCALE, None, ALU.mult).then_inc(
                                    S["scores_read"], 1)
                            else:
                                bias = NAB[:, qt, :, :] if br == "d" else winmask[:, qt, :].unsqueeze(1).broadcast_to((P, 4, DEC))
                                step(nc.vector.scalar_tensor_tensor(SCB[:, :, 0:DEC], psum[:, 4:8, 0:DEC], SCALE, bias, ALU.mult,
                                                                    ALU.add))
                                nc.vector.tensor_scalar(SCB[:, :, DEC:TOK], psum[:, 4:8, DEC:TOK], SCALE, None, ALU.mult).then_inc(
                                    S["scores_read"], 1)
                                settle()
                            dve.wait_ge(S["scores_read"], gs + 1)
                            step(nc.vector.tensor_reduce(MX, SCB[:, :, 0:w], AX_X, ALU.max))
                            settle()
                            if br == "c":
                                step(nc.vector.tensor_tensor(MX, MX, SINK, ALU.max))
                                settle()
                                step(nc.vector.tensor_tensor(DS, SINK, MX, ALU.subtract))
                            nc.vector.tensor_scalar(NM, MX, -1.0, None, ALU.mult).then_inc(S["nmax_ready"], 1)
                        if ge is not None:
                            br, qt = ATT[ge]
                            w = P if qt is None else TOK
                            dve.wait_ge(S["exps_done"], ge + 2)
                            if br == "c":
                                step(nc.vector.tensor_tensor(SM, SM, ES, ALU.add))
                                settle()
                            step(nc.vector.reciprocal(RI, SM))
                            settle()
                            nc.vector.tensor_tensor(SCB[:, :, 0:w], SCB[:, :, 0:w], RI.unsqueeze(2).broadcast_to((P, 4, w)),
                                                    ALU.mult).then_inc(S["p_ready"], 1)
                        if idx - 1 in ADA_AT:
                            ada_end(ADA_AT[idx - 1])
                    dve.wait_ge(S["gate_add"], 3 * KT)

                    def second_norm(t):
                        dve.wait_ge(S["n2_sq"], t + 1)
                        nc.vector.tensor_scalar(MS[:, t:t + 1], SS[:, t:t + 1], 1.0 / D, EPS, ALU.mult, ALU.add).then_inc(S["n2_ms"], 1)
                        dve.wait_ge(S["n2_sd"], t + 1)
                        nc.vector.reciprocal(RS[:, t:t + 1], SD[:, t:t + 1]).then_inc(S["n2_rs"], 1)
                        dve.wait_ge(S["n2_rs"], t + 1)
                        nc.vector.tensor_scalar(XN[:, t, :], X[:, t, :], RS[:, t:t + 1], None, ALU.mult).then_inc(S["n2_xn"], 1)

                    for i, (t, half) in enumerate((t, h) for t in range(TT) for h in range(2)):
                        ps = take(dve, f"wo{t}_{half}")
                        if i == 0:
                            for c in (4, 5):
                                for gi in range(2):
                                    copied(dve, f"gr{c}_{gi}")
                        cols = slice(half * CH, (half + 1) * CH)
                        if i:
                            dve.wait_ge(S["x_mixed"], i)
                        release(nc.vector.tensor_tensor(WOT[:, i % 2, :], ps, GROW[:, 0, min(t, 1), cols], ALU.mult), f"wo{t}_{half}")
                        copied(dve, f"wo{t}_{half}")
                        nc.vector.tensor_tensor(X[:, t, cols], X[:, t, cols], WOT[:, i % 2, :], ALU.add).then_inc(S["x_mixed"], 1)
                        if i in (2, 4):
                            second_norm(i // 2 - 1)
                    second_norm(2)
                    dve.wait_ge(S["sc_ready"], 4)
                    for c in (6, 7):
                        copied(dve, f"md{c}")
                    for k in range(1, KT, 2):
                        ps = take(dve, f"ya{k}")
                        modulate_dve(HT[:, k, 0:P], ps[:, 0:P], 1, 3, k, 0)
                        release(modulate_dve(HT[:, k, P:2 * P], ps[:, P:2 * P], 1, 3, k, 1), f"ya{k}")
                    ps = take(dve, "yb1")
                    for k in range(4):
                        ins = modulate_dve(HT[:, 4 + k, 2 * P:TOK], ps[:, k * P:(k + 1) * P], 1, 3, 4 + k, 1)
                    release(ins, "yb1")

            with nc.Block() as block:
                @block.sync
                def _(sp):
                    def load(g, j, e):
                        done = 4 * g + j + 1
                        for name, half, s in E_SRC:
                            if s == 0:
                                sp.wait_ge(S["e_half"], done)
                            elif s == 1:
                                e_take(sp, g, f"gu{j}_1")
                            elif s == 4:
                                sp.wait_ge(S["e_down_half"], done)
                            elif s == 5:
                                e_take(sp, g, f"y{j}")
                            sp.dma_start(e_dst(s), e_unit(l, e, name, half)).then_inc(e_land[s], 16)

                    with sp.Fori(0, NE // GRP - 1) as g:
                        for j in range(GRP):
                            load(g, j, g * GRP + (j + 1))
                    last = NE // GRP - 1
                    for j in range(GRP - 1):
                        load(last, j, last * GRP + j + 1)
                    with sp.If(l < DEPTH - 1):
                        after = nc.s_assert_within(l + 1, 1, DEPTH - 1, skip_runtime_bounds_check_because="only before the last layer")
                        sp.wait_ge(S["e_half"], NE)
                        for c in (0, 2):
                            load_ada(sp, after, c)
                        e_take(sp, last, f"gu{GRP - 1}_1")
                        for c in (1, 3):
                            load_ada(sp, after, c)

                @block.tensor
                def _(pe):
                    for b in range(8):
                        pe.sem_inc(e_free[b], 1)
                    ps = open_tile(pe, "rt")
                    pe.wait_ge(S["wr_in"], 16)
                    for t in range(TT):
                        for k in range(KT):
                            ins = nc.tensor.matmul(ps[:, t * NE:(t + 1) * NE], HT[:, k, t * P:(t + 1) * P], WR[:, k, :],
                                                   start=(k == 0), stop=(k == KT - 1))
                    close_tile(ins, "rt")
                    ps = open_tile(pe, "aft")
                    pe.wait_ge(S["aff_ready"], 1)
                    for t in range(TT):
                        ins = nc.tensor.transpose(ps[0:NE, t * P:(t + 1) * P], AFF[:, t, :], ident)
                    close_tile(ins, "aft")
                    ps = open_tile(pe, "post")
                    pe.wait_ge(S["cum_ready"], 1)
                    for t in range(TT):
                        ins = nc.tensor.transpose(ps[:, t * NE:(t + 1) * NE], CUM[0:NE, t * P:(t + 1) * P], ident[0:NE, 0:NE])
                    close_tile(ins, "post")

                    with pe.Fori(0, NE // GRP) as g:
                        pe.wait_ge(S["sel_ready"], g + 1)
                        for k in range(KT):
                            ps = e_open(pe, g, f"xe{k}")
                            for t in (1, 2, 0):
                                c0 = 0 if t else P
                                ins = nc.tensor.matmul(ps[:, c0:c0 + P], XN[:, t, k * P:(k + 1) * P],
                                                       SEL[:, t].rearrange("p e s -> p (e s)"), start=(t != 2), stop=(t != 1))
                            e_close(ins, f"xe{k}")
                        ps = e_open(pe, g, "pg")
                        pe.wait_ge(S["selg_ready"], g + 1)
                        for t in range(TT):
                            ins = nc.tensor.transpose(ps[:, t * P:(t + 1) * P], SELG[:, t].rearrange("p e s -> p (e s)"), ident)
                        e_close(ins, "pg")

                        def gate_up(j):
                            pb = [e_open(pe, g, f"gu{j}_{half}") for half in range(2)]
                            n_landed = 16 * (j + 1)
                            for k in range(KT):
                                if k % 4 == 0:
                                    pe.wait_ge(e_land[k // 4], g * 64 + n_landed)
                                    pe.wait_ge(e_land[2 + k // 4], g * 64 + n_landed)
                                if j == 0:
                                    e_copied(pe, g, f"xe{k}")
                                for half in range(2):
                                    for m in range(2):
                                        w = e_dst(2 * m + k // 4)
                                        ins = nc.tensor.matmul(pb[half][64 * m:64 * m + 64, :], XE[:, k, j, :],
                                                               w[:, k % 4, half * CH:(half + 1) * CH], start=(k == 0), stop=(k == KT - 1))
                                    if k == KT - 1:
                                        e_close(ins, f"gu{j}_{half}")
                                if k == 3:
                                    ins.then_inc(S["e_half"], 1)

                        def down(j):
                            ps = e_open(pe, g, f"at{j}")
                            for k in range(KT):
                                if k % 4 == 0:
                                    e_copied(pe, g, f"gu{j}_{k // 4}")
                                    ins = nc.tensor.matmul(ps[:, k * 64:(k + 1) * 64], AA[0:64, k * P:(k + 1) * P],
                                                           ident[0:64, 0:64], start=True, stop=True)
                                else:
                                    ins = nc.tensor.transpose(ps[:, k * 64:(k + 1) * 64], AA[0:64, k * P:(k + 1) * P],
                                                              ident[0:64, 0:64])
                            e_close(ins, f"at{j}")
                            ps = e_open(pe, g, f"y{j}")
                            e_copied(pe, g, f"at{j}")
                            for k in range(KT):
                                if k % 4 == 0:
                                    pe.wait_ge(e_land[4 + k // 4], g * 64 + 16 * (j + 1))
                                for half in range(2):
                                    ins = nc.tensor.matmul(ps[64 * half:64 * half + 64, :], AT[:, k, :],
                                                           e_dst(4 + k // 4)[:, k % 4, half * CH:(half + 1) * CH],
                                                           start=(k == 0), stop=(k == KT - 1))
                                if k == 3:
                                    ins.then_inc(S["e_down_half"], 1)
                            e_close(ins, f"y{j}")

                        for j in range(GRP):
                            gate_up(j)
                            down(j)
                        e_copied(pe, g, "pg")
                        e_copied(pe, g, f"y{GRP-2}")
                        e_copied(pe, g, f"y{GRP-1}")
                        for i, (t, half) in enumerate((t, h) for t in range(TT) for h in range(2)):
                            ps = e_open(pe, g, f"cm{i}")
                            e_close(nc.tensor.matmul(ps, PG[:, t, :], (YS if t else YP)[:, half * CH:(half + 1) * CH],
                                                     start=True, stop=True), f"cm{i}")

                @block.scalar
                def _(act):
                    ps = take(act, "rt")
                    act.wait_ge(S["router_max"], 1)
                    for t in range(TT):
                        ins = nc.scalar.activation(AFF[:, t, :], ps[:, t * NE:(t + 1) * NE], ACT.Exp, bias=RMX[:, t:t + 1],
                                                   accum_out=RSM[:, t:t + 1])
                    release(ins, "rt")
                    act.wait_ge(S["aff_ready"], 1)
                    nc.scalar.activation(AFFG.rearrange("p g (t e) -> p g t e", t=TT),
                                         AFF.rearrange("p t (g e) -> p g t e", g=NE // GRP), ACT.Copy).then_inc(S["affg_ready"], 1)
                    with act.Fori(0, NE // GRP) as g:
                        for k in range(0, KT, 2):
                            ps = e_take(act, g, f"xe{k}")[:, 0:2 * P].rearrange("p (x e s) -> p x e s", x=2, e=GRP)
                            modulate_act(XE[:, k, :, 0:SLOTS], ps[:, 0], 1, 3, k, 1)
                            e_release(modulate_act(XE[:, k, :, SLOTS:2 * SLOTS], ps[:, 1], 1, 3, k, 0), f"xe{k}")
                        ps = e_take(act, g, "pg")
                        e_release(nc.scalar.activation(PG, ps[:, 0:384].rearrange("p (t n) -> p t n", t=TT), ACT.Copy), "pg")

                        def at_copy(j):
                            ps = e_take(act, g, f"at{j}")
                            e_release(nc.scalar.activation(AT.rearrange("p k s -> p (k s)"), ps, ACT.Copy), f"at{j}")

                        def y_copy(j):
                            ps = e_take(act, g, f"y{j}")
                            rows = slice(32 * j, 32 * j + 32)
                            nc.scalar.activation(YS[rows, CH:D], ps[64:96, :], ACT.Copy)
                            e_release(nc.scalar.activation(YP[rows, CH:D], ps[96:128, :], ACT.Copy), f"y{j}")

                        for j in range(GRP):
                            for half in range(2):
                                ps = e_take(act, g, f"gu{j}_{half}")
                                if j:
                                    e_copied(act, g, f"gu{j-1}_{half}")
                                nc.scalar.activation(TMP[64:128, half * CH:(half + 1) * CH], ps[0:64, :], ACT.Silu).then_inc(
                                    S["silu_done"], 1)
                            at_copy(j)
                            y_copy(j)

                @block.vector
                def _(dve):
                    steps = [0]

                    def step(ins):
                        steps[0] += 1
                        ins.then_inc(S["route_step"], 1)

                    def settle():
                        dve.wait_ge(S["route_step"], steps[0])

                    step(nc.vector.memset(ONE[0:NE, :], 1.0))
                    ps = take(dve, "rt")
                    step(nc.vector.tensor_reduce(RRI[:, 0:TT], ps[:, 0:TT * NE].rearrange("p (t e) -> p t e", t=TT), AX_X, ALU.max))
                    settle()
                    nc.vector.tensor_scalar(RMX[:, 0:TT], RRI[:, 0:TT], -1.0, None, ALU.mult).then_inc(S["router_max"], 1)
                    dve.wait_ge(S["router_max"], 1)
                    copied(dve, "rt")
                    step(nc.vector.reciprocal(RRI[:, 0:TT], RSM[:, 0:TT]))
                    settle()
                    nc.vector.tensor_tensor(AFF, AFF, RRI[:, 0:TT].unsqueeze(2).broadcast_to((P, TT, NE)), ALU.mult).then_inc(
                        S["aff_ready"], 1)
                    ps = take(dve, "aft")
                    step(nc.vector.tensor_copy(WK[0:NE, :], ps[0:NE, 0:TOK]))
                    settle()
                    for lo, hi, cap in ((0, SEQ, CAP_P), (SEQ, TOK, CAP_S)):
                        for r in range(cap // 8):
                            step(nc.vector.max(M8[0:NE, :], WK[0:NE, lo:hi]))
                            settle()
                            step(nc.vector.match_replace(WK[0:NE, lo:hi], M8[0:NE, :], WK[0:NE, lo:hi], -1.0))
                            settle()
                    release(nc.vector.tensor_scalar(MSK[0:NE, :], WK[0:NE, :], 0.0, None, ALU.is_lt), "aft")
                    copied(dve, "aft")
                    for lo, hi in ((0, SEQ), (SEQ, TOK)):
                        step(nc.vector.tensor_tensor_scan(CUM[0:NE, lo:hi], ONE[0:NE, lo:hi], MSK[0:NE, lo:hi], 0.0, ALU.mult, ALU.add))
                    settle()
                    nc.vector.tensor_tensor(CUM[0:NE, :], CUM[0:NE, :], MSK[0:NE, :], ALU.mult).then_inc(S["cum_ready"], 1)
                    ps = take(dve, "post")
                    release(nc.vector.tensor_scalar(POSG.rearrange("p g (t e) -> p g t e", t=TT),
                                                    ps[:, 0:TT * NE].rearrange("p (t g e) -> p g t e", t=TT, g=NE // GRP),
                                                    -1.0, None, ALU.add), "post")
                    copied(dve, "post")
                    dve.wait_ge(S["affg_ready"], 1)
                    with dve.Fori(0, NE // GRP) as g:
                        sel = SEL.rearrange("p t e s -> p (t e) s")
                        n = TT * GRP
                        nc.vector.tensor_tensor(sel, iota.unsqueeze(1).broadcast_to((P, n, SLOTS)),
                                                POSG[:, bass.ds(g, 1), :].rearrange("p o n -> p (o n)").unsqueeze(2).broadcast_to((P, n, SLOTS)),
                                                ALU.is_equal).then_inc(S["sel_ready"], 1)
                        dve.wait_ge(S["sel_ready"], g + 1)
                        nc.vector.tensor_tensor(SELG.rearrange("p t e s -> p (t e) s"), sel,
                                                AFFG[:, bass.ds(g, 1), :].rearrange("p o n -> p (o n)").unsqueeze(2).broadcast_to((P, n, SLOTS)),
                                                ALU.mult).then_inc(S["selg_ready"], 1)
                        for k in range(1, KT, 2):
                            ps = e_take(dve, g, f"xe{k}")[:, 0:2 * P].rearrange("p (x e s) -> p x e s", x=2, e=GRP)
                            modulate_dve(XE[:, k, :, 0:SLOTS], ps[:, 0], 1, 3, k, 1)
                            e_release(modulate_dve(XE[:, k, :, SLOTS:2 * SLOTS], ps[:, 1], 1, 3, k, 0), f"xe{k}")

                        def y_copy(j):
                            ps = e_take(dve, g, f"y{j}")
                            rows = slice(32 * j, 32 * j + 32)
                            nc.vector.tensor_copy(YS[rows, 0:CH], ps[0:32, :])
                            e_release(nc.vector.tensor_copy(YP[rows, 0:CH], ps[32:64, :]), f"y{j}")

                        for j in range(GRP):
                            for half in range(2):
                                ps = e_take(dve, g, f"gu{j}_{half}")
                                dve.wait_ge(S["silu_done"], g * 8 + 2 * j + half + 1)
                                if j and half == 0:
                                    e_take(dve, g, f"at{j-1}")
                                cols = slice(half * CH, (half + 1) * CH)
                                e_release(nc.vector.tensor_tensor(AA[0:64, cols], TMP[64:128, cols], ps[64:128, :], ALU.mult),
                                          f"gu{j}_{half}")
                            y_copy(j)
                        for i, (t, half) in enumerate((t, h) for t in range(TT) for h in range(2)):
                            ps = e_take(dve, g, f"cm{i}")
                            cols = slice(half * CH, (half + 1) * CH)
                            e_release(nc.vector.tensor_tensor(CMB[:, i % 2, :], ps, GROW[:, 1, min(t, 1), cols], ALU.mult), f"cm{i}")
                            e_copied(dve, g, f"cm{i}")
                            nc.vector.tensor_tensor(X[:, t, cols], X[:, t, cols], CMB[:, i % 2, :], ALU.add).then_inc(S["x_done"], 1)
                            dve.wait_ge(S["x_done"], g * 6 + (i + 1))

            nums = [s.num for s in sems]
            assert max(nums) - min(nums) == len(nums) - 1
            nc.all_engine_barrier(sems_to_clear=range(min(nums), max(nums) + 1))

        with nc.Block() as block:
            @block.sync
            def _(sp):
                sp.dma_start(GROW[:, 0, 0, :], A["final_norm_g"].rearrange("(o d) -> o d", o=1).broadcast_to((P, D))).then_inc(
                    once["fin_g_in"], 16)
                sp.wait_ge(once["fin_y"], 1)
                sp.dma_start(A["y_prompt"].rearrange("b s d -> (b s) d"), XN[:, 0, :]).then_inc(once["fin_out"], 16)
                sp.wait_ge(once["fin_y"], TT)
                sp.dma_start(A["y_sample"].rearrange("b (t p) d -> p (b t) d", p=P), XN[:, 1:3, :]).then_inc(once["fin_out"], 16)
                sp.wait_ge(once["fin_out"], 32)

            @block.scalar
            def _(act):
                rms_part_act(act, once["fin_sq"], once["fin_ms"], once["fin_sd"])

            @block.vector
            def _(dve):
                rms_part_dve(dve, once["fin_sq"], once["fin_ms"], once["fin_sd"], once["fin_rs"], once["fin_n"])
                dve.wait_ge(once["fin_g_in"], 16)
                for t in range(TT):
                    dve.wait_ge(once["fin_n"], t + 1)
                    nc.vector.tensor_tensor(XN[:, t, :], XN[:, t, :], GROW[:, 0, 0, :], ALU.mult).then_inc(once["fin_y"], 1)


INS = ["x_prompt", "x_sample", "cache_win_k", "cache_win_v", "cache_nat_k", "cache_nat_v", "c", "c_ctx", "norm1_g", "norm2_g",
       "w_ada", "b_ada", "w_in", "conv_w", "conv_b", "conv_ln_g", "conv_ln_b", "win_sink", "w_branch", "w_out", "w_router",
       "w_e_gate", "w_e_up", "w_e_down", "final_norm_g"]
OUTS = [("y_prompt", (1, SEQ, D)), ("y_sample", (1, DEC, D)), ("new_win_k", (1, DEPTH, 2, SEQ, HD)),
        ("new_win_v", (1, DEPTH, 2, SEQ, HD)), ("new_nat_k", (1, DEPTH, 4, SEQ, HD)), ("new_nat_v", (1, DEPTH, 4, SEQ, HD))]


def bias_grid(na_bias):
    t = np.arange(DEC)
    row, col = t // 64, t % 64
    dr = row[None, :] - row[:, None] + 7
    dc = np.clip(col[None, :] - col[:, None] + 15, 0, 30)
    g = na_bias[:, :, dr, dc]
    return np.ascontiguousarray(g.reshape(DEPTH, 4, 2, P, DEC).transpose(0, 2, 3, 1, 4).reshape(DEPTH, 2, P, 4 * DEC))


def kernel(**inputs):
    import numpy as _np
    import concourse.bacc as _bacc
    from concourse import mybir as _mybir
    from concourse.bass_utils import run_bass_kernel_spmd as _run

    nc = _bacc.Bacc("TRN2", target_bir_lowering=False, num_devices=1)
    arrays, A = {}, {}
    data = {n: _np.asarray(inputs[n]) for n in INS}
    data["na_grid"] = bias_grid(_np.asarray(inputs["na_bias"]))
    data["const"] = constants()
    for name, a in data.items():
        a = _np.ascontiguousarray(a)
        arrays[f"in_{name}"] = a
        A[name] = nc.dram_tensor(f"in_{name}", a.shape, _mybir.dt.from_np(a.dtype), kind="ExternalInput").ap()
    for name, shape in OUTS:
        A[name] = nc.dram_tensor(f"out_{name}", shape, F32, kind="ExternalOutput").ap()
    build(nc, A)
    r = _run(nc, [arrays], core_ids=[0])
    return tuple(r.results[0][f"out_{name}"] for name, _ in OUTS)
```

```python
from contextlib import ExitStack

import numpy as np

import concourse.bass as bass
from concourse import mybir

F32 = mybir.dt.float32
F32R = mybir.dt.float32r
ALU = mybir.AluOpType
ACT = mybir.ActivationFunctionType
AX_X = mybir.AxisListType.X

P = 128
D = 1024
KT = D // P
SEQ, DEC = 128, 256
TOK = SEQ + DEC
TT = TOK // P
DEPTH = 2
BW = 256
HD = 64
CONV_K = 31
NE, FF = 16, 1024
CAP_P, CAP_S = 2 * SEQ // NE, 2 * DEC // NE
SLOTS = 32
GRP = 4
EPS = 1e-6
NEG = -1e30
SCALE = HD ** -0.5
CH = 512
NADA = 6 * D // CH
PADC = CONV_K // 2
UW = PADC + SEQ + 2 * PADC + DEC + PADC
AW = UW - CONV_K + 1
USAMP = PADC + SEQ + 2 * PADC
NSLOT = 6
ARENA = 16000

CONST_COLS = dict(ident=128, esum=256, cos=256, sin=256, rot=128, winmask=512, iota=32,
                  namask=512, dft_s=1024, dft_p=256, dftc=256)
FIRST = 384
HELD = 1568


def const_at(name):
    at = 0
    for n, w in CONST_COLS.items():
        if n == name:
            return at, at + w
        at += w


def constants():
    c = np.zeros((P, sum(CONST_COLS.values())), np.float32)

    def put(name, a):
        lo, hi = const_at(name)
        c[:, lo:hi] = np.asarray(a, np.float64).reshape(P, hi - lo)

    put("ident", np.eye(P))

    def dft(n):
        k = np.outer(np.arange(n), np.arange(n)) % n
        return np.cos(2 * np.pi * k / n), np.sin(2 * np.pi * k / n)

    cs, ss = dft(DEC)
    both = np.concatenate([cs, ss], 1) / np.sqrt(DEC)
    put("dft_s", both.reshape(2, P, 2 * DEC).transpose(1, 0, 2))
    cp, sp = dft(SEQ)
    put("dft_p", np.concatenate([cp, sp], 1) / np.sqrt(SEQ))
    cc, sc = dft(HD)
    eye2 = np.eye(2)
    put("dftc", np.concatenate([np.kron(eye2, cc), -np.kron(eye2, sc)], 1) / np.sqrt(HD))
    t = np.arange(DEC)
    row, col = t // 64, t % 64
    d = np.arange(P) % HD
    freqs = (1.0 / (np.float32(10000.0) ** (np.arange(16, dtype=np.float32) / np.float32(16)))).astype(np.float32)
    pos = np.where((d // 32 == 0)[:, None], row[None], col[None]).astype(np.float32)
    ang = pos * freqs[d % 16][:, None]
    put("cos", np.cos(ang))
    put("sin", np.sin(ang))
    r = np.zeros((P, P))
    for m in range(P):
        if m % 32 < 16:
            r[m + 16, m] = -1.0
        else:
            r[m - 16, m] = 1.0
    put("rot", r)
    q, k = np.arange(DEC)[:, None], np.arange(DEC)[None]
    win = np.where(np.abs(k - q) <= 128, 0.0, NEG)
    put("winmask", win.reshape(2, P, DEC).transpose(1, 0, 2))
    start = np.clip(q % 64 - 8, 0, 48)
    na = np.where((k % 64 >= start) & (k % 64 < start + 16), 0.0, NEG)
    put("namask", na.reshape(2, P, DEC).transpose(1, 0, 2))
    put("iota", np.tile(np.arange(SLOTS), (P, 1)))
    e = np.zeros((P, 2, P))
    for i in range(2):
        e[i::32, i, :] = 1.0
    put("esum", e)
    return c


class BankTurns:

    def __init__(self):
        self.at, self.turns, self.copies = {}, [0] * 8, [0] * 8

    def add(self, name, bank, copies=1):
        self.at[name] = (bank, self.turns[bank], self.copies[bank], copies)
        self.turns[bank] += 1
        self.copies[bank] += copies


def build(nc, A):
    ctx = ExitStack()
    with ctx:
        def sb(name, shape):
            return ctx.enter_context(nc.sbuf_tensor(name, shape, F32))

        sems = []

        def sem(name):
            s = ctx.enter_context(nc.semaphore(name))
            sems.append(s)
            return s

        once = {n: ctx.enter_context(nc.semaphore(n)) for n in
                ("x_in", "const_in", "prm_in", "ada_in0", "ada_in1", "ada_in2", "ada_in3", "cond_in", "cond_t", "cond_zero", "cond_ready",
                 "fin_g_in", "fin_sq", "fin_ms", "fin_sd", "fin_rs", "fin_y", "fin_out")}

        starts = {}

        def slab(name, shape):
            t = sb(name, shape)
            starts[name] = nc.sbuf_base - 4 * int(np.prod(shape[1:]))
            return t

        def over(name, host, word, words):
            return nc.alloc_sbuf_tensor_at(name, [P, words], F32R, offset=starts[host] + 4 * word)

        ring = slab("ring", [P, NSLOT, KT // 2 * D])
        X = sb("X", [P, TT, D])
        XN = slab("XN", [P, TT, D])
        C = sb("C", [P, HELD])
        assert const_at("iota")[1] == HELD and const_at("esum")[1] == FIRST
        GROW = sb("GROW", [P, 2, 2, D])
        condT = sb("condT", [P, KT, 32])
        MOD = sb("MOD", [P, 48, 2])
        SC = sb("SC", [P, 2, KT, 2])
        PRM = sb("PRM", [P, 132])
        SS = sb("SS", [P, 4])
        MS = sb("MS", [P, 4])
        SD = sb("SD", [P, 4])
        RS = sb("RS", [P, 4])
        WR = sb("WR", [P, KT, NE])
        arena = slab("arena", [P, ARENA])
        psum = ctx.enter_context(nc.psum_tensor("psum", [P, 8, 512], F32))

        def cst(name):
            lo, hi = const_at(name)
            return C[:, lo:hi]

        ident = cst("ident")
        cosT, sinT, rot = cst("cos"), cst("sin"), cst("rot")
        winmask = cst("winmask").rearrange("p (q n) -> p q n", q=2)
        iota = cst("iota")
        esum = cst("esum").rearrange("p (i n) -> p i n", i=2)

        cursor = [0]

        def part(n, base=None):
            lo = cursor[0] if base is None else base
            if base is None:
                cursor[0] += n
            return arena[:, lo:lo + n]

        HT = part(KT * TOK).rearrange("p (k t) -> p k t", k=KT)
        part(KT * TOK)
        HTH = over("HTH", "arena", 0, KT * TOK)[:, :].rearrange("p (k t) -> p k t", k=KT)
        HTL = over("HTL", "arena", KT * TOK, KT * TOK)[:, :].rearrange("p (k t) -> p k t", k=KT)
        mrg_at = cursor[0]
        MRG = part(KT * TOK).rearrange("p (k t) -> p k t", k=KT)
        ADAS = part(2 * CH, mrg_at + 768).rearrange("p (b n) -> p b n", b=2)
        ZF = part(2 * TOK, mrg_at + 1792).rearrange("p (c t) -> p c t", c=2)
        VT = part(3 * TOK, mrg_at + 1792).rearrange("p (c t) -> p c t", c=3)
        U = part(2 * UW).rearrange("p (c n) -> p c n", c=2)
        ACC = part(2 * AW).rearrange("p (c n) -> p c n", c=2)
        branch_weights_at = cursor[0] - 2 * AW - 2 * UW + 2 * CH
        LATE = part(2 * CH, cursor[0] - 2 * AW - 2 * UW).rearrange("p (b n) -> p b n", b=2)

        def adas(c):
            return ADAS[:, c // 2, :] if c < 4 else LATE[:, c % 2, :]

        CT = part(3 * P).rearrange("p (c n) -> p c n", c=3)
        kc_at = cursor[0]
        KC = part(6 * HD).rearrange("p (h d) -> p h d", h=6)
        KO = part(384)
        GP = part(2 * TOK, kc_at).rearrange("p (b n) -> p b n", b=2)
        VC = part(6 * HD).rearrange("p (h d) -> p h d", h=6)
        ZV = part(TT * 384).rearrange("p (t c) -> p t c", t=TT)
        SIG = part(2 * TOK).rearrange("p (b n) -> p b n", b=2)
        PTB = part(2 * 384).rearrange("p (b n) -> p b n", b=2)
        WOT = part(2 * CH, cursor[0] - 4 * TOK).rearrange("p (b n) -> p b n", b=2)
        pr_at = cursor[0]
        PR = part(2 * P).rearrange("p (b n) -> p b n", b=2)
        BN = part(TT * 6).rearrange("p (t n) -> p t n", t=TT)
        MV = part(TT * 2).rearrange("p (t n) -> p t n", t=TT)
        LSD = part(TT)
        LRS = part(TT)
        SINK = part(4)
        MX = part(4)
        NM = part(4)
        DS = part(4)
        ES = part(4)
        SM = part(4)
        RI = part(4)
        assert branch_weights_at + 4 * P <= kc_at
        BWH = over("BWH", "arena", branch_weights_at, 4 * P)[:, :].rearrange("p (b c n) -> p b c n", b=2, c=2)
        BWL = over("BWL", "arena", ARENA - 4 * P, 4 * P)[:, :].rearrange("p (b c n) -> p b c n", b=2, c=2)
        part(4 * P)
        assert cursor[0] <= ARENA, cursor[0]
        tmp = ring[:, 4:6, :].rearrange("p s n -> p (s n)")
        QC = tmp[:, 0:768].rearrange("p (a t) -> p a t", a=2)
        KTC = tmp[:, 768:1152]
        DQ = tmp[:, 1152:1920].rearrange("p (a t) -> p a t", a=2)
        DK = tmp[:, 1920:2688].rearrange("p (a t) -> p a t", a=2)
        NAB = tmp[:, 2688:4736].rearrange("p (q h n) -> p q h n", q=2, h=4)
        SCB = tmp[:, 4736:6272].rearrange("p (h n) -> p h n", h=4)
        FG = tmp[:, 6272:7808].rearrange("p (t c x n) -> p t c x n", t=TT, c=2, x=2)
        LNX = tmp[:, 6272:7040].rearrange("p (t c) -> p t c", t=TT)
        ROTT = tmp[:, 7808:8064]
        NAM = tmp[:, 1152:1664]
        namask = NAM.rearrange("p (q n) -> p q n", q=2)
        DFT = tmp[:, 4736:6272]
        dft_s = DFT[:, 0:1024].rearrange("p (k n) -> p k n", k=2)
        dft_p = DFT[:, 1024:1280]
        dftc = DFT[:, 1280:1536]
        WSR = over("WSR", "ring", 3 * 4 * D, 4 * D)[:, :].rearrange("p (x b k n) -> p x b k n", x=2, b=2, k=KT)
        BRT = XN[:, :, :].rearrange("p t n -> p (t n)").rearrange("p (b c t) -> p b c t", b=4, c=2)
        BRH = over("BRH", "ring", 4 * 4 * D + 6272, 4 * TOK)[:, :].rearrange("p (b c t) -> p b c t", b=2, c=2)
        BRL = over("BRL", "XN", 0, 8 * TOK)[:, :].rearrange("p (b c t) -> p b c t", b=4, c=2)
        cursor[0] = 0
        XE = part(KT * GRP * 64).rearrange("p (k e s) -> p k e s", k=KT, e=GRP)
        SEL = part(TT * P).rearrange("p (t e s) -> p t e s", t=TT, e=GRP)
        SELG = part(TT * P).rearrange("p (t e s) -> p t e s", t=TT, e=GRP)
        PG = part(TT * P).rearrange("p (t n) -> p t n", t=TT)
        TMP = part(FF)
        AA = part(FF)
        AT = part(KT * 64).rearrange("p (k s) -> p k s", k=KT)
        YS = part(D)
        YP = part(D)
        CMB = part(2 * CH).rearrange("p (b n) -> p b n", b=2)
        AFF = part(TT * NE).rearrange("p (t e) -> p t e", t=TT)
        POSG = part(TT * (NE + GRP)).rearrange("p (g n) -> p g n", g=NE // GRP + 1)
        AFFG = part(TT * (NE + GRP)).rearrange("p (g n) -> p g n", g=NE // GRP + 1)
        WK = part(TOK)
        MSK = part(TOK)
        ONE = part(TOK)
        CUM = part(TOK)
        M8 = part(8)
        RMX = part(4)
        RSM = part(4)
        RRI = part(4)
        SEVENTH = part(4 * D)
        assert cursor[0] <= pr_at, cursor[0]

        land = [sem(f"land{s}") for s in range(NSLOT)]
        e_land = [sem(f"e_land{s}") for s in range(NSLOT)]
        e_land.append(sem(f"e_land{NSLOT}"))
        full = [sem(f"full{b}") for b in range(8)]
        free = [sem(f"free{b}") for b in range(8)]
        e_full = [sem(f"e_full{b}") for b in range(8)]
        e_free = [sem(f"e_free{b}") for b in range(8)]
        names = ("x_mixed b_high b_rest br_high br_rest rest_in grow_in sink_in cache_in nab_in nab_ready u_zero sq_done ms_ready sd_ready rs_ready xn_ready "
                 "sc_ready dve_step route_step conv_step rope_ready scores_done scores_read nmax_ready exps_done p_ready "
                 "pv0 pv1 high_act rest_pool high_dve rest_dve w_high w_rest mask_in dft_in gate_add out_kv n2_sq n2_ms n2_sd n2_rs n2_xn wr_in router_max router_exp aff_ready affg_ready "
                 "cum_ready sel_ready selg_ready e_half e_down_half silu_done x_done").split()
        S = {n: sem(n) for n in names}

        GATE_ORDER = [1, 0, 2, 3]
        ADA_AT = {0: 4, 4: 5, 8: 6, 11: 7, 20: 8, 24: 9, 28: 10, 30: 11}

        order = ["ada0", "ada1", "ada3", "ada2", "w0", "w1", "w2", "w3", "w6", "wb01", "ada4", "w7", "ada5", "w4", "ada6",
                 "w5", "ada7", "w8", "wb23", "w9", "ada8", "w10", "ada9", "w11", "ada10", "ada11", "wo0", "wo1"]
        done_at = {n: i - 8 for i, n in enumerate(order[:8])}
        done_at.update(wb01=15, wb23=31, wo0=32, wo1=32)
        done_at.update({f"w{4 + 2 * n + h}": 4 * (2 * GATE_ORDER.index(n) + h) + 1.6 for n in range(4) for h in range(2)})
        done_at.update({f"ada{c}": idx + 0.5 for idx, c in ADA_AT.items()})
        unit_at, used, before, latest, units = {}, [0] * NSLOT, {}, {}, []
        for name in order:
            s = min(range(4 if name == "ada2" else 3), key=lambda x: done_at[latest[x]] if x in latest else x - 100)
            units.append((name, s))
            unit_at[name] = (s, used[s])
            before[name] = latest.get(s)
            latest[s] = name
            used[s] += name not in order[:4]

        def slot(name, cols):
            return ring[:, unit_at[name][0], :].rearrange("p (k n) -> p k n", n=cols)

        parts = [("gb0", "w0", 256), ("ga0", "w0", 0), ("gb1", "w0", 384), ("ga1", "w0", 128),
                 ("zf0", "w1", 0), ("zf1", "w1", 128), ("cq0", "w1", 256), ("cq1", "w1", 384),
                 ("ck", "w2", 0), ("dq0", "w2", 256), ("dq1", "w2", 384), ("zcv", "w2", 128),
                 ("dk0", "w3", 0), ("dk1", "w3", 128), ("dv0", "w3", 256), ("dv1", "w3", 384)]
        EARLY = len(parts)
        for n in GATE_ORDER:
            for k in range(KT):
                parts.append((f"g{n}_{k}", f"w{4 + 2 * n + k // 4}", (k % 4) * P))
        part_of = {tile: i for i, (tile, _, _) in enumerate(parts)}

        ln_var_step = [2 + 3 + 3 + 3 + 1]

        T = BankTurns()
        seq = {"a": 0, "b": 0}

        def tile_a(name):
            T.add(name, seq["a"] % 4)
            seq["a"] += 1

        def tile_b(name):
            T.add(name, 4 + seq["b"] % 4)
            seq["b"] += 1

        for half in range(2):
            for c in (half, half + 2):
                tile_a(f"ada{c}")
                tile_b(f"md{c}")
            if half == 0:
                tile_b("prm")
            for k in range(4 * half, 4 * half + 4):
                tile_a(f"xt{k}")
        for n, _, _ in parts[:EARLY]:
            tile_a(n)
        for n in ("fa0", "fa1", "fa2", "ctxT", "fo0", "fo1", "ko", "vt0", "vt1", "vt2", "rot0", "rot1", "rotk"):
            tile_b(n)
        for n in ("lt0", "lt1", "lt2"):
            tile_b(n)
        GATE_CHUNKS = (4, 5, 10, 11)

        def ada_small_tiles(c):
            for n in ([f"gr{c}_0", f"gr{c}_1"] if c in GATE_CHUNKS else [f"md{c}"]):
                tile_a(n)

        ATT = [("c", 0), ("c", 1), ("c", None), ("d", 0), ("d", 1), ("d", None)]
        OUT_OF = {"c": ("o0", "o1", "o2"), "d": ("o3", "o4", "o5")}

        def scores_at(idx):
            return (idx - 1) // 3 if idx % 3 == 1 and (idx - 1) // 3 < len(ATT) else None

        def out_at(idx):
            return (idx - 4) // 3 if idx % 3 == 1 and 0 <= (idx - 4) // 3 < len(ATT) else None

        for n in GATE_ORDER:
            for k in range(KT):
                idx = GATE_ORDER.index(n) * KT + k
                g = out_at(idx)
                if g is not None:
                    for h in range(4):
                        tile_b(f"pt{g}_{h}")
                tile_a(f"g{n}_{k}")
                if g is not None:
                    tile_a(f"o{g}")
                tile_a(f"p{n}_{k}")
                if idx == 0:
                    tile_b("lb0")
                    tile_b("lb1")
                    while seq["b"] % 4:
                        seq["b"] += 1
                if idx in ADA_AT:
                    tile_a(f"ada{ADA_AT[idx]}")
                if idx - 1 in ADA_AT:
                    ada_small_tiles(ADA_AT[idx - 1])
        for t in range(TT):
            for half in range(2):
                tile_a(f"wo{t}_{half}")

        for t in range(TT):
            for j in range(2):
                tile_b(f"y{t}_{j}")
        tile_a("rt")
        tile_b("aft")
        tile_b("post")

        def open_tile(pe, name):
            b, _, copies_before, _ = T.at[name]
            if copies_before:
                pe.wait_ge(free[b], copies_before)
            return psum[:, b, :]

        def close_tile(ins, name):
            ins.then_inc(full[T.at[name][0]], 1)

        def take(eng, name):
            b, n, _, _ = T.at[name]
            eng.wait_ge(full[b], n + 1)
            return psum[:, b, :]

        def release(ins, name):
            ins.then_inc(free[T.at[name][0]], 1)

        def copied(eng, name):
            b, _, copies_before, copies = T.at[name]
            eng.wait_ge(free[b], copies_before + copies)

        last_tile = {f"ada{c}": f"ada{c}" for c in range(NADA)}
        last_tile.update(wo0="wo2_1", wo1="wo2_1")
        last_part = {unit: i for i, (_, unit, _) in enumerate(parts)}

        def used_up(eng, name):
            if name in last_part:
                eng.wait_ge(S["w_rest"], last_part[name] + 1)
            elif name in ("wb01", "wb23"):
                eng.wait_ge(S["b_rest"], 2 * KT if name == "wb01" else 4 * KT)
            else:
                take(eng, last_tile[name])

        def landed(eng, name):
            s, n = unit_at[name]
            eng.wait_ge(land[s], 16 * (n + 1))

        def part_src(i):
            _, unit, c0 = parts[i]
            return slot(unit, CH)[:, :, c0:c0 + P]

        def branch_part_src(idx):
            n, k = GATE_ORDER[idx // KT], idx % KT
            return slot("wb01" if n < 2 else "wb23", D)[:, 2 * (n % 2):2 * (n % 2) + 2, k * P:(k + 1) * P]

        SPLIT_AFTER = (-1, 1, 11, 20)

        def w_unit(l, name):
            kind = name[:3]
            if kind == "ada":
                c = int(name[3:])
                return A["w_ada"][bass.ds(l, 1), :, c * CH:(c + 1) * CH].rearrange("o (k p) n -> p (o k) n", p=P)
            if name[:2] == "wb":
                b = int(name[2])
                return A["w_branch"][bass.ds(l, 1), b:b + 2].rearrange("o b (c p) n -> p (o b c) n", p=P)
            if name[:2] == "wo":
                h = int(name[2])
                return A["w_out"][bass.ds(l, 1), h * 512:(h + 1) * 512, :].rearrange("o (k p) n -> p (o k) n", p=P)
            c = int(name[1:])
            return A["w_in"][bass.ds(l, 1), :, c * CH:(c + 1) * CH].rearrange("o (k p) n -> p (o k) n", p=P)

        E_SRC = (("w_e_gate", 0, 0), ("w_e_up", 0, 2), ("w_e_gate", 1, 1), ("w_e_up", 1, 3), ("w_e_down", 0, 4), ("w_e_down", 1, 5))

        def e_unit(l, e, name, half):
            return A[name][bass.ds(l, 1), bass.ds(e, 1), half * 512:(half + 1) * 512, :].rearrange(
                "o e (k p) n -> p (o e k) n", p=P)

        def down_slot(j):
            return NSLOT - 1 + j % 2

        def e_dst(s):
            if s == NSLOT:
                return SEVENTH.rearrange("p (k n) -> p k n", n=D)
            return ring[:, s, :].rearrange("p (k n) -> p k n", n=D)

        E = BankTurns()
        for k in range(KT):
            E.add(f"xe{k}", 6 + k % 2)
        E.add("pg", 7)
        for j in range(GRP):
            for half in range(2):
                E.add(f"gu{j}_{half}", 2 * (j % 2) + half)
            E.add(f"at{j}", 6)
            E.add(f"y{j}", 4 + j % 2, 2)
        for i in range(6):
            E.add(f"cm{i}", i)

        def e_open(pe, g, name):
            b, _, copies_before, _ = E.at[name]
            pe.wait_ge(e_free[b], g * E.copies[b] + copies_before + 1)
            return psum[:, b, :]

        def e_close(ins, name):
            ins.then_inc(e_full[E.at[name][0]], 1)

        def e_take(eng, g, name):
            b, n, _, _ = E.at[name]
            eng.wait_ge(e_full[b], g * E.turns[b] + n + 1)
            return psum[:, b, :]

        def e_release(ins, name):
            ins.then_inc(e_free[E.at[name][0]], 1)

        def e_copied(eng, g, name):
            b, _, copies_before, copies = E.at[name]
            eng.wait_ge(e_free[b], g * E.copies[b] + copies_before + copies + 1)

        def modulate_act(dst, src, which, sec, k, i):
            return nc.scalar.activation(dst, src, ACT.Identity, scale=SC[:, which, k, i:i + 1], bias=MOD[:, sec * KT + k, i:i + 1])

        def modulate_dve(dst, src, which, sec, k, i):
            return nc.vector.tensor_scalar(dst, src, SC[:, which, k, i:i + 1], MOD[:, sec * KT + k, i:i + 1], ALU.mult, ALU.add)

        def rms_part_act(act, sq_sem, ms_sem, sd_sem):
            for t in range(TT):
                nc.scalar.activation(XN[:, t, :], X[:, t, :], ACT.Square, accum_out=SS[:, t:t + 1]).then_inc(sq_sem, 1)
            act.wait_ge(ms_sem, 1)
            nc.scalar.activation(SD[:, 0:TT], MS[:, 0:TT], ACT.Sqrt).then_inc(sd_sem, 1)

        def rms_part_dve(dve, sq_sem, ms_sem, sd_sem, rs_sem, xn_sem):
            dve.wait_ge(sq_sem, TT)
            nc.vector.tensor_scalar(MS[:, 0:TT], SS[:, 0:TT], 1.0 / D, EPS, ALU.mult, ALU.add).then_inc(ms_sem, 1)
            dve.wait_ge(sd_sem, 1)
            nc.vector.reciprocal(RS[:, 0:TT], SD[:, 0:TT]).then_inc(rs_sem, 1)
            dve.wait_ge(rs_sem, 1)
            for t in range(TT):
                nc.vector.tensor_scalar(XN[:, t, :], X[:, t, :], RS[:, t:t + 1], None, ALU.mult).then_inc(xn_sem, 1)

        def load_ada(eng, layer, c):
            eng.dma_start(slot(f"ada{c}", CH), w_unit(layer, f"ada{c}")).then_inc(once[f"ada_in{c}"], 16)

        def load_parameters(eng, layer):
            def rows(name):
                return A[name][bass.ds(layer, 1)]

            for dst, src in ((PR[0:48, 0, :], rows("b_ada").rearrange("o (r p) -> (o r) p", p=P)),
                             (PR[48:56, 0, :], rows("norm1_g").rearrange("o (r p) -> (o r) p", p=P)),
                             (PR[56:64, 0, :], rows("norm2_g").rearrange("o (r p) -> (o r) p", p=P)),
                             (PR[0:62, 1, :], rows("conv_w").rearrange("o k (c p) -> (o k c) p", p=P)),
                             (PR[62:64, 1, :], rows("conv_b").rearrange("o (r p) -> (o r) p", p=P)),
                             (PR[64:66, 1, :], rows("conv_ln_g").rearrange("o (r p) -> (o r) p", p=P)),
                             (PR[66:68, 1, :], rows("conv_ln_b").rearrange("o (r p) -> (o r) p", p=P))):
                eng.dma_start(dst, src).then_inc(once["prm_in"], 16)

        with nc.Block() as block:
            @block.sync
            def _(sp):
                sp.dma_start(XN[0:8, 0, 0:P], A["c_ctx"].rearrange("(k p) -> k p", p=P)).then_inc(once["cond_in"], 16)
                sp.dma_start(XN[8:16, 0, 0:P], A["c"].rearrange("b (k p) -> (b k) p", p=P)).then_inc(once["cond_in"], 16)
                sp.dma_start(C[:, 0:FIRST], A["const"][:, 0:FIRST]).then_inc(once["const_in"], 16)
                load_parameters(sp, 0)
                load_ada(sp, 0, 0)
                sp.dma_start(X[:, 0, :], A["x_prompt"].rearrange("b s d -> (b s) d")).then_inc(once["x_in"], 16)
                sp.dma_start(X[:, 1:3, :], A["x_sample"].rearrange("b (t p) d -> p (b t) d", p=P)).then_inc(once["x_in"], 16)
                for c in (2, 1, 3):
                    load_ada(sp, 0, c)

            @block.vector
            def _(dve):
                nc.vector.memset(condT[:, :, :], 0.0).then_inc(once["cond_zero"], 1)

            @block.tensor
            def _(pe):
                pe.wait_ge(once["cond_in"], 32)
                pe.wait_ge(once["const_in"], 16)
                nc.tensor.transpose(psum[:, 0, 0:16], XN[0:16, 0, 0:P], ident[0:16, 0:16]).then_inc(once["cond_t"], 1)

            @block.scalar
            def _(act):
                act.wait_ge(once["cond_zero"], 1)
                act.wait_ge(once["cond_t"], 1)
                nc.scalar.activation(condT[:, :, 0:2], psum[:, 0, 0:16].rearrange("p (i k) -> p k i", i=2),
                                     ACT.Silu).then_inc(once["cond_ready"], 1)
                act.wait_ge(once["cond_ready"], 1)

        with nc.Fori(0, DEPTH) as l:
            with nc.Block() as block:
                @block.sync
                def _(sp):
                    def caches():
                        sp.dma_start(SINK, A["win_sink"][bass.ds(l, 1)].broadcast_to((P, 4))).then_inc(S["sink_in"], 16)
                        for name, h0, nh in (("cache_win", 0, 2), ("cache_nat", 2, 4)):
                            for kv, dst in (("k", KC), ("v", VC)):
                                sp.dma_start(dst[:, h0:h0 + nh, :], A[f"{name}_{kv}"][:, bass.ds(l, 1)].rearrange(
                                    "b o h t d -> t (b o h) d")).then_inc(S["cache_in"], 16)

                    def late_constants():
                        sp.dma_start(C[:, FIRST:HELD], A["const"][:, FIRST:HELD]).then_inc(S["rest_in"], 16)
                        sp.dma_start(DFT, A["const"][:, const_at("dft_s")[0]:]).then_inc(S["dft_in"], 16)
                        sp.dma_start(NAM, A["const"][:, const_at("namask")[0]:const_at("namask")[1]]).then_inc(S["mask_in"], 16)
                        sp.dma_start(NAB[:, :, :, :].rearrange("p q h n -> p q (h n)"),
                                     A["na_grid"][bass.ds(l, 1)].rearrange("o q p n -> p (o q) n")).then_inc(S["nab_in"], 16)

                    def gate_biases():
                        sp.dma_start(WR[:, :, :], A["w_router"][bass.ds(l, 1)].rearrange("o (k p) e -> p (o k) e", p=P)).then_inc(
                            S["wr_in"], 16)
                        for gate, sec in ((0, 2), (1, 5)):
                            for i in range(2):
                                sp.dma_start(GROW[:, gate, i, :], A["b_ada"][bass.ds(l, 1), sec * D:(sec + 1) * D].broadcast_to(
                                    (P, D))).then_inc(S["grow_in"], 16)

                    def prompt_kv():
                        copied(sp, "ko")
                        copied(sp, "vt0")
                        for name, src, h0, nh in (("new_win_k", KO, 0, 2), ("new_nat_k", KO, 2, 4),
                                                  ("new_win_v", ZV[:, 0, :], 0, 2), ("new_nat_v", ZV[:, 0, :], 2, 4)):
                            sp.dma_start(A[name][:, bass.ds(l, 1)].rearrange("b o h t d -> t (b o h) d"),
                                         src[:, h0 * HD:(h0 + nh) * HD].rearrange("p (h d) -> p h d", d=HD)).then_inc(S["out_kv"], 16)

                    for name, s in units[4:]:
                        cols = D if name[:2] in ("wb", "wo") else CH
                        used_up(sp, before[name])
                        sp.dma_start(slot(name, cols), w_unit(l, name)).then_inc(land[s], 16)
                        if name == "w1":
                            late_constants()
                            caches()
                        elif name == "w3":
                            gate_biases()
                        elif name == "w7":
                            prompt_kv()
                    sp.wait_ge(S["out_kv"], 64)
                    held_to_the_end = [unit_at[n][0] for n in ("wo0", "wo1")]
                    for name, half, s in sorted(E_SRC, key=lambda x: (x[2] in held_to_the_end, -x[2])):
                        if s == 3:
                            take(sp, parts[-1][0])
                        elif s in latest:
                            used_up(sp, latest[s])
                        elif s == NSLOT - 2:
                            copied(sp, f"o{len(ATT) - 1}")
                        elif s == NSLOT - 1:
                            take(sp, f"p{GATE_ORDER[-1]}_{KT - 1}")
                        sp.dma_start(e_dst(s), e_unit(l, 0, name, half)).then_inc(e_land[s], 16)

                @block.gpsimd
                def _(pool):
                    nc.gpsimd.memset(U[:, :, :], 0.0).then_inc(S["u_zero"], 1)
                    def rest_of_input(k):
                        pool.wait_ge(S["high_act"], k // 2 + 1)
                        nc.gpsimd.tensor_tensor(HTL[:, k, :], SIG[:, (k // 2) % 2, :], HTH[:, k, :].bitcast(F32),
                                                ALU.subtract).then_inc(S["rest_pool"], 1)

                    def rest_of_branch_part(idx):
                        pool.wait_ge(S["b_high"], idx + 1)
                        nc.gpsimd.tensor_tensor(BWL[:, idx % 2], branch_part_src(idx), BWH[:, idx % 2].bitcast(F32),
                                                ALU.subtract).then_inc(S["b_rest"], 1)

                    def rest_of_branch(q):
                        n = GATE_ORDER[q]
                        pool.wait_ge(S["br_high"], q + 1)
                        nc.gpsimd.tensor_tensor(BRL[:, n], BRT[:, n], BRH[:, (q + 1) % 2].bitcast(F32),
                                                ALU.subtract).then_inc(S["br_rest"], 1)

                    rest_of_input(0)
                    rest_of_input(2)
                    for i in range(len(parts)):
                        pool.wait_ge(S["w_high"], i + 1)
                        nc.gpsimd.tensor_tensor(WSR[:, 1, i % 2], part_src(i), WSR[:, 0, i % 2].bitcast(F32),
                                                ALU.subtract).then_inc(S["w_rest"], 1)
                        if i - EARLY - 1 >= 0:
                            rest_of_branch_part(i - EARLY - 1)
                        if i == EARLY - 1 or i - EARLY - 2 in SPLIT_AFTER[1:]:
                            rest_of_branch(0 if i == EARLY - 1 else SPLIT_AFTER.index(i - EARLY - 2))
                        if i == 0:
                            rest_of_input(4)
                            rest_of_input(6)
                        if i == 9:
                            pool.wait_ge(S["nab_in"], 16)
                            pool.wait_ge(S["mask_in"], 16)
                            nc.gpsimd.tensor_tensor(NAB, NAB, namask.unsqueeze(2).broadcast_to((P, 2, 4, DEC)),
                                                    ALU.add).then_inc(S["nab_ready"], 1)
                    rest_of_branch_part(4 * KT - 1)

                @block.tensor
                def _(pe):
                    def ada_main(c):
                        name = f"ada{c}"
                        ps = open_tile(pe, name)
                        if c < 4:
                            pe.wait_ge(once[f"ada_in{c}"], l * 16 + 16)
                        else:
                            landed(pe, name)
                        w = slot(name, CH)
                        for k2 in range(2):
                            for j in range(4):
                                ins = nc.tensor.matmul(ps[32 * j:32 * j + 32, :], condT[:, 4 * k2 + j, :], w[:, 4 * k2 + j, :],
                                                       start=(k2 == 0), stop=(k2 == 1))
                        close_tile(ins, name)

                    def ada_mod(c):
                        ps = open_tile(pe, f"md{c}")
                        copied(pe, f"ada{c}")
                        for s in range(4):
                            ins = nc.tensor.matmul(ps[:, 2 * s:2 * s + 2], adas(c)[:, s * P:(s + 1) * P], esum[:, :, 0],
                                                   start=True, stop=True)
                        close_tile(ins, f"md{c}")

                    def ada_gate(c):
                        for i in range(2):
                            ps = open_tile(pe, f"gr{c}_{i}")
                            copied(pe, f"ada{c}")
                            ins = nc.tensor.matmul(ps[:, :], esum[:, i, :], adas(c), start=True, stop=True)
                            close_tile(ins, f"gr{c}_{i}")

                    def ada_small(c):
                        (ada_gate if c in GATE_CHUNKS else ada_mod)(c)

                    for half in range(2):
                        for c in (half, half + 2):
                            ada_main(c)
                        for c in (half, half + 2):
                            ada_mod(c)
                        if half == 0:
                            ps = open_tile(pe, "prm")
                            pe.wait_ge(once["prm_in"], l * 112 + 112)
                            nc.tensor.matmul(ps[:, 0:64], PR[0:64, 0, :], ident[0:64, 0:64], start=True, stop=True)
                            close_tile(nc.tensor.transpose(ps[:, 64:132], PR[0:68, 1, :], ident[0:68, 0:68]), "prm")
                            pe.wait_ge(S["xn_ready"], TT)
                        for k in range(4 * half, 4 * half + 4):
                            ps = open_tile(pe, f"xt{k}")
                            for t in range(TT):
                                ins = nc.tensor.transpose(ps[:, t * P:(t + 1) * P], XN[:, t, k * P:(k + 1) * P], ident)
                            close_tile(ins, f"xt{k}")

                    def zt(tile):
                        i = part_of[tile]
                        ps = open_tile(pe, tile)
                        pe.wait_ge(S["w_rest"], i + 1)
                        for k in range(KT):
                            if i == 0:
                                pe.wait_ge(S["rest_dve" if k % 2 else "rest_pool"], k // 2 + 1)
                            for w, x in ((0, HTH), (0, HTL), (1, HTH)):
                                ins = nc.tensor.matmul(ps[:, 0:TOK], WSR[:, w, i % 2, k, :], x[:, k, :],
                                                       start=(k == 0 and w == 0 and x is HTH), stop=(k == KT - 1 and w == 1))
                        close_tile(ins, tile)

                    for n in ("gb0", "ga0", "gb1", "ga1", "zf0", "zf1", "cq0"):
                        zt(n)
                    pe.wait_ge(S["dft_in"], 16)
                    for c in range(2):
                        copied(pe, f"zf{c}")
                    for t in range(TT):
                        ps = open_tile(pe, f"fa{t}")
                        for c in range(2):
                            ins = nc.tensor.matmul(ps[:, c * 256:(c + 1) * 256], ZF[:, c, t * P:(t + 1) * P], dftc,
                                                   start=True, stop=True)
                        close_tile(ins, f"fa{t}")
                    zt("cq1")
                    ps = open_tile(pe, "ctxT")
                    pe.wait_ge(S["cache_in"], 64)
                    for c in range(3):
                        ins = nc.tensor.transpose(ps[:, c * P:(c + 1) * P],
                                                  KC[:, 2 * c:2 * c + 2, :].rearrange("p h d -> p (h d)"), ident)
                    close_tile(ins, "ctxT")
                    zt("ck")
                    for t in range(TT):
                        copied(pe, f"fa{t}")
                    for c in range(2):
                        ps = open_tile(pe, f"fo{c}")
                        for x in range(2):
                            for t in (1, 2):
                                ins = nc.tensor.matmul(ps[:, P:TOK], FG[:, t, c, x, :], dft_s[:, t - 1, x * DEC:(x + 1) * DEC],
                                                       start=(x == 0 and t == 1), stop=(x == 1 and t == 2))
                        for x in range(2):
                            ins = nc.tensor.matmul(ps[:, 0:P], FG[:, 0, c, x, :], dft_p[:, x * SEQ:(x + 1) * SEQ],
                                                   start=(x == 0), stop=(x == 1))
                        close_tile(ins, f"fo{c}")
                    for n in ("dq0", "dq1", "zcv", "dk0", "dk1", "dv0", "dv1"):
                        zt(n)
                    ps = open_tile(pe, "ko")
                    for n in ("cq0", "cq1", "ck", "dk0", "dk1"):
                        copied(pe, n)
                    for c, src in enumerate((KTC[:, 0:P], DK[:, 0, 0:P], DK[:, 1, 0:P])):
                        ins = nc.tensor.transpose(ps[:, c * P:(c + 1) * P], src, ident)
                    close_tile(ins, "ko")
                    for n in ("zcv", "dv0", "dv1"):
                        copied(pe, n)
                    for t in range(TT):
                        ps = open_tile(pe, f"vt{t}")
                        for c in range(3):
                            ins = nc.tensor.transpose(ps[:, c * P:(c + 1) * P], VT[:, c, t * P:(t + 1) * P], ident)
                        close_tile(ins, f"vt{t}")
                    pe.wait_ge(S["rest_in"], 16)
                    for n, src in (("rot0", QC[:, 0, P:TOK]), ("rot1", QC[:, 1, P:TOK]), ("rotk", KTC[:, P:TOK])):
                        ps = open_tile(pe, n)
                        close_tile(nc.tensor.matmul(ps[:, 0:DEC], rot, src, start=True, stop=True), n)
                    pe.wait_ge(S["conv_step"], 2 * CONV_K)
                    for t in range(TT):
                        ps = open_tile(pe, f"lt{t}")
                        a0 = 0 if t == 0 else USAMP - PADC + (t - 1) * P
                        for c in range(2):
                            ins = nc.tensor.transpose(ps[:, c * P:(c + 1) * P], ACC[:, c, a0:a0 + P], ident)
                        close_tile(ins, f"lt{t}")
                    def normed_back():
                        for t in range(TT):
                            copied(pe, f"lt{t}")
                        for c in range(2):
                            ps = open_tile(pe, f"lb{c}")
                            for t in range(TT):
                                ins = nc.tensor.transpose(ps[:, t * P:(t + 1) * P], LNX[:, t, c * P:(c + 1) * P], ident)
                            close_tile(ins, f"lb{c}")

                    def att_scores(g):
                        br, qt = ATT[g]
                        if g == 0:
                            pe.wait_ge(S["rope_ready"], 3)
                            for n in ("ctxT", "dq0", "dq1", "vt0", "vt1", "vt2"):
                                copied(pe, n)
                        q0 = 0 if qt is None else P + qt * P
                        for h in range(4):
                            b = 4 + h
                            pe.wait_ge(free[b], T.at[f"pt{g}_{h}"][2])
                            if br == "c":
                                r = slice(64 * (h // 2), 64 * (h // 2) + 64)
                                q, kk, ct = QC[r, h % 2, q0:q0 + P], KTC[r, :], CT[r, 0, :]
                            else:
                                r = slice(64 * (h % 2), 64 * (h % 2) + 64)
                                q, kk, ct = DQ[r, h // 2, q0:q0 + P], DK[r, h // 2, :], CT[r, 1 + h // 2, :]
                            if qt is None:
                                ins = nc.tensor.matmul(psum[:, b, 0:P], q, kk[:, 0:P], start=True, stop=True)
                            else:
                                nc.tensor.matmul(psum[:, b, 0:DEC], q, kk[:, P:TOK], start=True, stop=True)
                                ins = nc.tensor.matmul(psum[:, b, DEC:DEC + P], q, ct, start=True, stop=True)
                        ins.then_inc(S["scores_done"], 1)

                    def probs_t(g, h):
                        if h == 0:
                            pe.wait_ge(S["scores_read"], g + 1)
                            pe.wait_ge(S["p_ready"], g + 1)
                        name = f"pt{g}_{h}"
                        b = T.at[name][0]
                        for j in range(1 if ATT[g][1] is None else 3):
                            ins = nc.tensor.transpose(psum[:, b, j * P:(j + 1) * P], SCB[:, h, j * P:(j + 1) * P], ident)
                        close_tile(ins, name)

                    def pv(g, h):
                        br, qt = ATT[g]
                        if h == 0:
                            open_tile(pe, f"o{g}")
                        po = psum[:, T.at[f"o{g}"][0], :]
                        copied(pe, f"pt{g}_{h}")
                        if br == "c":
                            kv = h // 2
                            vl, vc = slice(kv * HD, (kv + 1) * HD), kv
                        else:
                            vl, vc = slice(P + h * HD, P + (h + 1) * HD), 2 + h
                        vs = [ZV[:, 0, vl]] if qt is None else [ZV[:, 1, vl], ZV[:, 2, vl], VC[:, vc, :]]
                        for j, v in enumerate(vs):
                            ins = nc.tensor.matmul(po[64 * (h % 2):64 * (h % 2) + 64, (h // 2) * P:(h // 2 + 1) * P],
                                                   v, PTB[:, h % 2, j * P:(j + 1) * P],
                                                   start=(j == 0), stop=(j == len(vs) - 1))
                        if h < 2:
                            ins.then_inc(S[f"pv{h}"], 1)
                        elif h == 3:
                            close_tile(ins, f"o{g}")

                    for n in GATE_ORDER:
                        for k in range(KT):
                            idx = GATE_ORDER.index(n) * KT + k
                            go, gs = out_at(idx), scores_at(idx)
                            if go is not None:
                                probs_t(go, 0)
                                probs_t(go, 1)
                            zt(f"g{n}_{k}")
                            if go is not None:
                                pv(go, 0)
                                probs_t(go, 2)
                                pv(go, 1)
                                probs_t(go, 3)
                            ps = open_tile(pe, f"p{n}_{k}")
                            q = idx // KT
                            pe.wait_ge(S["br_rest"], q + 1)
                            pe.wait_ge(S["b_rest"], idx + 1)
                            ins = None
                            for c in range(2):
                                for w, x in ((BWH, BRH[:, (q + 1) % 2]), (BWH, BRL[:, n]), (BWL, BRH[:, (q + 1) % 2])):
                                    ins = nc.tensor.matmul(ps[:, 0:TOK], w[:, idx % 2, c, :], x[:, c, :],
                                                           start=(ins is None), stop=(c == 1 and w is BWL))
                            close_tile(ins, f"p{n}_{k}")
                            if idx == 0:
                                normed_back()
                            if go is not None:
                                pv(go, 2)
                                pv(go, 3)
                            if gs is not None:
                                att_scores(gs)
                            if idx in ADA_AT:
                                ada_main(ADA_AT[idx])
                            if idx - 1 in ADA_AT:
                                ada_small(ADA_AT[idx - 1])

                    landed(pe, "wo0")
                    landed(pe, "wo1")
                    pe.wait_ge(S["gate_add"], 3 * KT)

                    def transposed(t):
                        pe.wait_ge(S["n2_xn"], t + 1)
                        for j in range(2):
                            ps = open_tile(pe, f"y{t}_{j}")
                            for k in range(4):
                                ins = nc.tensor.transpose(ps[:, k * P:(k + 1) * P], XN[:, t, (4 * j + k) * P:(4 * j + k + 1) * P], ident)
                            close_tile(ins, f"y{t}_{j}")

                    def logits(t):
                        for j in range(2):
                            copied(pe, f"y{t}_{j}")
                        for k in range(KT):
                            ins = nc.tensor.matmul(ps_rt[:, t * NE:(t + 1) * NE], HT[:, k, t * P:(t + 1) * P], WR[:, k, :],
                                                   start=(k == 0), stop=(k == KT - 1))
                        return ins

                    for t in range(TT):
                        for half in range(2):
                            if (t, half) == (TT - 1, 1):
                                transposed(0)
                            ps = open_tile(pe, f"wo{t}_{half}")
                            for k in range(KT):
                                wo = slot(f"wo{k // 4}", D)
                                ins = nc.tensor.matmul(ps[:, :], MRG[:, k, t * P:(t + 1) * P],
                                                       wo[:, k % 4, half * CH:(half + 1) * CH], start=(k == 0), stop=(k == KT - 1))
                            close_tile(ins, f"wo{t}_{half}")
                    transposed(1)
                    ps_rt = open_tile(pe, "rt")
                    pe.wait_ge(S["wr_in"], 16)
                    logits(0)
                    transposed(2)
                    logits(1)
                    close_tile(logits(2), "rt")

                @block.scalar
                def _(act):
                    act.wait_ge(once["x_in"], 32)
                    rms_part_act(act, S["sq_done"], S["ms_ready"], S["sd_ready"])

                    def copy_out(name, dst, src):
                        ps = take(act, name)
                        release(nc.scalar.activation(dst, src(ps), ACT.Copy), name)

                    def w_high(i):
                        if i < len(parts):
                            if i < 2:
                                take(act, "ada2")
                            landed(act, parts[i][1])
                            nc.scalar.activation(WSR[:, 0, i % 2], part_src(i), ACT.Copy).then_inc(S["w_high"], 1)

                    for k in range(0, KT, 2):
                        if k % 4 == 0:
                            for c in (k // 4, k // 4 + 2):
                                if k:
                                    copied(act, f"md{c - 1}")
                                copy_out(f"ada{c}", adas(c), lambda ps: ps)
                            if k:
                                w_high(0)
                            act.wait_ge(S["sc_ready"], k // 4 + 1)
                        ps = take(act, f"xt{k}")
                        hx = SIG[:, (k // 2) % 2, :]
                        if k >= 4:
                            act.wait_ge(S["rest_pool"], k // 2 - 1)
                        modulate_act(hx[:, 0:P], ps[:, 0:P], 0, 0, k, 0)
                        release(modulate_act(hx[:, P:TOK], ps[:, P:TOK], 0, 0, k, 1), f"xt{k}")
                        copied(act, f"xt{k}")
                        nc.scalar.activation(HTH[:, k, :], hx, ACT.Copy).then_inc(S["high_act"], 1)

                    w_high(1)
                    for c in range(2):
                        ps = take(act, f"gb{c}")
                        w_high(part_of[f"gb{c}"] + 2)
                        if c == 0:
                            act.wait_ge(S["rest_pool"], KT // 2)
                        release(nc.scalar.activation(SIG[:, c, :], ps[:, 0:TOK], ACT.Sigmoid), f"gb{c}")
                        take(act, f"ga{c}")
                        w_high(part_of[f"ga{c}"] + 2)

                    def copy_z(name, dst):
                        ps = take(act, name)
                        w_high(part_of[name] + 2)
                        release(nc.scalar.activation(dst, ps[:, 0:TOK], ACT.Copy), name)

                    for c in range(2):
                        copy_z(f"zf{c}", ZF[:, c, :])

                    def query(a):
                        ps = take(act, f"cq{a}")
                        w_high(part_of[f"cq{a}"] + 2)
                        nc.scalar.activation(QC[64 * a:64 * a + 64, 0, :], ps[0:64, 0:TOK], ACT.Copy)
                        release(nc.scalar.activation(QC[64 * a:64 * a + 64, 1, :], ps[64:128, 0:TOK], ACT.Copy), f"cq{a}")

                    query(0)
                    for t in range(TT):
                        copy_out(f"fa{t}", FG[:, t].rearrange("p c x n -> p (c x n)"), lambda ps: ps)
                    query(1)
                    copy_out("ctxT", CT, lambda ps: ps[:, 0:384].rearrange("p (c n) -> p c n", c=3))
                    copy_z("ck", KTC)
                    for c in range(2):
                        copy_out(f"fo{c}", BRT[:, 1, c, :], lambda ps: ps[:, 0:TOK])

                    def branch_high(q):
                        n = GATE_ORDER[q]
                        for x in {1: ("fo0", "fo1"), 0: ("lb0", "lb1"), 2: OUT_OF["c"], 3: OUT_OF["d"]}[n]:
                            copied(act, x)
                        nc.scalar.activation(BRH[:, (q + 1) % 2], BRT[:, n], ACT.Copy).then_inc(S["br_high"], 1)

                    def branch_part_high(idx):
                        landed(act, "wb01" if idx < 2 * KT else "wb23")
                        nc.scalar.activation(BWH[:, idx % 2], branch_part_src(idx), ACT.Copy).then_inc(S["b_high"], 1)

                    branch_high(0)
                    act.wait_ge(S["nab_ready"], 1)
                    for n, dst in (("dq0", DQ[:, 0, :]), ("dq1", DQ[:, 1, :]), ("zcv", VT[:, 0, :]), ("dk0", DK[:, 0, :]),
                                   ("dk1", DK[:, 1, :]), ("dv0", VT[:, 1, :]), ("dv1", VT[:, 2, :])):
                        copy_z(n, dst)
                    copy_out("ko", KO, lambda ps: ps[:, 0:384])
                    for t in range(TT):
                        copy_out(f"vt{t}", ZV[:, t, :], lambda ps: ps[:, 0:384])
                    act.wait_ge(S["dve_step"], ln_var_step[0])
                    nc.scalar.activation(LSD, MV[:, :, 1], ACT.Sqrt).then_inc(S["exps_done"], 1)
                    take(act, "lt2")
                    branch_part_high(0)
                    for idx in range(4 * KT):
                        n, k = GATE_ORDER[idx // KT], idx % KT
                        go, ge = out_at(idx), scores_at(idx - 1)
                        nk = 1 if go is not None and ATT[go][1] is None else 3
                        if go is not None:
                            copy_out(f"pt{go}_0", PTB[:, 0, 0:nk * P], lambda ps: ps[:, 0:nk * P])
                        ps = take(act, f"g{n}_{k}")
                        w_high(EARLY + idx + 2)
                        if idx == 0:
                            copied(act, "ga0")
                            copied(act, "ga1")
                        if idx >= 2:
                            m, kk = GATE_ORDER[(idx - 2) // KT], (idx - 2) % KT
                            copied(act, f"p{m}_{kk}")
                        release(nc.scalar.activation(SIG[:, idx % 2, :], ps[:, 0:TOK], ACT.Sigmoid), f"g{n}_{k}")
                        if idx + 1 < 4 * KT:
                            branch_part_high(idx + 1)
                        if idx == 0:
                            for c in range(2):
                                ps = take(act, f"lb{c}")
                                release(nc.scalar.activation(BRT[:, 0, c, :], ps[:, 0:TOK], ACT.Silu, scale=PRM[:, 128 + c:129 + c],
                                                             bias=PRM[:, 130 + c:131 + c]), f"lb{c}")
                        if go is not None:
                            act.wait_ge(S["pv0"], go + 1)
                            copy_out(f"pt{go}_2", PTB[:, 0, 0:nk * P], lambda ps: ps[:, 0:nk * P])
                        if ge is not None:
                            w = P if ATT[ge][1] is None else TOK
                            act.wait_ge(S["nmax_ready"], ge + 1)
                            if ATT[ge][0] == "c":
                                nc.scalar.activation(ES, DS, ACT.Exp)
                            for h in range(4):
                                ins = nc.scalar.activation(SCB[:, h, 0:w], SCB[:, h, 0:w], ACT.Exp, bias=NM[:, h:h + 1],
                                                           accum_out=SM[:, h:h + 1])
                            ins.then_inc(S["exps_done"], 1)
                        if idx in ADA_AT:
                            copy_out(f"ada{ADA_AT[idx]}", adas(ADA_AT[idx]), lambda ps: ps)
                        if idx in SPLIT_AFTER:
                            branch_high(SPLIT_AFTER.index(idx))
                    def square_root(t):
                        act.wait_ge(S["x_mixed"], 2 * t + 2)
                        nc.scalar.activation(XN[:, t, :], X[:, t, :], ACT.Square, accum_out=SS[:, t:t + 1]).then_inc(S["n2_sq"], 1)
                        act.wait_ge(S["n2_ms"], t + 1)
                        nc.scalar.activation(SD[:, t:t + 1], MS[:, t:t + 1], ACT.Sqrt).then_inc(S["n2_sd"], 1)

                    def modulated(t):
                        ps = take(act, f"y{t}_0")
                        for k in range(4):
                            ins = modulate_act(HT[:, k, t * P:(t + 1) * P], ps[:, k * P:(k + 1) * P], 1, 3, k, min(t, 1))
                        release(ins, f"y{t}_0")

                    act.wait_ge(S["sc_ready"], 4)
                    for c in (6, 7):
                        copied(act, f"md{c}")
                    square_root(0)
                    square_root(1)
                    modulated(0)
                    square_root(2)
                    modulated(1)
                    modulated(2)
                    nc.scalar.activation(ES, DS, ACT.Exp)
                    ps = take(act, "rt")
                    act.wait_ge(S["router_max"], 1)
                    for t in range(TT):
                        ins = nc.scalar.activation(AFF[:, t, :], ps[:, t * NE:(t + 1) * NE], ACT.Exp, bias=RMX[:, t:t + 1],
                                                   accum_out=RSM[:, t:t + 1])
                    release(ins, "rt")

                @block.vector
                def _(dve):
                    steps = [0]

                    def step(ins):
                        steps[0] += 1
                        ins.then_inc(S["dve_step"], 1)

                    def settle():
                        dve.wait_ge(S["dve_step"], steps[0])

                    rms_part_dve(dve, S["sq_done"], S["ms_ready"], S["sd_ready"], S["rs_ready"], S["xn_ready"])
                    ps = take(dve, "prm")
                    release(nc.vector.tensor_copy(PRM[:, :], ps[:, 0:132]), "prm")

                    def shift_scale(c):
                        ps = take(dve, f"md{c}")
                        release(nc.vector.tensor_tensor(MOD[:, 4 * c:4 * c + 4, :], ps[:, 0:8].rearrange("p (n i) -> p n i", i=2),
                                                        PRM[:, 4 * c:4 * c + 4].unsqueeze(2).broadcast_to((P, 4, 2)), ALU.add), f"md{c}")

                    def gain(which, scale_sec, col, half):
                        ks = slice(4 * half, 4 * half + 4)
                        copied(dve, f"md{2 * scale_sec + half}")
                        nc.vector.scalar_tensor_tensor(
                            SC[:, which, ks, :], MOD[:, scale_sec * KT + 4 * half:scale_sec * KT + 4 * half + 4, :], 1.0,
                            PRM[:, col + 4 * half:col + 4 * half + 4].unsqueeze(2).broadcast_to((P, 4, 2)), ALU.add,
                            ALU.mult).then_inc(S["sc_ready"], 1)

                    copied(dve, "prm")
                    for k in range(1, KT, 2):
                        if k % 4 == 1:
                            half = k // 4
                            shift_scale(half)
                            shift_scale(half + 2)
                            gain(0, 1, 48, half)
                            dve.wait_ge(S["sc_ready"], half + 1)
                        ps = take(dve, f"xt{k}")
                        hx = PTB[:, (k // 2) % 2, :]
                        if k >= 4:
                            dve.wait_ge(S["rest_dve"], k // 2 - 1)
                        modulate_dve(hx[:, 0:P], ps[:, 0:P], 0, 0, k, 0)
                        release(modulate_dve(hx[:, P:TOK], ps[:, P:TOK], 0, 0, k, 1), f"xt{k}")
                        copied(dve, f"xt{k}")
                        nc.vector.tensor_copy(HTH[:, k, :], hx).then_inc(S["high_dve"], 1)
                        dve.wait_ge(S["high_dve"], k // 2 + 1)
                        nc.vector.tensor_tensor(HTL[:, k, :], hx, HTH[:, k, :].bitcast(F32), ALU.subtract).then_inc(S["rest_dve"], 1)
                    dve.wait_ge(S["u_zero"], 1)
                    for c in range(2):
                        ps = take(dve, f"ga{c}")
                        copied(dve, f"gb{c}")
                        step(nc.vector.tensor_tensor(U[:, c, PADC:PADC + SEQ], ps[:, 0:P], SIG[:, c, 0:P], ALU.mult))
                        release(nc.vector.tensor_tensor(U[:, c, USAMP:USAMP + DEC], ps[:, P:TOK], SIG[:, c, P:TOK], ALU.mult),
                                f"ga{c}")
                    settle()
                    copied(dve, "ga0")
                    copied(dve, "ga1")
                    for k in range(CONV_K):
                        for c in range(2):
                            w = PRM[:, 64 + 2 * k + c:65 + 2 * k + c]
                            if k == 0:
                                ins = nc.vector.tensor_scalar(ACC[:, c, :], U[:, c, 0:AW], w, PRM[:, 126 + c:127 + c],
                                                              ALU.mult, ALU.add)
                            else:
                                dve.wait_ge(S["conv_step"], 2 * (k - 1) + c + 1)
                                ins = nc.vector.scalar_tensor_tensor(ACC[:, c, :], U[:, c, k:k + AW], w, ACC[:, c, :],
                                                                     ALU.mult, ALU.add)
                            ins.then_inc(S["conv_step"], 1)
                    dve.wait_ge(S["rest_in"], 16)
                    for i, (n, x) in enumerate((("rot0", QC[:, 0, P:TOK]), ("rot1", QC[:, 1, P:TOK]), ("rotk", KTC[:, P:TOK]))):
                        ps = take(dve, n)
                        step(nc.vector.tensor_tensor(x, x, cosT, ALU.mult))
                        release(nc.vector.tensor_tensor(ROTT, ps[:, 0:DEC], sinT, ALU.mult), n)
                        settle()
                        copied(dve, n)
                        nc.vector.tensor_tensor(x, x, ROTT, ALU.add).then_inc(S["rope_ready"], 1)
                        dve.wait_ge(S["rope_ready"], i + 1)
                    dve.wait_ge(S["grow_in"], 64)

                    def gate_rows(c):
                        gate, half = (0, c - 4) if c < 6 else (1, c - 10)
                        for i in range(2):
                            ps = take(dve, f"gr{c}_{i}")
                            dst = GROW[:, gate, i, half * CH:(half + 1) * CH]
                            release(nc.vector.tensor_tensor(dst, dst, ps, ALU.add), f"gr{c}_{i}")

                    def ada_end(c):
                        if c in GATE_CHUNKS:
                            gate_rows(c)
                        else:
                            shift_scale(c)
                        if c in (8, 9):
                            gain(1, 4, 56, c - 8)

                    for t in range(TT):
                        ps = take(dve, f"lt{t}")
                        step(nc.vector.bn_stats(BN[:, t, :], ps[:, 0:BW]))
                    settle()
                    for t in range(TT):
                        step(nc.vector.bn_aggr(MV[:, t, :], BN[:, t, :]))
                    settle()
                    step(nc.vector.tensor_scalar(MV[:, :, 1], MV[:, :, 1], EPS, None, ALU.add))
                    assert steps[0] == ln_var_step[0], steps[0]
                    dve.wait_ge(S["exps_done"], 1)
                    step(nc.vector.reciprocal(LRS, LSD))
                    settle()
                    for t in range(TT):
                        release(nc.vector.tensor_scalar(LNX[:, t, :], psum[:, T.at[f"lt{t}"][0], 0:BW], MV[:, t, 0:1],
                                                        LRS[:, t:t + 1], ALU.subtract, ALU.mult), f"lt{t}")
                    dve.wait_ge(S["sink_in"], 16)
                    dve.wait_ge(S["nab_ready"], 1)
                    adds = [0]

                    def gate_mul(idx):
                        n, k = GATE_ORDER[idx // KT], idx % KT
                        copied(dve, f"g{n}_{k}")
                        ps = take(dve, f"p{n}_{k}")
                        if idx == KT:
                            dve.wait_ge(S["out_kv"], 64)
                        if idx < KT:
                            release(nc.vector.tensor_tensor(MRG[:, k, :], SIG[:, idx % 2, :], ps[:, 0:TOK], ALU.mult), f"p{n}_{k}")
                        else:
                            if adds[0]:
                                dve.wait_ge(S["gate_add"], adds[0])
                            release(nc.vector.tensor_tensor(GP[:, idx % 2, :], SIG[:, idx % 2, :], ps[:, 0:TOK], ALU.mult),
                                    f"p{n}_{k}")
                            copied(dve, f"p{n}_{k}")
                            nc.vector.tensor_tensor(MRG[:, k, :], MRG[:, k, :], GP[:, idx % 2, :], ALU.add).then_inc(S["gate_add"], 1)
                            adds[0] += 1

                    for idx in range(4 * KT):
                        go, gs, ge = out_at(idx), scores_at(idx), scores_at(idx - 1)
                        if go is not None:
                            nk = 1 if ATT[go][1] is None else 3
                            for h in (1, 3):
                                ps = take(dve, f"pt{go}_{h}")
                                if h == 3:
                                    dve.wait_ge(S["pv1"], go + 1)
                                release(nc.vector.tensor_copy(PTB[:, 1, 0:nk * P], ps[:, 0:nk * P]), f"pt{go}_{h}")
                        gate_mul(idx)
                        if go is not None:
                            br, qt = ATT[go]
                            ps = take(dve, f"o{go}")
                            t0 = 0 if qt is None else P + qt * P
                            release(nc.vector.tensor_copy(BRT[:, 2 if br == "c" else 3, :, t0:t0 + P],
                                                          ps[:, 0:2 * P].rearrange("p (c n) -> p c n", c=2)), f"o{go}")
                        if gs is not None:
                            br, qt = ATT[gs]
                            w = P if qt is None else TOK
                            dve.wait_ge(S["scores_done"], gs + 1)
                            if qt is None:
                                nc.vector.tensor_scalar(SCB[:, :, 0:P], psum[:, 4:8, 0:P], SCALE, None, ALU.mult).then_inc(
                                    S["scores_read"], 1)
                            else:
                                bias = NAB[:, qt, :, :] if br == "d" else winmask[:, qt, :].unsqueeze(1).broadcast_to((P, 4, DEC))
                                step(nc.vector.scalar_tensor_tensor(SCB[:, :, 0:DEC], psum[:, 4:8, 0:DEC], SCALE, bias, ALU.mult,
                                                                    ALU.add))
                                nc.vector.tensor_scalar(SCB[:, :, DEC:TOK], psum[:, 4:8, DEC:TOK], SCALE, None, ALU.mult).then_inc(
                                    S["scores_read"], 1)
                                settle()
                            dve.wait_ge(S["scores_read"], gs + 1)
                            step(nc.vector.tensor_reduce(MX, SCB[:, :, 0:w], AX_X, ALU.max))
                            settle()
                            if br == "c":
                                step(nc.vector.tensor_tensor(MX, MX, SINK, ALU.max))
                                settle()
                                step(nc.vector.tensor_tensor(DS, SINK, MX, ALU.subtract))
                            nc.vector.tensor_scalar(NM, MX, -1.0, None, ALU.mult).then_inc(S["nmax_ready"], 1)
                        if ge is not None:
                            br, qt = ATT[ge]
                            w = P if qt is None else TOK
                            dve.wait_ge(S["exps_done"], ge + 2)
                            if br == "c":
                                step(nc.vector.tensor_tensor(SM, SM, ES, ALU.add))
                                settle()
                            step(nc.vector.reciprocal(RI, SM))
                            settle()
                            nc.vector.tensor_tensor(SCB[:, :, 0:w], SCB[:, :, 0:w], RI.unsqueeze(2).broadcast_to((P, 4, w)),
                                                    ALU.mult).then_inc(S["p_ready"], 1)
                        if idx - 1 in ADA_AT:
                            ada_end(ADA_AT[idx - 1])
                    dve.wait_ge(S["gate_add"], 3 * KT)

                    def second_norm(t):
                        dve.wait_ge(S["n2_sq"], t + 1)
                        nc.vector.tensor_scalar(MS[:, t:t + 1], SS[:, t:t + 1], 1.0 / D, EPS, ALU.mult, ALU.add).then_inc(S["n2_ms"], 1)
                        dve.wait_ge(S["n2_sd"], t + 1)
                        nc.vector.reciprocal(RS[:, t:t + 1], SD[:, t:t + 1]).then_inc(S["n2_rs"], 1)
                        dve.wait_ge(S["n2_rs"], t + 1)
                        nc.vector.tensor_scalar(XN[:, t, :], X[:, t, :], RS[:, t:t + 1], None, ALU.mult).then_inc(S["n2_xn"], 1)

                    def modulated(t):
                        ps = take(dve, f"y{t}_1")
                        for k in range(4):
                            ins = modulate_dve(HT[:, 4 + k, t * P:(t + 1) * P], ps[:, k * P:(k + 1) * P], 1, 3, 4 + k, min(t, 1))
                        release(ins, f"y{t}_1")

                    for i, (t, half) in enumerate((t, h) for t in range(TT) for h in range(2)):
                        ps = take(dve, f"wo{t}_{half}")
                        if i == 0:
                            for c in (4, 5):
                                for gi in range(2):
                                    copied(dve, f"gr{c}_{gi}")
                        cols = slice(half * CH, (half + 1) * CH)
                        if i:
                            dve.wait_ge(S["x_mixed"], i)
                        release(nc.vector.tensor_tensor(WOT[:, i % 2, :], ps, GROW[:, 0, min(t, 1), cols], ALU.mult), f"wo{t}_{half}")
                        copied(dve, f"wo{t}_{half}")
                        nc.vector.tensor_tensor(X[:, t, cols], X[:, t, cols], WOT[:, i % 2, :], ALU.add).then_inc(S["x_mixed"], 1)
                        if i in (2, 4):
                            second_norm(i // 2 - 1)
                        if i == 4:
                            dve.wait_ge(S["sc_ready"], 4)
                            for c in (6, 7):
                                copied(dve, f"md{c}")
                            modulated(0)
                    second_norm(2)
                    modulated(1)
                    modulated(2)
                    ps = take(dve, "rt")
                    step(nc.vector.tensor_reduce(RRI[:, 0:TT], ps[:, 0:TT * NE].rearrange("p (t e) -> p t e", t=TT), AX_X, ALU.max))
                    settle()
                    nc.vector.tensor_scalar(RMX[:, 0:TT], RRI[:, 0:TT], -1.0, None, ALU.mult).then_inc(S["router_max"], 1)

            with nc.Block() as block:
                @block.sync
                def _(sp):
                    def down_of_next(e):
                        return A["w_e_down"][bass.ds(l, 1), bass.ds(e, 2), D // 2:D, :][:, 1:2].rearrange(
                            "o e (k p) n -> p (o e k) n", p=P)

                    def load(g, j, e, after_next):
                        done = 4 * g + j + 1
                        for name, half, s in E_SRC:
                            if s == 0:
                                sp.wait_ge(S["e_half"], done)
                            elif s == 1:
                                e_take(sp, g, f"gu{j}_1")
                            elif s == 4:
                                sp.wait_ge(S["e_down_half"], done)
                            elif s == 5:
                                if after_next is None:
                                    continue
                                e_take(sp, g, f"y{j}")
                                s = down_slot(j)
                                sp.dma_start(e_dst(s), after_next).then_inc(e_land[s], 16)
                                continue
                            sp.dma_start(e_dst(s), e_unit(l, e, name, half)).then_inc(e_land[s], 16)

                    sp.dma_start(e_dst(NSLOT), e_unit(l, 1, "w_e_down", 1)).then_inc(e_land[NSLOT], 16)
                    with sp.Fori(0, NE // GRP - 1) as g:
                        for j in range(GRP):
                            load(g, j, g * GRP + (j + 1), down_of_next(g * GRP + (j + 1)))
                    last = NE // GRP - 1
                    for j in range(GRP - 1):
                        e = last * GRP + j + 1
                        load(last, j, e, down_of_next(e) if e + 1 < NE else None)
                    with sp.If(l < DEPTH - 1):
                        after = nc.s_assert_within(l + 1, 1, DEPTH - 1, skip_runtime_bounds_check_because="only before the last layer")
                        load_parameters(sp, after)
                        sp.wait_ge(S["e_half"], NE)
                        load_ada(sp, after, 0)
                        e_take(sp, last, f"gu{GRP - 1}_1")
                        for c in (2, 1, 3):
                            load_ada(sp, after, c)

                @block.tensor
                def _(pe):
                    for b in range(8):
                        pe.sem_inc(e_free[b], 1)
                    ps = open_tile(pe, "aft")
                    pe.wait_ge(S["aff_ready"], 1)
                    for t in range(TT):
                        ins = nc.tensor.transpose(ps[0:NE, t * P:(t + 1) * P], AFF[:, t, :], ident)
                    close_tile(ins, "aft")
                    ps = open_tile(pe, "post")
                    pe.wait_ge(S["cum_ready"], 1)
                    for t in range(TT):
                        ins = nc.tensor.transpose(ps[:, t * NE:(t + 1) * NE], CUM[0:NE, t * P:(t + 1) * P], ident[0:NE, 0:NE])
                    close_tile(ins, "post")

                    with pe.Fori(0, NE // GRP) as g:
                        def gather(k):
                            ps = e_open(pe, g, f"xe{k}")
                            for t in (1, 2, 0):
                                c0 = 0 if t else P
                                ins = nc.tensor.matmul(ps[:, c0:c0 + P], XN[:, t, k * P:(k + 1) * P],
                                                       SEL[:, t].rearrange("p e s -> p (e s)"), start=(t != 2), stop=(t != 1))
                            e_close(ins, f"xe{k}")

                        def affinities_t():
                            ps = e_open(pe, g, "pg")
                            pe.wait_ge(S["selg_ready"], g + 1)
                            for t in range(TT):
                                ins = nc.tensor.transpose(ps[:, t * P:(t + 1) * P], SELG[:, t].rearrange("p e s -> p (e s)"), ident)
                            e_close(ins, "pg")

                        pe.wait_ge(S["sel_ready"], g + 1)
                        for k in range(KT // 2 + 1):
                            gather(k)

                        def gate_up(j):
                            pb = [e_open(pe, g, f"gu{j}_{half}") for half in range(2)]
                            n_landed = 16 * (j + 1)
                            for k in range(KT):
                                if j == 0 and k == KT // 2:
                                    for kk in range(KT // 2 + 1, KT):
                                        gather(kk)
                                    affinities_t()
                                if k % 4 == 0:
                                    pe.wait_ge(e_land[k // 4], g * 64 + n_landed)
                                    pe.wait_ge(e_land[2 + k // 4], g * 64 + n_landed)
                                if j == 0:
                                    e_copied(pe, g, f"xe{k}")
                                for half in range(2):
                                    for m in range(2):
                                        w = e_dst(2 * m + k // 4)
                                        ins = nc.tensor.matmul(pb[half][64 * m:64 * m + 64, :], XE[:, k, j, :],
                                                               w[:, k % 4, half * CH:(half + 1) * CH], start=(k == 0), stop=(k == KT - 1))
                                    if k == KT - 1:
                                        e_close(ins, f"gu{j}_{half}")
                                if k == 3:
                                    ins.then_inc(S["e_half"], 1)

                        def down(j):
                            ps = e_open(pe, g, f"at{j}")
                            for k in range(KT):
                                if k % 4 == 0:
                                    e_copied(pe, g, f"gu{j}_{k // 4}")
                                    ins = nc.tensor.matmul(ps[:, k * 64:(k + 1) * 64], AA[0:64, k * P:(k + 1) * P],
                                                           ident[0:64, 0:64], start=True, stop=True)
                                else:
                                    ins = nc.tensor.transpose(ps[:, k * 64:(k + 1) * 64], AA[0:64, k * P:(k + 1) * P],
                                                              ident[0:64, 0:64])
                            e_close(ins, f"at{j}")
                            ps = e_open(pe, g, f"y{j}")
                            e_copied(pe, g, f"at{j}")
                            for k in range(KT):
                                if k == 0:
                                    pe.wait_ge(e_land[4], g * 64 + 16 * (j + 1))
                                elif k == 4:
                                    pe.wait_ge(e_land[down_slot(j)], g * 32 + 16 * (j // 2 + 1))
                                for half in range(2):
                                    ins = nc.tensor.matmul(ps[64 * half:64 * half + 64, :], AT[:, k, :],
                                                           e_dst(4 if k < 4 else down_slot(j))[:, k % 4, half * CH:(half + 1) * CH],
                                                           start=(k == 0), stop=(k == KT - 1))
                                if k == 3:
                                    ins.then_inc(S["e_down_half"], 1)
                            e_close(ins, f"y{j}")

                        for j in range(GRP):
                            gate_up(j)
                            down(j)
                        e_copied(pe, g, "pg")
                        e_copied(pe, g, f"y{GRP-2}")
                        e_copied(pe, g, f"y{GRP-1}")
                        for i, (t, half) in enumerate((t, h) for t in range(TT) for h in range(2)):
                            ps = e_open(pe, g, f"cm{i}")
                            e_close(nc.tensor.matmul(ps, PG[:, t, :], (YS if t else YP)[:, half * CH:(half + 1) * CH],
                                                     start=True, stop=True), f"cm{i}")

                @block.scalar
                def _(act):
                    act.wait_ge(S["aff_ready"], 1)
                    nc.scalar.activation(AFFG[:, 0:NE // GRP].rearrange("p g (t e) -> p g t e", t=TT),
                                         AFF.rearrange("p t (g e) -> p g t e", g=NE // GRP), ACT.Copy).then_inc(S["affg_ready"], 1)
                    with act.Fori(0, NE // GRP) as g:
                        for k in range(KT):
                            ps = e_take(act, g, f"xe{k}")[:, 0:2 * P].rearrange("p (x e s) -> p x e s", x=2, e=GRP)
                            modulate_act(XE[:, k, :, 0:SLOTS], ps[:, 0], 1, 3, k, 1)
                            e_release(modulate_act(XE[:, k, :, SLOTS:2 * SLOTS], ps[:, 1], 1, 3, k, 0), f"xe{k}")
                        ps = e_take(act, g, "pg")
                        e_release(nc.scalar.activation(PG, ps[:, 0:384].rearrange("p (t n) -> p t n", t=TT), ACT.Copy), "pg")

                        def at_copy(j):
                            ps = e_take(act, g, f"at{j}")
                            e_release(nc.scalar.activation(AT.rearrange("p k s -> p (k s)"), ps, ACT.Copy), f"at{j}")

                        def y_copy(j):
                            ps = e_take(act, g, f"y{j}")
                            rows = slice(32 * j, 32 * j + 32)
                            nc.scalar.activation(YS[rows, CH:D], ps[64:96, :], ACT.Copy)
                            e_release(nc.scalar.activation(YP[rows, CH:D], ps[96:128, :], ACT.Copy), f"y{j}")

                        for j in range(GRP):
                            for half in range(2):
                                ps = e_take(act, g, f"gu{j}_{half}")
                                if j:
                                    e_copied(act, g, f"gu{j-1}_{half}")
                                nc.scalar.activation(TMP[64:128, half * CH:(half + 1) * CH], ps[0:64, :], ACT.Silu).then_inc(
                                    S["silu_done"], 1)
                            at_copy(j)
                            y_copy(j)

                @block.vector
                def _(dve):
                    steps = [0]

                    def step(ins):
                        steps[0] += 1
                        ins.then_inc(S["route_step"], 1)

                    def settle():
                        dve.wait_ge(S["route_step"], steps[0])

                    copied(dve, "rt")
                    step(nc.vector.reciprocal(RRI[:, 0:TT], RSM[:, 0:TT]))
                    settle()
                    nc.vector.tensor_tensor(AFF, AFF, RRI[:, 0:TT].unsqueeze(2).broadcast_to((P, TT, NE)), ALU.mult).then_inc(
                        S["aff_ready"], 1)
                    step(nc.vector.memset(ONE[0:NE, :], 1.0))
                    step(nc.vector.memset(POSG[:, NE // GRP, :], 0.0))
                    step(nc.vector.memset(AFFG[:, NE // GRP, :], 0.0))
                    ps = take(dve, "aft")
                    step(nc.vector.tensor_copy(WK[0:NE, :], ps[0:NE, 0:TOK]))
                    settle()
                    for lo, hi, cap in ((0, SEQ, CAP_P), (SEQ, TOK, CAP_S)):
                        for r in range(cap // 8):
                            step(nc.vector.max(M8[0:NE, :], WK[0:NE, lo:hi]))
                            settle()
                            step(nc.vector.match_replace(WK[0:NE, lo:hi], M8[0:NE, :], WK[0:NE, lo:hi], -1.0))
                            settle()
                    release(nc.vector.tensor_scalar(MSK[0:NE, :], WK[0:NE, :], 0.0, None, ALU.is_lt), "aft")
                    copied(dve, "aft")
                    for lo, hi in ((0, SEQ), (SEQ, TOK)):
                        step(nc.vector.tensor_tensor_scan(CUM[0:NE, lo:hi], ONE[0:NE, lo:hi], MSK[0:NE, lo:hi], 0.0, ALU.mult, ALU.add))
                    settle()
                    nc.vector.tensor_tensor(CUM[0:NE, :], CUM[0:NE, :], MSK[0:NE, :], ALU.mult).then_inc(S["cum_ready"], 1)
                    ps = take(dve, "post")
                    release(nc.vector.tensor_scalar(POSG[:, 0:NE // GRP].rearrange("p g (t e) -> p g t e", t=TT),
                                                    ps[:, 0:TT * NE].rearrange("p (t g e) -> p g t e", t=TT, g=NE // GRP),
                                                    -1.0, None, ALU.add), "post")
                    copied(dve, "post")
                    dve.wait_ge(S["affg_ready"], 1)
                    def select(g, turn):
                        sel = SEL.rearrange("p t e s -> p (t e) s")
                        n = TT * GRP
                        nc.vector.tensor_tensor(sel, iota.unsqueeze(1).broadcast_to((P, n, SLOTS)),
                                                POSG[:, bass.ds(g, 1), :].rearrange("p o n -> p (o n)").unsqueeze(2).broadcast_to((P, n, SLOTS)),
                                                ALU.is_equal).then_inc(S["sel_ready"], 1)
                        dve.wait_ge(S["sel_ready"], turn)
                        nc.vector.tensor_tensor(SELG.rearrange("p t e s -> p (t e) s"), sel,
                                                AFFG[:, bass.ds(g, 1), :].rearrange("p o n -> p (o n)").unsqueeze(2).broadcast_to((P, n, SLOTS)),
                                                ALU.mult).then_inc(S["selg_ready"], 1)

                    select(0, 1)
                    with dve.Fori(0, NE // GRP) as g:
                        def y_copy(j):
                            ps = e_take(dve, g, f"y{j}")
                            rows = slice(32 * j, 32 * j + 32)
                            nc.vector.tensor_copy(YS[rows, 0:CH], ps[0:32, :])
                            e_release(nc.vector.tensor_copy(YP[rows, 0:CH], ps[32:64, :]), f"y{j}")

                        for j in range(GRP):
                            for half in range(2):
                                ps = e_take(dve, g, f"gu{j}_{half}")
                                dve.wait_ge(S["silu_done"], g * 8 + 2 * j + half + 1)
                                if j and half == 0:
                                    e_take(dve, g, f"at{j-1}")
                                cols = slice(half * CH, (half + 1) * CH)
                                e_release(nc.vector.tensor_tensor(AA[0:64, cols], TMP[64:128, cols], ps[64:128, :], ALU.mult),
                                          f"gu{j}_{half}")
                            if j == GRP - 1:
                                select(g + 1, g + 2)
                            y_copy(j)
                        for i, (t, half) in enumerate((t, h) for t in range(TT) for h in range(2)):
                            ps = e_take(dve, g, f"cm{i}")
                            cols = slice(half * CH, (half + 1) * CH)
                            e_release(nc.vector.tensor_tensor(CMB[:, i % 2, :], ps, GROW[:, 1, min(t, 1), cols], ALU.mult), f"cm{i}")
                            e_copied(dve, g, f"cm{i}")
                            nc.vector.tensor_tensor(X[:, t, cols], X[:, t, cols], CMB[:, i % 2, :], ALU.add).then_inc(S["x_done"], 1)
                            dve.wait_ge(S["x_done"], g * 6 + (i + 1))

            nums = [s.num for s in sems]
            assert max(nums) - min(nums) == len(nums) - 1
            nc.all_engine_barrier(sems_to_clear=range(min(nums), max(nums) + 1))

        with nc.Block() as block:
            @block.sync
            def _(sp):
                sp.dma_start(GROW[:, 0, 0, :], A["final_norm_g"].rearrange("(o d) -> o d", o=1).broadcast_to((P, D))).then_inc(
                    once["fin_g_in"], 16)
                for t in range(TT):
                    dst = A["y_prompt"] if t == 0 else A["y_sample"][:, (t - 1) * P:t * P]
                    sp.wait_ge(once["fin_y"], t + 1)
                    sp.dma_start(dst.rearrange("b s d -> (b s) d"), XN[:, t, :]).then_inc(once["fin_out"], 16)
                sp.wait_ge(once["fin_out"], TT * 16)

            @block.scalar
            def _(act):
                for t in range(TT):
                    nc.scalar.activation(XN[:, t, :], X[:, t, :], ACT.Square, accum_out=SS[:, t:t + 1]).then_inc(once["fin_sq"], 1)
                for t in range(TT):
                    act.wait_ge(once["fin_ms"], t + 1)
                    nc.scalar.activation(SD[:, t:t + 1], MS[:, t:t + 1], ACT.Sqrt).then_inc(once["fin_sd"], 1)

            @block.vector
            def _(dve):
                for t in range(TT):
                    dve.wait_ge(once["fin_sq"], t + 1)
                    nc.vector.tensor_scalar(MS[:, t:t + 1], SS[:, t:t + 1], 1.0 / D, EPS, ALU.mult, ALU.add).then_inc(once["fin_ms"], 1)
                dve.wait_ge(once["fin_g_in"], 16)
                for t in range(TT):
                    dve.wait_ge(once["fin_sd"], t + 1)
                    nc.vector.reciprocal(RS[:, t:t + 1], SD[:, t:t + 1]).then_inc(once["fin_rs"], 1)
                    dve.wait_ge(once["fin_rs"], t + 1)
                    nc.vector.scalar_tensor_tensor(XN[:, t, :], X[:, t, :], RS[:, t:t + 1], GROW[:, 0, 0, :], ALU.mult,
                                                   ALU.mult).then_inc(once["fin_y"], 1)


INS = ["x_prompt", "x_sample", "cache_win_k", "cache_win_v", "cache_nat_k", "cache_nat_v", "c", "c_ctx", "norm1_g", "norm2_g",
       "w_ada", "b_ada", "w_in", "conv_w", "conv_b", "conv_ln_g", "conv_ln_b", "win_sink", "w_branch", "w_out", "w_router",
       "w_e_gate", "w_e_up", "w_e_down", "final_norm_g"]
OUTS = [("y_prompt", (1, SEQ, D)), ("y_sample", (1, DEC, D)), ("new_win_k", (1, DEPTH, 2, SEQ, HD)),
        ("new_win_v", (1, DEPTH, 2, SEQ, HD)), ("new_nat_k", (1, DEPTH, 4, SEQ, HD)), ("new_nat_v", (1, DEPTH, 4, SEQ, HD))]


def bias_grid(na_bias):
    t = np.arange(DEC)
    row, col = t // 64, t % 64
    dr = row[None, :] - row[:, None] + 7
    dc = np.clip(col[None, :] - col[:, None] + 15, 0, 30)
    g = na_bias[:, :, dr, dc]
    return np.ascontiguousarray(g.reshape(DEPTH, 4, 2, P, DEC).transpose(0, 2, 3, 1, 4).reshape(DEPTH, 2, P, 4 * DEC))


def kernel(**inputs):
    import numpy as _np
    import concourse.bacc as _bacc
    from concourse import mybir as _mybir
    from concourse.bass_utils import run_bass_kernel_spmd as _run

    nc = _bacc.Bacc("TRN2", target_bir_lowering=False, num_devices=1)
    arrays, A = {}, {}
    data = {n: _np.asarray(inputs[n]) for n in INS}
    data["na_grid"] = bias_grid(_np.asarray(inputs["na_bias"]))
    data["const"] = constants()
    for name, a in data.items():
        a = _np.ascontiguousarray(a)
        arrays[f"in_{name}"] = a
        A[name] = nc.dram_tensor(f"in_{name}", a.shape, _mybir.dt.from_np(a.dtype), kind="ExternalInput").ap()
    for name, shape in OUTS:
        A[name] = nc.dram_tensor(f"out_{name}", shape, F32, kind="ExternalOutput").ap()
    build(nc, A)
    r = _run(nc, [arrays], core_ids=[0])
    return tuple(r.results[0][f"out_{name}"] for name, _ in OUTS)
```
